# Optimizing a Trainium2 kernel written in Bass

```python
import math
import jax, jax.numpy as jnp
from jax import lax
import numpy as np
import math, functools

D_MODEL = 1024
BATCH = 1
SEQ = 256
DEPTH = 2

N_A_LAYERS = DEPTH // 2
N_B_LAYERS = DEPTH - N_A_LAYERS

EXPAND = 2
D_A = EXPAND * D_MODEL
POOL_WINDOWS = (2, 4, 8, 16)
N_POOL_GROUPS = len(POOL_WINDOWS)
POOL_GW = D_A // N_POOL_GROUPS

ATTN_PAIRS = ((128, 1), (512, 4), (2048, 16))
N_GROUPS = len(ATTN_PAIRS)
N_HEADS = 16
HEAD_DIM = D_MODEL // N_HEADS
D_B = N_HEADS * HEAD_DIM
BLK = 128

DN_ALPHA = (2 * DEPTH) ** 0.25
DN_BETA = (8 * DEPTH) ** -0.25
LN_EPS = 1e-5
NEG_INF = -1e30


def layer_norm(x, g, b):
    xf = x.astype(jnp.float32)
    mu = jnp.mean(xf, axis=-1, keepdims=True)
    var = jnp.mean(jnp.square(xf - mu), axis=-1, keepdims=True)
    y = (xf - mu) * lax.rsqrt(var + LN_EPS) * g.astype(jnp.float32) + b.astype(jnp.float32)
    return y.astype(x.dtype)

def alibi_slopes():
    n = N_GROUPS * N_HEADS
    i = jnp.arange(1, n + 1, dtype=jnp.float32)
    return (2.0 ** (-8.0 * i / n)).reshape(N_GROUPS, N_HEADS)

def pool_mixer(h, w_in, w_grp, scale, w_out):
    B, S, _ = h.shape
    proj = h @ w_in
    u, gate = proj[..., :D_A], proj[..., D_A:]
    uf = u.astype(jnp.float32).reshape(B, S, N_POOL_GROUPS, POOL_GW)
    pos = jnp.arange(S)
    pooled = []
    for g, w in enumerate(POOL_WINDOWS):
        ug = uf[:, :, g]
        cs = jnp.cumsum(ug, axis=1)
        shifted = jnp.pad(cs, ((0, 0), (w, 0), (0, 0)))[:, :S]
        cnt = jnp.minimum(pos + 1, w).astype(jnp.float32)
        pooled.append((cs - shifted) / cnt[None, :, None] - ug)
    pooled = jnp.stack(pooled, axis=2)
    mixed = jnp.einsum('bsgc,gce->bsge', pooled, w_grp.astype(jnp.float32))
    mixed = (mixed.reshape(B, S, D_A) * scale.astype(jnp.float32)).astype(h.dtype)
    return (mixed * jax.nn.silu(gate)) @ w_out

def dilated_window_attention(q, k, v, window, dilation, slopes):
    B, S, H, dh = q.shape
    L = S // dilation
    nblk = -(-L // BLK)
    Lp = nblk * BLK
    win_sub = window // dilation

    def to_sub(t):
        t = t.reshape(B, L, dilation, H, dh)
        t = jnp.pad(t, ((0, 0), (0, Lp - L), (0, 0), (0, 0), (0, 0)))
        return t.reshape(B, nblk, BLK, dilation, H, dh)

    qb, kb, vb = to_sub(q), to_sub(k), to_sub(v)

    def with_prev(t):
        prev = jnp.concatenate([jnp.zeros_like(t[:, :1]), t[:, :-1]], axis=1)
        return jnp.concatenate([prev, t], axis=2)

    kk, vv = with_prev(kb), with_prev(vb)
    scores = jnp.einsum('bnqrhd,bnkrhd->bnrhqk', qb, kk) * (HEAD_DIM ** -0.5)

    a = jnp.arange(BLK)[:, None]
    c = jnp.arange(2 * BLK)[None, :]
    rel = BLK + a - c
    key_pos = (jnp.arange(nblk)[:, None, None] - 1) * BLK + c[None]
    valid = (rel >= 0)[None] & (rel <= win_sub)[None] & (key_pos >= 0)
    bias = -slopes[:, None, None] * (dilation * rel).astype(jnp.float32)[None]
    scores = jnp.where(valid[None, :, None, None], scores + bias[None, None, None], NEG_INF)

    lse = jax.nn.logsumexp(scores, axis=-1)
    p = jnp.exp(scores - lse[..., None])
    out = jnp.einsum('bnrhqk,bnkrhd->bnqrhd', p, vv)
    out = out.reshape(B, Lp, dilation, H, dh)[:, :L].reshape(B, S, H, dh)
    lse = jnp.transpose(lse, (0, 1, 4, 2, 3)).reshape(B, Lp, dilation, H)[:, :L].reshape(B, S, H)
    return out, lse

def dilated_mixer(h, w_in, w_out, k_sh, v_sh, slopes):
    B, S, _ = h.shape
    proj = h @ w_in
    q_all = proj[..., :N_GROUPS * D_B].astype(jnp.float32).reshape(B, S, N_GROUPS, N_HEADS, HEAD_DIM)
    gate = proj[..., N_GROUPS * D_B:]
    kf = k_sh.astype(jnp.float32)
    vf = v_sh.astype(jnp.float32)
    outs, lses = [], []
    for g, (window, dilation) in enumerate(ATTN_PAIRS):
        o, l = dilated_window_attention(q_all[:, :, g], kf[:, :, g], vf[:, :, g], window, dilation, slopes[g])
        outs.append(o)
        lses.append(l)
    wts = jax.nn.softmax(jnp.stack(lses, axis=0), axis=0)
    merged = jnp.sum(wts[..., None] * jnp.stack(outs, axis=0), axis=0)
    merged = merged.reshape(B, S, D_B).astype(h.dtype)
    return (merged * jax.nn.silu(gate)) @ w_out

def first_inputs(seed: int = 0) -> dict:
    key = jax.random.key(seed)
    ks = jax.random.split(key, 12)
    f32 = jnp.float32
    x = jax.random.normal(ks[0], (BATCH, SEQ, D_MODEL), f32)
    w_in_a = jax.random.normal(ks[1], (N_A_LAYERS, D_MODEL, 2 * D_A), f32) * D_MODEL ** -0.5
    w_grp_a = jax.random.normal(ks[2], (N_A_LAYERS, N_POOL_GROUPS, POOL_GW, POOL_GW), f32) * POOL_GW ** -0.5
    scale_a = 1.0 + 0.1 * jax.random.normal(ks[3], (N_A_LAYERS, D_A), f32)
    w_out_a = jax.random.normal(ks[4], (N_A_LAYERS, D_A, D_MODEL), f32) * (D_A ** -0.5) * DN_BETA
    w_kv = jax.random.normal(ks[5], (D_MODEL, 2 * N_GROUPS * D_B), f32) * D_MODEL ** -0.5
    w_in_b = jax.random.normal(ks[6], (N_B_LAYERS, D_MODEL, (N_GROUPS + 1) * D_B), f32) * D_MODEL ** -0.5
    w_out_b = jax.random.normal(ks[7], (N_B_LAYERS, D_B, D_MODEL), f32) * (D_B ** -0.5) * DN_BETA
    ln_g = 1.0 + 0.02 * jax.random.normal(ks[8], (DEPTH, D_MODEL), f32)
    ln_b = 0.02 * jax.random.normal(ks[9], (DEPTH, D_MODEL), f32)
    return {"x": x, "w_in_a": w_in_a, "w_grp_a": w_grp_a, "scale_a": scale_a, "w_out_a": w_out_a,
            "w_kv": w_kv, "w_in_b": w_in_b, "w_out_b": w_out_b, "ln_g": ln_g, "ln_b": ln_b}

def first_block(x, w_in_a, w_grp_a, scale_a, w_out_a, w_kv, w_in_b, w_out_b, ln_g, ln_b):
    B, S, _ = x.shape
    slopes = alibi_slopes()
    h = x
    k_sh = None
    v_sh = None
    for l in range(DEPTH):
        if l < N_A_LAYERS:
            y = pool_mixer(h, w_in_a[l], w_grp_a[l], scale_a[l], w_out_a[l])
        else:
            j = l - N_A_LAYERS
            y = dilated_mixer(h, w_in_b[j], w_out_b[j], k_sh, v_sh, slopes)
        h = layer_norm(DN_ALPHA * h + y, ln_g[l], ln_b[l])
        if l == N_A_LAYERS - 1:
            kv = h @ w_kv
            k_sh = kv[..., :N_GROUPS * D_B].reshape(B, S, N_GROUPS, N_HEADS, HEAD_DIM)
            v_sh = kv[..., N_GROUPS * D_B:].reshape(B, S, N_GROUPS, N_HEADS, HEAD_DIM)
    return h


GRID_W = 64
CTX_LEN = 256
HEAD_DIM_2 = 64
ROPE_THETA = 10000.0
ROPE_FREQS = HEAD_DIM_2 // 4
Q_BLOCK = 128
A_HEADS = 8
A_KV_HEADS = 2
B_HEADS = 4
B_V_DIM = 2 * HEAD_DIM_2
C_HEADS = 8
C_KV_HEADS = 2
C_WINDOW = 128
D_HEADS = 8
NA_ROWS = 8
NA_COLS = 16
EVEN_SPLITS = (A_HEADS * HEAD_DIM_2, A_KV_HEADS * HEAD_DIM_2, A_KV_HEADS * HEAD_DIM_2,
               2 * B_HEADS * HEAD_DIM_2, 2 * B_HEADS * HEAD_DIM_2, B_HEADS * B_V_DIM)
ODD_SPLITS = (C_HEADS * HEAD_DIM_2, C_KV_HEADS * HEAD_DIM_2, C_KV_HEADS * HEAD_DIM_2,
              D_HEADS * HEAD_DIM_2, D_HEADS * HEAD_DIM_2, D_HEADS * HEAD_DIM_2)
IN_WIDTH = sum(EVEN_SPLITS)
MIX_WIDTH = A_HEADS * HEAD_DIM_2 + B_HEADS * B_V_DIM
D_FF = 4 * D_MODEL
N_EVEN = (DEPTH + 1) // 2
N_ODD = DEPTH // 2
EPS = 1e-6
NEG = -1e30


def split_cols(p, sizes):
    return jnp.split(p, np.cumsum(sizes)[:-1].tolist(), axis=-1)

def rms_norm(x, g):
    xf = x.astype(jnp.float32)
    y = xf * lax.rsqrt(jnp.mean(jnp.square(xf), axis=-1, keepdims=True) + EPS)
    return (y * g.astype(jnp.float32)).astype(x.dtype)

def modulate(h, shift, scale):
    return h * (1 + scale) + shift

def lambda_init(layer):
    return 0.8 - 0.6 * math.exp(-0.3 * layer)

def axial_rope_tables(T, dtype):
    t = jnp.arange(T, dtype=jnp.int32)
    pos = jnp.stack([t // GRID_W, t % GRID_W], axis=-1).astype(jnp.float32)
    inv = ROPE_THETA ** (-jnp.arange(ROPE_FREQS, dtype=jnp.float32) / ROPE_FREQS)
    ang = pos[..., None] * inv
    return jnp.cos(ang).astype(dtype), jnp.sin(ang).astype(dtype)

def apply_axial_rope(x, cos, sin):
    xs = x.reshape(x.shape[:-1] + (2, 2, ROPE_FREQS))
    x1, x2 = xs[..., 0, :], xs[..., 1, :]
    c, s = cos[:, None], sin[:, None]
    return jnp.stack([x1 * c - x2 * s, x2 * c + x1 * s], axis=-2).reshape(x.shape)

def map_query_blocks(fn, *qs):
    B, T = qs[0].shape[:2]
    nb = T // Q_BLOCK
    blocks = tuple(jnp.moveaxis(a.reshape((B, nb, Q_BLOCK) + a.shape[2:]), 1, 0) for a in qs)
    out = lax.map(lambda args: fn(*args), blocks)
    return jnp.moveaxis(out, 0, 1).reshape((B, T) + out.shape[3:])

def gqa_attend(q, k, v):
    s = jnp.einsum('bqkgd,bskd->bkgqs', q, k).astype(jnp.float32)
    p = jax.nn.softmax(s, axis=-1).astype(v.dtype)
    return jnp.einsum('bkgqs,bskd->bqkgd', p, v)

def diff_attend(q, k, v, lam):
    s = jnp.einsum('bqhjd,bshjd->bhjqs', q, k).astype(jnp.float32)
    p = jax.nn.softmax(s, axis=-1)
    a = (p[:, :, 0] - lam * p[:, :, 1]).astype(v.dtype)
    return jnp.einsum('bhqs,bshe->bqhe', a, v)

def sink_attend(q, k, v, sink):
    s = jnp.einsum('bqkgd,bskd->bkgqs', q, k).astype(jnp.float32)
    sk = jnp.broadcast_to(sink.astype(jnp.float32)[None, :, :, None, None], s.shape[:-1] + (1,))
    p = jax.nn.softmax(jnp.concatenate([sk, s], axis=-1), axis=-1)[..., 1:].astype(v.dtype)
    return jnp.einsum('bkgqs,bskd->bqkgd', p, v)

def windowed_attend(q, k, v, k_ctx, v_ctx, sink):
    B, T = q.shape[:2]
    L = k_ctx.shape[1]
    nb = T // C_WINDOW

    def band(a):
        ap = jnp.pad(a, ((0, 0), (C_WINDOW, C_WINDOW), (0, 0), (0, 0)))
        ap = ap.reshape((B, nb + 2, C_WINDOW) + a.shape[2:])
        return jnp.concatenate([ap[:, :-2], ap[:, 1:-1], ap[:, 2:]], axis=2)

    kb, vb = band(k), band(v)
    qb = q.reshape((B, nb, C_WINDOW) + q.shape[2:])
    i = jnp.arange(C_WINDOW)[:, None]
    j = jnp.arange(3 * C_WINDOW)[None, :]
    kpos = jnp.arange(nb)[:, None, None] * C_WINDOW - C_WINDOW + j
    valid = (jnp.abs(j - C_WINDOW - i) <= C_WINDOW)[None] & (kpos >= 0) & (kpos < T)
    s_loc = jnp.einsum('bnqkgd,bnskd->bnkgqs', qb, kb).astype(jnp.float32)
    s_loc = jnp.where(valid[None, :, None, None], s_loc, NEG)
    s_ctx = jnp.einsum('bnqkgd,bskd->bnkgqs', qb, k_ctx).astype(jnp.float32)
    sk = jnp.broadcast_to(sink.astype(jnp.float32)[None, None, :, :, None, None], s_ctx.shape[:-1] + (1,))
    p = jax.nn.softmax(jnp.concatenate([sk, s_ctx, s_loc], axis=-1), axis=-1)
    p_ctx = p[..., 1:1 + L].astype(v.dtype)
    p_loc = p[..., 1 + L:].astype(v.dtype)
    o = (jnp.einsum('bnkgqs,bskd->bnqkgd', p_ctx, v_ctx)
         + jnp.einsum('bnkgqs,bnskd->bnqkgd', p_loc, vb))
    return o.reshape(q.shape)

def neighborhood_attend(q, k, v, k_ctx, v_ctx, rpb):
    B, T, H, Dh = q.shape
    rows = T // GRID_W
    kh = min(NA_ROWS, rows)
    kw = NA_COLS
    L = k_ctx.shape[1]
    r = jnp.arange(rows)
    rs = jnp.clip(r - kh // 2, 0, rows - kh)
    row_idx = rs[:, None] + jnp.arange(kh)[None, :]

    def gather_rows(a):
        return a.reshape(B, rows, GRID_W, H, Dh)[:, row_idx].reshape(B, rows, kh * GRID_W, H, Dh)

    kg, vg = gather_rows(k), gather_rows(v)
    qg = q.reshape(B, rows, GRID_W, H, Dh)
    cq = jnp.arange(GRID_W)
    cs = jnp.clip(cq - kw // 2, 0, GRID_W - kw)
    ck = jnp.tile(jnp.arange(GRID_W), kh)
    col_valid = (ck[None] >= cs[:, None]) & (ck[None] < cs[:, None] + kw)
    dr = jnp.repeat(row_idx - r[:, None], GRID_W, axis=1)
    dc = jnp.clip(ck[None] - cq[:, None], -(kw - 1), kw - 1)
    bias = rpb[:, dr[:, None, :] + NA_ROWS - 1, dc[None] + NA_COLS - 1]
    bias = jnp.moveaxis(bias, 0, 1).astype(jnp.float32)
    s_loc = jnp.einsum('brqhd,brshd->brhqs', qg, kg).astype(jnp.float32) + bias
    s_loc = jnp.where(col_valid, s_loc, NEG)
    s_ctx = jnp.einsum('brqhd,bshd->brhqs', qg, k_ctx).astype(jnp.float32)
    p = jax.nn.softmax(jnp.concatenate([s_ctx, s_loc], axis=-1), axis=-1)
    p_ctx = p[..., :L].astype(v.dtype)
    p_loc = p[..., L:].astype(v.dtype)
    o = (jnp.einsum('brhqs,bshd->brqhd', p_ctx, v_ctx)
         + jnp.einsum('brhqs,brshd->brqhd', p_loc, vg))
    return o.reshape(B, T, H * Dh)

def even_mixer(h_x, h_c, w_in, w_out, qk_g, lam_p, subln_g, lam0, cos, sin, with_ctx):
    scale = HEAD_DIM_2 ** -0.5
    g_a = A_HEADS // A_KV_HEADS

    def project(h, rope):
        n, s = h.shape[:2]
        qa, ka, va, qb, kb, vb = split_cols(h @ w_in, EVEN_SPLITS)
        qa = rms_norm(qa.reshape(n, s, A_HEADS, HEAD_DIM_2), qk_g[0])
        ka = rms_norm(ka.reshape(n, s, A_KV_HEADS, HEAD_DIM_2), qk_g[1])
        qb = qb.reshape(n, s, 2 * B_HEADS, HEAD_DIM_2)
        kb = kb.reshape(n, s, 2 * B_HEADS, HEAD_DIM_2)
        if rope:
            qa, ka = apply_axial_rope(qa, cos, sin), apply_axial_rope(ka, cos, sin)
            qb, kb = apply_axial_rope(qb, cos, sin), apply_axial_rope(kb, cos, sin)
        return ((qa * scale).reshape(n, s, A_KV_HEADS, g_a, HEAD_DIM_2), ka,
                va.reshape(n, s, A_KV_HEADS, HEAD_DIM_2),
                (qb * scale).reshape(n, s, B_HEADS, 2, HEAD_DIM_2),
                kb.reshape(n, s, B_HEADS, 2, HEAD_DIM_2),
                vb.reshape(n, s, B_HEADS, B_V_DIM))

    lam = (jnp.exp(jnp.sum(lam_p[0] * lam_p[1]).astype(jnp.float32))
           - jnp.exp(jnp.sum(lam_p[2] * lam_p[3]).astype(jnp.float32)) + lam0)
    qa_x, ka_x, va_x, qb_x, kb_x, vb_x = project(h_x, True)
    qa_c, ka_c, va_c, qb_c, kb_c, vb_c = project(h_c, False)
    ka_all = jnp.concatenate([ka_c, ka_x], axis=1)
    va_all = jnp.concatenate([va_c, va_x], axis=1)
    kb_all = jnp.concatenate([kb_c, kb_x], axis=1)
    vb_all = jnp.concatenate([vb_c, vb_x], axis=1)
    B, T = h_x.shape[:2]
    o_a = map_query_blocks(lambda q: gqa_attend(q, ka_all, va_all), qa_x).reshape(B, T, -1)
    o_b = map_query_blocks(lambda q: diff_attend(q, kb_all, vb_all, lam), qb_x)
    o_b = (rms_norm(o_b, subln_g) * (1 - lam0)).reshape(B, T, -1)
    out_x = jnp.concatenate([o_a, o_b], axis=-1) @ w_out
    out_c = None
    if with_ctx:
        n, L = h_c.shape[:2]
        oa_c = gqa_attend(qa_c, ka_c, va_c).reshape(n, L, -1)
        ob_c = (rms_norm(diff_attend(qb_c, kb_c, vb_c, lam), subln_g) * (1 - lam0)).reshape(n, L, -1)
        out_c = jnp.concatenate([oa_c, ob_c], axis=-1) @ w_out
    return out_x, out_c

def odd_mixer(h_x, h_c, w_in, w_out, sink, rpb, cos, sin, with_ctx):
    scale = HEAD_DIM_2 ** -0.5
    g_c = C_HEADS // C_KV_HEADS
    sink = sink.reshape(C_KV_HEADS, g_c)

    def project(h, rope):
        n, s = h.shape[:2]
        qc, kc, vc, qd, kd, vd = split_cols(h @ w_in, ODD_SPLITS)
        qc = qc.reshape(n, s, C_HEADS, HEAD_DIM_2)
        kc = kc.reshape(n, s, C_KV_HEADS, HEAD_DIM_2)
        if rope:
            qc, kc = apply_axial_rope(qc, cos, sin), apply_axial_rope(kc, cos, sin)
        return ((qc * scale).reshape(n, s, C_KV_HEADS, g_c, HEAD_DIM_2), kc,
                vc.reshape(n, s, C_KV_HEADS, HEAD_DIM_2),
                qd.reshape(n, s, D_HEADS, HEAD_DIM_2) * scale,
                kd.reshape(n, s, D_HEADS, HEAD_DIM_2),
                vd.reshape(n, s, D_HEADS, HEAD_DIM_2))

    qc_x, kc_x, vc_x, qd_x, kd_x, vd_x = project(h_x, True)
    qc_c, kc_c, vc_c, qd_c, kd_c, vd_c = project(h_c, False)
    B, T = h_x.shape[:2]
    o_c = windowed_attend(qc_x, kc_x, vc_x, kc_c, vc_c, sink).reshape(B, T, -1)
    o_d = neighborhood_attend(qd_x, kd_x, vd_x, kd_c, vd_c, rpb)
    out_x = jnp.concatenate([o_c, o_d], axis=-1) @ w_out
    out_c = None
    if with_ctx:
        n, L = h_c.shape[:2]
        oc_c = sink_attend(qc_c, kc_c, vc_c, sink).reshape(n, L, -1)
        od_c = gqa_attend(qd_c[:, :, :, None], kd_c, vd_c).reshape(n, L, -1)
        out_c = jnp.concatenate([oc_c, od_c], axis=-1) @ w_out
    return out_x, out_c

def squared_relu_mlp(h, w1, w2):
    return jnp.square(jax.nn.relu(h @ w1)) @ w2

def second_inputs(seed: int = 0) -> dict:
    key = jax.random.key(seed)
    ks = jax.random.split(key, 16)
    f32 = jnp.float32

    def nrm(k, shape, s):
        return jax.random.normal(k, shape, f32) * s

    return {
        "x": nrm(ks[0], (BATCH, SEQ, D_MODEL), 1.0),
        "c": nrm(ks[1], (BATCH, D_MODEL), 1.0),
        "ctx": nrm(ks[2], (BATCH, CTX_LEN, D_MODEL), 1.0),
        "c_ctx": nrm(ks[3], (D_MODEL,), 1.0),
        "w_mod": nrm(ks[4], (DEPTH, D_MODEL, 6 * D_MODEL), D_MODEL ** -0.5),
        "b_mod": nrm(ks[5], (DEPTH, 6 * D_MODEL), 0.02),
        "norm_g": 1.0 + nrm(ks[6], (DEPTH, 4, D_MODEL), 0.02),
        "w_in": nrm(ks[7], (DEPTH, D_MODEL, IN_WIDTH), D_MODEL ** -0.5),
        "w_out": nrm(ks[8], (DEPTH, MIX_WIDTH, D_MODEL), MIX_WIDTH ** -0.5),
        "w_mlp_in": nrm(ks[9], (DEPTH, D_MODEL, D_FF), D_MODEL ** -0.5),
        "w_mlp_out": nrm(ks[10], (DEPTH, D_FF, D_MODEL), D_FF ** -0.5),
        "qk_norm_a": 1.0 + nrm(ks[11], (N_EVEN, 2, HEAD_DIM_2), 0.02),
        "diff_lambda": nrm(ks[12], (N_EVEN, 4, HEAD_DIM_2), 0.1),
        "diff_subln": 1.0 + nrm(ks[13], (N_EVEN, B_V_DIM), 0.02),
        "sink_c": nrm(ks[14], (N_ODD, C_HEADS), 0.5),
        "rpb_d": nrm(ks[15], (N_ODD, D_HEADS, 2 * NA_ROWS - 1, 2 * NA_COLS - 1), 0.1),
    }

def second_block(x, c, ctx, c_ctx, w_mod, b_mod, norm_g, w_in, w_out, w_mlp_in, w_mlp_out,
              qk_norm_a, diff_lambda, diff_subln, sink_c, rpb_d):
    T = x.shape[1]
    cos, sin = axial_rope_tables(T, x.dtype)
    s_x = jax.nn.silu(c)
    s_c = jax.nn.silu(c_ctx)
    for l in range(DEPTH):
        last = l == DEPTH - 1
        mod_x = (s_x @ w_mod[l] + b_mod[l])[:, None, :]
        mod_c = s_c @ w_mod[l] + b_mod[l]
        sh1_x, sc1_x, g1_x, sh2_x, sc2_x, g2_x = jnp.split(mod_x, 6, axis=-1)
        sh1_c, sc1_c, g1_c, sh2_c, sc2_c, g2_c = jnp.split(mod_c, 6, axis=-1)
        h_x = modulate(rms_norm(x, norm_g[l, 0]), sh1_x, sc1_x)
        h_c = modulate(rms_norm(ctx, norm_g[l, 0]), sh1_c, sc1_c)
        if l % 2 == 0:
            i = l // 2
            m_x, m_c = even_mixer(h_x, h_c, w_in[l], w_out[l], qk_norm_a[i], diff_lambda[i],
                                  diff_subln[i], lambda_init(l), cos, sin, not last)
        else:
            i = l // 2
            m_x, m_c = odd_mixer(h_x, h_c, w_in[l], w_out[l], sink_c[i], rpb_d[i],
                                 cos, sin, not last)
        x = x + g1_x * rms_norm(m_x, norm_g[l, 1])
        f_x = squared_relu_mlp(modulate(rms_norm(x, norm_g[l, 2]), sh2_x, sc2_x), w_mlp_in[l], w_mlp_out[l])
        x = x + g2_x * rms_norm(f_x, norm_g[l, 3])
        if not last:
            ctx = ctx + g1_c * rms_norm(m_c, norm_g[l, 1])
            f_c = squared_relu_mlp(modulate(rms_norm(ctx, norm_g[l, 2]), sh2_c, sc2_c), w_mlp_in[l], w_mlp_out[l])
            ctx = ctx + g2_c * rms_norm(f_c, norm_g[l, 3])
    return x


def setup_inputs(seed=0):
    out = dict(first_inputs(seed))
    for name, value in second_inputs(seed + 1).items():
        if name != "x":
            out[name + "_2"] = value
    return out


def reference(
    x, w_in_a, w_grp_a, scale_a, w_out_a, w_kv, w_in_b, w_out_b, ln_g, ln_b, c_2, ctx_2,
    c_ctx_2, w_mod_2, b_mod_2, norm_g_2, w_in_2, w_out_2, w_mlp_in_2, w_mlp_out_2, qk_norm_a_2,
    diff_lambda_2, diff_subln_2, sink_c_2, rpb_d_2,
):
    x = first_block(
        x, w_in_a, w_grp_a, scale_a, w_out_a, w_kv, w_in_b, w_out_b, ln_g, ln_b,
    )
    return second_block(
        x, c_2, ctx_2, c_ctx_2, w_mod_2, b_mod_2, norm_g_2, w_in_2, w_out_2, w_mlp_in_2,
        w_mlp_out_2, qk_norm_a_2, diff_lambda_2, diff_subln_2, sink_c_2, rpb_d_2,
    )


_drawn_inputs = setup_inputs


def setup_inputs(seed=0):
    import zlib

    import numpy as np

    out = dict(_drawn_inputs(seed))
    spreads = {}
    factors = {'scale_a': 3.795,
     'qk_norm_a_2': 8.0,
     'diff_subln_2': 6.116,
     'sink_c_2': 8.0,
     'rpb_d_2': 8.0}
    for name, (base, spread) in spreads.items():
        noise = np.random.default_rng([zlib.crc32(name.encode()), seed]).standard_normal(out[name].shape)
        drawn = base * np.exp(spread * noise) if base else spread * noise
        out[name] = __import__('jax').numpy.asarray(drawn.astype(out[name].dtype))
    for name, factor in factors.items():
        out[name] = (out[name] * factor).astype(out[name].dtype)
    return out
```

```python
from contextlib import ExitStack

import concourse.bass as bass
import numpy as np
from concourse import mybir

F32 = mybir.dt.float32
F32R = mybir.dt.float32r
I32 = mybir.dt.int32
ALU = mybir.AluOpType
ACT = mybir.ActivationFunctionType
AX_X = mybir.AxisListType.X

P = 128
D = 1024
KD = D // P
S = 256
XT = S // P
NW = 512
D_A = 2 * D
POOL_WINDOWS = (2, 4, 8, 16)
PAIRS = ((128, 1), (512, 4), (2048, 16))
NG = len(PAIRS)
HEADS = 16
DH = 64
ALPHA = 4.0 ** 0.25
LN_EPS = 1e-5
EPS = 1e-6
LAM0 = 0.8 - 0.6
QSCALE = DH ** -0.5
GRID = 64
MASKED = -1e30
RSQRT_START = float(0x5F3759DF)
NEWTON_STEPS = 4
FAR = 3e32
SLOPES = [[2.0 ** (-8.0 * (g * HEADS + h + 1) / (NG * HEADS)) for h in range(HEADS)] for g in range(NG)]

CHUNK = 2048
RAW_SLOTS = 3
SPLIT_SLOTS = 4
ETILE = 1024


class Unit:

    def __init__(self, name, kind, nk, width, pieces):
        self.name, self.kind, self.nk, self.width, self.pieces = name, kind, nk, width, pieces


def plan_units():
    units = []

    def std(name, src, idx, row, col, kind="w"):
        units.append(Unit(name, kind, 4, NW, [(src, idx, row, col), (src, idx, row + 512, col)]))

    def mods(layer, lo, hi):
        for j in range(lo, hi):
            std(("mod", layer, j), "w_mod_2", (layer,), 0, j * NW, "mod")

    for g in range(4):
        std(("gate", g), "w_in_a", (0,), 0, D_A + g * NW)
    grp = [Unit(("grp", g), "w", 4, NW, [("w_grp_a", (0, g), 0, 0)]) for g in range(4)]
    for g in range(4):
        std(("u", g), "w_in_a", (0,), 0, g * NW)
        if g:
            units.append(grp[g - 1])
    units.append(grp[3])
    for n in range(2):
        for kh in range(2):
            std(("outa", n, kh), "w_out_a", (0,), kh * D, n * NW)
    for hf in range(2):
        for g in range(NG):
            std(("k", hf, g), "w_kv", (), 0, g * D + hf * NW)
        for g in range(NG):
            std(("q", hf, g), "w_in_b", (0,), 0, g * D + hf * NW)
        for g in range(NG):
            std(("v", hf, g), "w_kv", (), 0, (NG + g) * D + hf * NW)
        std(("gb", hf), "w_in_b", (0,), 0, NG * D + hf * NW)
        mods(0, 6 * hf, 6 * hf + 6)
    for n in range(2):
        std(("outb", n), "w_out_b", (0,), 0, n * NW)
    for l in range(2):
        std(("q2", l, 0), "w_in_2", (l,), 0, 0)
        units.append(Unit(("k2", l, 0), "w", 8, 256, [("w_in_2", (l,), 0, 512)]))
        if l == 0:
            mods(1, 0, 8)
        std(("q2", l, 1), "w_in_2", (l,), 0, 768)
        std(("k2", l, 1), "w_in_2", (l,), 0, 1280)
        std(("v2", l, 1), "w_in_2", (l,), 0, 1792)
        if l == 0:
            mods(1, 8, 12)
        for n in range(2):
            std(("out2", l, n), "w_out_2", (l,), 0, n * NW)
        for j in range(9):
            if j < 8:
                std(("in", l, j), "w_mlp_in_2", (l,), 0, j * NW)
            if j:
                units.append(Unit(("out", l, j - 1), "w", 4, NW,
                                  [("w_mlp_out_2", (l,), (j - 1) * NW, n * NW) for n in range(2)]))
    c = w = 0
    for n, u in enumerate(units):
        u.at, u.c0, u.w0 = n, c, w
        c += len(u.pieces)
        if u.kind == "w":
            w += len(u.pieces)
    return units


UNITS = plan_units()
UNIT = {u.name: u for u in UNITS}
CHUNKS = sum(len(u.pieces) for u in UNITS)
assert CHUNKS % RAW_SLOTS == 0
SPLIT = [(u.c0 + i, u) for u in UNITS if u.kind == "w" for i in range(len(u.pieces))]
WUNITS = [u for u in UNITS if u.kind == "w"]
for _n, _u in enumerate(WUNITS):
    _u.wn = _n


def constants():
    s = np.arange(S)
    pool = np.zeros((P, 4, 272), np.float32)
    for g, w in enumerate(POOL_WINDOWS):
        m = np.zeros((S, S))
        for t in range(S):
            m[t, max(0, t - w + 1):t + 1] = 1.0 / min(t + 1, w)
            m[t, t] -= 1.0
        pool[:, g, :144] = m[:144, :P].T
        pool[:, g, 144:] = m[P:, P:].T
    dist = np.zeros((P, NG, 256), np.float32)
    for g, (window, dilation) in enumerate(PAIRS):
        rel = P + np.arange(P)[:, None] - np.arange(256)[None, :]
        ok = (rel >= 0) & (rel <= window) & (rel % dilation == 0)
        dist[:, g] = np.where(ok, rel, FAR)
    pos = np.stack([s // GRID, s % GRID], -1).astype(np.float32)
    inv = (np.float32(10000.0) ** (-np.arange(16, dtype=np.float32) / np.float32(16))).astype(np.float32)
    ang = pos[..., None] * inv
    cos, sin = np.cos(ang), np.sin(ang)
    rc = np.stack([cos, cos], 2).reshape(2, P, DH).transpose(1, 0, 2)
    rs = np.stack([-sin, sin], 2).reshape(2, P, DH).transpose(1, 0, 2)
    band = np.zeros((P, 2, S), np.float32)
    for qt in range(2):
        band[:, qt] = np.where(np.abs(qt * P + np.arange(P)[:, None] - s[None]) <= P, 0.0, MASKED)
    cq = (np.arange(P) % GRID)[:, None]
    ck = (s % GRID)[None]
    start = np.clip(cq - 8, 0, GRID - 16)
    cols = np.where((ck >= start) & (ck < start + 16), 0.0, MASKED)
    out = {"t_ident": np.eye(P), "t_pool": pool.reshape(P, -1), "t_dist": dist.reshape(P, -1),
           "t_rope": np.stack([rc, rs], 1).reshape(P, -1), "t_band": band.reshape(P, -1), "t_cols": cols}
    return {k: np.ascontiguousarray(v, dtype=np.float32) for k, v in out.items()}


def plan_stage():
    slot, before = {}, {}
    for l in range(2):
        for part in range(2 - l):
            tiles = [("q", l, part, t) for t in range(4 if l == 0 else 2)] + [("k", l, part, t) for t in range(4)]
            for n, key in enumerate(tiles):
                slot[key] = n % 3
                before[key] = (tiles[n - 3][0] + "turn",) + tiles[n - 3][1:] if n >= 3 else None
    return slot, before


STAGE, STAGE_BEFORE = plan_stage()


class Counts:

    def __init__(self, known=None):
        self.known, self.now, self.marks, self.banks = known, {}, {}, {}
        self.sems = {}

    def did(self, sem, *labels):
        n = self.now[sem] = self.now.get(sem, 0) + 1
        for label in labels:
            assert label not in self.marks, label
            self.marks[label] = (sem, n)
        return self.sems[sem], 1

    def used(self, c, *labels):
        sem, n = f"raw_used{c % RAW_SLOTS}", c // RAW_SLOTS + 1
        for label in labels:
            self.marks[label] = (sem, n)
        return self.sems[sem], 1

    def after(self, *label):
        if self.known is None:
            return self.sems["tensor"], 1
        sem, n = self.known.marks[label]
        return self.sems[sem], n

    def bank(self, *label):
        return 0 if self.known is None else self.known.banks[label]


def heads_view(ap, *dims):
    return bass.AP(tensor=ap.tensor, offset=ap.offset, ap=[list(ap.ap[0])] + [list(d) for d in dims])


def rows_to_all(ap, offset, n):
    return bass.AP(tensor=ap.tensor, offset=ap.offset + offset, ap=[[0, P], [1, n]])


def build(nc, T, out, counts):
    did, after = counts.did, counts.after
    with ExitStack() as ctx:
        def sem(name):
            s = ctx.enter_context(nc.semaphore(name))
            counts.sems[name] = s
            return s

        def tile(stack, name, shape, dt=F32):
            return stack.enter_context(nc.sbuf_tensor(name, shape, dt))

        raw = tile(ctx, "raw", [P, RAW_SLOTS, CHUNK])
        whi = tile(ctx, "whi", [P, SPLIT_SLOTS, CHUNK], F32R)
        wlo = tile(ctx, "wlo", [P, SPLIT_SLOTS, CHUNK], F32R)
        fhi = tile(ctx, "fhi", [P, KD, 512], F32R)
        flo = tile(ctx, "flo", [P, KD, 512], F32R)
        hx = tile(ctx, "hx", [P, XT, D])
        ident = tile(ctx, "ident", [P, P])
        cond = tile(ctx, "cond", [P, KD, 2])
        modrow = tile(ctx, "modrow", [2, NW])
        modc = tile(ctx, "modc", [96, P])
        modb = tile(ctx, "modb", [P, 2, 48])
        normc = tile(ctx, "normc", [P, 2, 4, KD])
        modT = tile(ctx, "modT", [P, 2, 48])
        modA = tile(ctx, "modA", [P, 2, 2, 2, KD])
        modB = tile(ctx, "modB", [P, 2, 2, 2, KD])
        gcol = tile(ctx, "gcol", [P, 2, 2, KD])
        grow = tile(ctx, "grow", [32, P])
        scol = tile(ctx, "scol", [P, 16])
        stats = tile(ctx, "stats", [P, XT, 2, 6])
        mv = tile(ctx, "mv", [P, XT, 2])
        rstd = tile(ctx, "rstd", [P, 8])
        sumsq = tile(ctx, "sumsq", [P, 4])
        sumh = tile(ctx, "sumh", [P, 4, 2])
        newton = tile(ctx, "newton", [P, 2, 8])
        hss = tile(ctx, "hss", [P, 3, 8])
        hrs = tile(ctx, "hrs", [P, 3, 8])
        nmax = tile(ctx, "nmax", [P, 4, 2])
        rsum = tile(ctx, "rsum", [P, 4, 2])
        rinv = tile(ctx, "rinv", [P, 4, 2])
        esink = tile(ctx, "esink", [P, 4])
        lam = tile(ctx, "lam", [P, 4])

        one = ExitStack()
        gsil_a = ExitStack()
        sgate = tile(gsil_a, "sgate", [P, 16, S])
        yhi = tile(gsil_a, "yhi", [P, 16, S], F32R)
        ylo = tile(gsil_a, "ylo", [P, 16, S], F32R)
        sub = ExitStack()
        utok = tile(sub, "utok", [P, XT, NW])
        phi = tile(sub, "phi", [P, 4, S], F32R)
        plo = tile(sub, "plo", [P, 4, S], F32R)
        poolT = tile(sub, "poolT", [P, 4, 272])
        sub.close()
        lnrow_a = tile(sub, "lnrow_a", [P, 2, D])
        sub.close()
        gsil_a.close()
        kT1 = tile(one, "kT1", [P, NG * 4, S])
        qT1 = tile(one, "qT1", [P, NG * 4, S])
        v1 = tile(one, "v1", [P, XT, NG, NW])
        gb = tile(one, "gb", [P, XT, D])
        e1 = tile(one, "e1", [P, 3, 768])
        p1 = tile(one, "p1", [P, 2, 768])
        dist = tile(one, "dist", [P, NG, 256])
        lnrow_b = tile(one, "lnrow_b", [P, 2, D])
        one.close()
        hc = tile(ctx, "hc", [P, XT, D])
        mix = tile(ctx, "mix", [P, 4, D])
        att = ExitStack()
        kT = tile(att, "kT", [P, 4, 512])
        qT = tile(att, "qT", [P, 4, 512])
        vv = tile(att, "vv", [P, 4, 512])
        e2 = tile(att, "e2", [P, 3, ETILE])
        p2 = tile(att, "p2", [P, 2, 512])
        rope = tile(att, "rope", [P, 2, 2, DH])
        ropeg = tile(att, "ropeg", [P, 2, 2, 2, DH])
        qkg = tile(att, "qkg", [P, 2, DH])
        sublng = tile(att, "sublng", [P, P])
        lamrow = tile(att, "lamrow", [P, 4, DH])
        att.close()
        ffn = ExitStack()
        hhi = tile(ffn, "hhi", [P, 2, 4, 512], F32R)
        hlo = tile(ffn, "hlo", [P, 2, 4, 512], F32R)
        htmp = tile(ffn, "htmp", [P, 2, 512])
        gates = tile(ffn, "gates", [P, 2, D])
        ffn.close()
        att_b = ExitStack()
        kT_b = tile(att_b, "kT_b", [P, 4, 512])
        qT_b = tile(att_b, "qT_b", [P, 4, 512])
        vv_b = tile(att_b, "vv_b", [P, 4, 512])
        e2_b = tile(att_b, "e2_b", [P, 3, ETILE])
        p2_b = tile(att_b, "p2_b", [P, 2, 512])
        rope_b = tile(att_b, "rope_b", [P, 2, 2, DH])
        band = tile(att_b, "band", [P, 2, S])
        colmask = tile(att_b, "colmask", [P, S])
        sinkr = tile(att_b, "sinkr", [P, 8])
        nsink = tile(att_b, "nsink", [P, 8])
        att_b.close()
        KT, QT, VV, EE, PP, RO = (kT, kT_b), (qT, qT_b), (vv, vv_b), (e2, e2_b), (p2, p2_b), (rope, rope_b)

        ps = ctx.enter_context(nc.psum_tensor("ps", [P, 8, 512], F32))
        modd = nc.dram_tensor("modd", (2, 2, 6 * D), F32, kind="Internal").ap()
        gated = nc.dram_tensor("gated", (2, 4, D), F32, kind="Internal").ap()

        for name in ("tensor", "scalar", "vector", "pool"):
            sem(name)
        raw_in = [sem(f"raw_in{i}") for i in range(RAW_SLOTS)]
        for i in range(RAW_SLOTS):
            sem(f"raw_used{i}")
        loads = {}

        def H(t):
            return hx[:, t, :] if t < XT else hc[:, t - XT, :]

        def bias_d(h, t):
            return mix[:, XT + h // 2, (h % 2 * 2 + t) * S:(h % 2 * 2 + t + 1) * S] if h < 4 else \
                hc[:, h // 2 - 2, (h % 2 * 2 + t) * S:(h % 2 * 2 + t + 1) * S]

        def load_sem(name):
            if name not in loads:
                loads[name] = sem("in_" + name)
            return loads[name]

        for name in ("x", "ident", "cond", "pool", "scol", "modb", "normc", "lna", "lnb", "dist", "ctx",
                     "ropes", "modsave", "modc0", "modc1", "gsave", "out",
                     "g00", "g01", "g10", "g11", "bias", "odd"):
            load_sem(name)

        def whalf(which, u, k, c0, c1):
            w = u.w0 + k // u.nk
            base = (k % u.nk) * u.width
            return which[:, w % SPLIT_SLOTS, base + c0:base + c1]

        def items_first(hf):
            return [("first", hf, h, qt) for h in range(8) for qt in range(2)]

        def items_second(l, part):
            if l == 0 and part == 0:
                return [("A", 0, h, t) for h in range(8) for t in range(4)]
            if l == 0:
                return [("B", 0, h, t) for h in range(4) for t in range(4)]
            return [("C" if part == 0 else "D", 1, h, t) for h in range(8) for t in range(2)]

        def mods_first(hf):
            return [(0, j) for j in range(6 * hf, 6 * hf + 6)]

        def mods_second(l, part):
            return [] if l else [(1, j) for j in (range(8) if part == 0 else range(8, 12))]

        def mods_at(i, items, mods):
            every = max(1, len(items) // (len(mods) + 1))
            return [mods[i // every - 1]] if i and i % every == 0 and i // every <= len(mods) else []

        def item_info(it):
            kind, _, h, t = it
            if kind == "first":
                n = 128 * (t + 1)
                return [(g, n) for g in range(NG)], NG * (t + 1), DH
            n = 512 if t < XT else 256
            return [(j, n) for j in range(2 if kind == "B" else 1)], n // P, (P if kind == "B" else DH)

        def key_tile(it, j):
            if it[0] == "first":
                nt = it[3] + 1
                return j // nt, j % nt
            return 0, j + (0 if it[3] < XT else XT)

        block = ctx.enter_context(nc.Block())

        @block.sync
        def _(sp):
            sp.dma_start(hx[:, :, :], T["x"].rearrange("a (t p) d -> p (a t) d", p=P)).then_inc(loads["x"], 16)
            sp.dma_start(ident[:, :], T["t_ident"]).then_inc(loads["ident"], 16)
            for s in range(RAW_SLOTS):
                sp.dma_start(raw[:, s, :], T["wstream"][s]).then_inc(raw_in[s], 16)
            with sp.Fori(1, CHUNKS // RAW_SLOTS) as i:
                for s in range(RAW_SLOTS):
                    sp.wait_ge(counts.sems[f"raw_used{s}"], i)
                    sp.dma_start(raw[:, s, :], T["wstream"][i * RAW_SLOTS + s]).then_inc(raw_in[s], 16)
            for t in range(XT):
                sp.wait_ge(*after("final", t))
                sp.dma_start(out.rearrange("a (t p) d -> t p (a d)", p=P)[t], hx[:, t, :]).then_inc(loads["out"], 16)
            sp.wait_ge(loads["out"], 16 * XT)

        def wait_raw(eng, c):
            eng.wait_ge(raw_in[c % RAW_SLOTS], 16 * (c // RAW_SLOTS + 1))

        @block.tensor
        def _(pe):
            mm = nc.tensor.matmul
            last = {}
            turn = [0]
            state = {"banks": list(range(8))}

            def job(*label):
                banks = state["banks"]
                b = banks[turn[0] % len(banks)]
                turn[0] += 1
                if b in last:
                    pe.wait_ge(*after("read", *last[b]))
                last[b] = label
                counts.banks[label] = b
                return ps[:, b, :]

            def mm3(o, lh, ll, rh, rl, start, stop):
                mm(o, lh, rh, start=start, stop=False)
                mm(o, lh, rl, start=False, stop=False)
                return mm(o, ll, rh, start=False, stop=stop)

            def wait_weights(u):
                for i in range(len(u.pieces)):
                    pe.wait_ge(*after("lo", u.w0 + i))

            def by_token(u, name, tiles, kt=KD, width=NW):
                wait_weights(u)
                for t in tiles:
                    o = job(*name, t)
                    for k in range(kt):
                        ins = mm3(o[:, 0:width], fhi[:, k, t * P:t * P + P], flo[:, k, t * P:t * P + P],
                                  whalf(whi, u, k, 0, width), whalf(wlo, u, k, 0, width), k == 0, k == kt - 1)
                    labels = [name + (t,)] + ([("used", u.wn)] if t == tiles[-1] else [])
                    ins.then_inc(*did("tensor", *labels))

            def by_feature(u, name, c0, c1):
                wait_weights(u)
                for e in range(4):
                    o = job(*name, e)
                    for k in range(KD):
                        ins = mm3(o[:, 0:c1 - c0], whalf(whi, u, k, e * P, e * P + P), whalf(wlo, u, k, e * P, e * P + P),
                                  fhi[:, k, c0:c1], flo[:, k, c0:c1], k == 0, k == KD - 1)
                    labels = [name + (e,)] + ([("used", u.wn)] if e == 3 else [])
                    ins.then_inc(*did("tensor", *labels))

            def turn_features(name, src, nt, ready):
                per = 4 // nt
                for j in range(KD // per):
                    o = job(name, j)
                    if j == 0:
                        for r in ready:
                            pe.wait_ge(*after(*r))
                    for q in range(per):
                        for t in range(nt):
                            k = j * per + q
                            c = (q * nt + t) * P
                            ins = nc.tensor.transpose(o[:, c:c + P], src(t)[:, k * P:k * P + P], ident[:, :])
                    ins.then_inc(*did("tensor", (name, j)))

            def wait_features(name, nt):
                for j in range(KD // (4 // nt)):
                    pe.wait_ge(*after("split", name, j))

            def mod(l, j):
                u = UNIT[("mod", l, j)]
                o = job("mod", l, j)
                if l == 0 and j == 0:
                    pe.wait_ge(*after("cond"))
                for i in range(2):
                    c = u.c0 + i
                    wait_raw(pe, c)
                    for k in range(4):
                        ins = mm(o[0:2, :], cond[:, i * 4 + k, :], raw[:, c % RAW_SLOTS, k * NW:k * NW + NW],
                                 start=i + k == 0, stop=i == 1 and k == 3)
                    ins.then_inc(*counts.used(c, *([("mod", l, j)] if i else [])))

            def mod_columns(l):
                o = job("modT", l)
                pe.wait_ge(loads[f"modc{l}"], 16)
                nc.tensor.transpose(o[:, 0:96], modc[:, :], ident[0:96, 0:96]).then_inc(*did("tensor", ("modT", l)))
                o = job("grow", l)
                pe.wait_ge(*after("gcol", l))
                nc.tensor.transpose(o[0:32, 0:P], gcol[:, :, :, :].rearrange("p a b c -> p (a b c)"),
                                    ident[:, :]).then_inc(*did("tensor", ("grow", l)))

            def scores(it):
                kind, l, h, t = it
                parts, _, _ = item_info(it)
                if kind == "first":
                    po, tq = (h % 2) * DH, h // 2
                    n = parts[0][1]
                    o = job("s", it, 0)
                    o2 = job("s", it, 1) if t else None
                    if h == 0 and t == 0:
                        for g in range(NG):
                            for e in range(4):
                                pe.wait_ge(*after("k1", l, g, e))
                                pe.wait_ge(*after("q1", l, g, e))
                    for g in range(NG):
                        dst = o[:, g * n:(g + 1) * n] if not t or g < 2 else o2[:, 0:n]
                        ins = mm(dst, qT1[po:po + DH, g * 4 + tq, t * P:t * P + P], kT1[po:po + DH, g * 4 + tq, 0:n],
                                 start=True, stop=True)
                else:
                    part = {"A": 0, "B": 1, "C": 0, "D": 1}[kind]
                    if h == 0 and t == 0:
                        for tt in range(4):
                            pe.wait_ge(*after("kT", l, part, tt))
                        for tt in range(4 if l == 0 else 2):
                            pe.wait_ge(*after("qT", l, part, tt))
                    k0, k1 = (0, 512) if t < XT else (256, 512)
                    for j, n in parts:
                        head = 2 * h + j if kind == "B" else h
                        po, tq = (head % 2) * DH, head // 2
                        tk = tq if kind in "BD" else h // 4
                        o = job("s", it, j)
                        ins = mm(o[:, 0:n], QT[l][po:po + DH, tq, t * P:t * P + P], KT[l][po:po + DH, tk, k0:k1],
                                 start=True, stop=True)
                ins.then_inc(*did("tensor", ("s", it)))

            def turns(i, it):
                _, kt, _ = item_info(it)
                e = e1 if it[0] == "first" else EE[it[1]]
                pe.wait_ge(*after("probs", it))
                for b in range(0, kt, 4):
                    o = job("t", it, b)
                    for j in range(b, min(kt, b + 4)):
                        ins = nc.tensor.transpose(o[:, (j - b) * P:(j - b + 1) * P], e[:, i % 3, j * P:j * P + P], ident[:, :])
                    ins.then_inc(*did("tensor", ("t", it, b)))

            def values(i, it):
                kind, l, h, t = it
                _, kt, dv = item_info(it)
                p = p1 if kind == "first" else PP[l]
                o = job("o", it)
                if h == 0 and t == 0:
                    for tt in range(2 if kind == "first" else 4):
                        for g in range(NG if kind == "first" else 1):
                            pe.wait_ge(*(after("v1", l, g, tt) if kind == "first"
                                         else after("vv", l, {"A": 0, "B": 1, "C": 0, "D": 1}[kind], tt)))
                for b in range(0, kt, 4):
                    pe.wait_ge(*after("pT", it, b))
                for j in range(kt):
                    g, tt = key_tile(it, j)
                    if kind == "first":
                        v = v1[:, tt, g, h * DH:(h + 1) * DH]
                    elif kind in "AC":
                        v = VV[l][:, tt, (h // 4) * DH:(h // 4 + 1) * DH]
                    else:
                        v = VV[l][:, tt, h * dv:(h + 1) * dv]
                    ins = mm(o[:, 0:dv], p[:, i % 2, j * P:j * P + P], v, start=j == 0, stop=j == kt - 1)
                ins.then_inc(*did("tensor", ("o", it)))

            def attend(items, mods):
                for i in range(len(items) + 3):
                    if i < len(items):
                        scores(items[i])
                    for m in mods_at(i, items, mods):
                        mod(*m)
                    if 0 <= i - 2 < len(items):
                        turns(i - 2, items[i - 2])
                    if 0 <= i - 3 < len(items):
                        values(i - 3, items[i - 3])

            pe.wait_ge(loads["x"], 16)
            pe.wait_ge(loads["ident"], 16)
            turn_features("fx", lambda t: hx[:, t, :], 2, [])
            wait_features("fx", 2)
            for g in range(4):
                by_feature(UNIT[("gate", g)], ("gate", g), 0, S)

            def pool(g):
                if g == 0:
                    pe.wait_ge(loads["pool"], 16)
                for t in range(XT):
                    pe.wait_ge(*after("utok", g, t))
                for c in range(0, 4, 2):
                    o = job("pooled", g, c)
                    for q in range(2):
                        cc = slice((c + q) * P, (c + q + 1) * P)
                        r = o[:, q * S:(q + 1) * S]
                        mm(r[:, 0:144], utok[:, 0, cc], poolT[:, g, 0:144], start=q == 0, stop=False, skip_group_check=True)
                        ins = mm(r[:, 128:256], utok[:, 1, cc], poolT[:, g, 144:272], start=False, stop=True,
                                 skip_group_check=True)
                    ins.then_inc(*did("tensor", ("pooled", g, c)))

            def group(g):
                u = UNIT[("grp", g)]
                wait_weights(u)
                for c in range(0, 4, 2):
                    pe.wait_ge(*after("pooled split", g, c))
                for e in range(4):
                    o = job("mixed", g, e)
                    for k in range(4):
                        ins = mm3(o[:, 0:S], whalf(whi, u, k, e * P, e * P + P), whalf(wlo, u, k, e * P, e * P + P),
                                  phi[:, k, :], plo[:, k, :], k == 0, k == 3)
                    labels = [("mixed", g, e)] + ([("used", u.wn)] if e == 3 else [])
                    ins.then_inc(*did("tensor", *labels))

            for g in range(4):
                by_token(UNIT[("u", g)], ("u", g), range(XT))
                if g:
                    pool(g - 1) if g == 1 else None
                    group(g - 1)
                    pool(g)
            group(3)

            for n in range(2):
                outs = []
                for kh in range(2):
                    u = UNIT[("outa", n, kh)]
                    wait_weights(u)
                    for t in range(XT):
                        if kh == 0:
                            outs.append(job("outa", n, t))
                        for k in range(KD):
                            kk = kh * KD + k
                            if n == 0 and t == 0:
                                pe.wait_ge(*after("y", kk))
                            ins = mm3(outs[t], yhi[:, kk, t * P:t * P + P], ylo[:, kk, t * P:t * P + P],
                                      whalf(whi, u, k, 0, NW), whalf(wlo, u, k, 0, NW), kk == 0, kk == 15)
                        labels = ([("outa", n, t)] if kh else []) + ([("used", u.wn)] if t == 1 else [])
                        if labels:
                            ins.then_inc(*did("tensor", *labels))
            turn_features("f1", lambda t: hx[:, t, :], 2, [("ln", 0, 0), ("ln", 0, 1)])
            wait_features("f1", 2)
            for hf in range(2):
                for g in range(NG):
                    by_feature(UNIT[("k", hf, g)], ("k", hf, g), 0, S)
                for g in range(NG):
                    by_feature(UNIT[("q", hf, g)], ("q", hf, g), 0, S)
                for g in range(NG):
                    by_token(UNIT[("v", hf, g)], ("v", hf, g), range(XT))
                by_token(UNIT[("gb", hf)], ("gb", hf), range(XT))
                attend(items_first(hf), mods_first(hf))
            turn_features("fo1", lambda t: gb[:, t, :], 2, [("gated", items_first(1)[-1])])
            wait_features("fo1", 2)
            for n in range(2):
                by_token(UNIT[("outb", n)], ("outb", n), range(XT))
            mod_columns(0)

            for l in range(2):
                nt = 4 if l == 0 else 2
                turn_features(("n1", l), lambda t: mix[:, t, :], 4, [("xn", l, 0, t) for t in range(4)])
                wait_features(("n1", l), 4)

                def turn_heads(what, part, tiles, ntile):
                    for t in tiles:
                        r = STAGE[(what, l, part, t)]
                        o = job(what + "turn", l, part, t)
                        pe.wait_ge(*after("staged", what, l, part, t))
                        off = 256 if what == "k" and part == 0 else 0
                        for j in range(ntile):
                            ins = nc.tensor.transpose(o[:, j * P:(j + 1) * P], EE[l][:, r, off + j * P:off + j * P + P], ident[:, :])
                        ins.then_inc(*did("tensor", (what + "turn", l, part, t)))

                for part in range(2):
                    if l == 1 and part == 1:
                        by_feature(UNIT[("q2", l, 1)], ("q2", l, 1), 0, S)
                        by_feature(UNIT[("k2", l, 1)], ("k2", l, 1), 0, 512)
                    else:
                        by_token(UNIT[("q2", l, part)], ("q2", l, part), range(nt))
                        by_token(UNIT[("k2", l, part)], ("k2", l, part), range(4), width=256 if part == 0 else NW)
                        turn_heads("q", part, range(nt), 4)
                        turn_heads("k", part, range(4), 2 if part == 0 else 4)
                    if part == 1:
                        by_token(UNIT[("v2", l, 1)], ("v2", l, 1), range(4))
                    attend(items_second(l, part), mods_second(l, part))
                if l == 0:
                    mod_columns(1)
                turn_features(("fo", l), lambda t: mix[:, t, :], nt, [("mixed out", l, t) for t in range(nt)])
                wait_features(("fo", l), nt)
                for n in range(2):
                    by_token(UNIT[("out2", l, n)], ("out2", l, n), range(nt))
                turn_features(("n2", l), lambda t: mix[:, t, :], nt, [("xn", l, 1, t) for t in range(nt)])
                wait_features(("n2", l), nt)
                if l == 1:
                    held = {}
                    for t in range(XT):
                        for n in range(2):
                            held[t, n] = job("acc", t, n)
                    state["banks"] = [b for b in range(8) if b not in [counts.banks[("acc", t, n)] for t in range(2) for n in range(2)]]
                for j in range(9):
                    if j < 8:
                        by_feature(UNIT[("in", l, j)], ("in", l, j), 0, nt * P)
                    if j:
                        u = UNIT[("out", l, j - 1)]
                        wait_weights(u)
                        for e in range(4):
                            pe.wait_ge(*after("hidden", l, j - 1, e))
                        b = (j - 1) % 2
                        for n in range(2):
                            w = (u.w0 + n) % SPLIT_SLOTS
                            for t in range(nt):
                                o = held[t, n] if l else job("acc", j - 1, t, n)
                                for k in range(4):
                                    first, stop = (k == 0, k == 3) if l == 0 else (j == 1 and k == 0, j == 8 and k == 3)
                                    ins = mm3(o, hhi[:, b, k, t * P:t * P + P], hlo[:, b, k, t * P:t * P + P],
                                              whi[:, w, k * NW:(k + 1) * NW], wlo[:, w, k * NW:(k + 1) * NW], first, stop)
                                labels = [("used", u.wn)] if n == 1 and t == nt - 1 else []
                                if l == 0:
                                    labels.append(("acc", j - 1, t, n))
                                elif j == 8:
                                    labels.append(("acc", t, n))
                                if labels:
                                    ins.then_inc(*did("tensor", *labels))

        def split_hi(act, upto, state):
            while state[0] < len(SPLIT) and SPLIT[state[0]][1].wn <= upto:
                w = state[0]
                c, _ = SPLIT[w]
                wait_raw(act, c)
                if w >= SPLIT_SLOTS:
                    act.wait_ge(*after("used", SPLIT[w - SPLIT_SLOTS][1].wn))
                nc.scalar.activation(whi[:, w % SPLIT_SLOTS, :], raw[:, c % RAW_SLOTS, :], ACT.Copy).then_inc(
                    *did("scalar", ("hi", w)))
                state[0] += 1

        def split_lo(eng, ops, upto, state, mine):
            while state[0] < len(SPLIT) and SPLIT[state[0]][1].wn <= upto:
                w = state[0]
                c, _ = SPLIT[w]
                if w % 2 == mine:
                    eng.wait_ge(*after("hi", w))
                    ops.tensor_tensor(wlo[:, w % SPLIT_SLOTS, :], raw[:, c % RAW_SLOTS, :],
                                      whi[:, w % SPLIT_SLOTS, :].bitcast(F32), ALU.subtract).then_inc(
                        *counts.used(c, ("lo", w)))
                state[0] += 1

        def ftmp(l, which, j):
            return EE[l][:, j % 2, 0:512] if which == 0 else htmp[:, j % 2, :]

        TILES = {0: (2, 3, 0, 1), 1: (0, 1, 2, 3)}

        @block.scalar
        def _(act):
            copy = nc.scalar.activation
            st = [0]
            act.dma_start(cond[:, :, :], T["cond"]).then_inc(loads["cond"], 16)
            act.dma_start(poolT[:, :, :], T["t_pool"].rearrange("p (g t) -> p g t", g=4)).then_inc(loads["pool"], 16)
            act.dma_start(scol[:, :], T["scale_cols"]).then_inc(loads["scol"], 16)
            act.dma_start(modb[:, :, :], T["b_mod_cols"]).then_inc(loads["modb"], 16)
            act.dma_start(normc[:, :, :, :], T["norm_cols"]).then_inc(loads["normc"], 16)

            def split_to(name, ahead=1):
                split_hi(act, UNIT[name].wn + ahead, st)

            def src(*label):
                return ps[:, counts.bank(*label), :]

            def split_features(name, nt, tmp=None):
                per = 4 // nt
                for j in range(KD // per):
                    dst = fhi[:, j * per:(j + 1) * per, 0:nt * P]
                    if tmp is None:
                        act.wait_ge(*after(name, j))
                        got = src(name, j)
                    else:
                        act.wait_ge(*after("modulated", name, j))
                        got = ftmp(*tmp, j)
                    copy(dst, got.rearrange("p (a b) -> p a b", a=per), ACT.Copy).then_inc(
                        *did("scalar", ("fhi", name, j)))

            act.wait_ge(loads["cond"], 16)
            copy(cond[:, :, :], cond[:, :, :], ACT.Silu).then_inc(*did("scalar", ("cond",)))
            split_features("fx", 2)
            split_hi(act, 1, st)
            for g in range(4):
                split_to(("gate", g))
                for e in range(4):
                    act.wait_ge(*after("gate", g, e))
                    copy(sgate[:, g * 4 + e, :], src("gate", g, e)[:, 0:S], ACT.Silu).then_inc(
                        *did("scalar", ("sgate", g * 4 + e), ("read", "gate", g, e)))

            def u_copy(g):
                split_to(("u", g))
                for t in range(XT):
                    act.wait_ge(*after("u", g, t))
                    if g:
                        act.wait_ge(*after("pooled", g - 1, 2))
                    copy(utok[:, t, :], src("u", g, t), ACT.Copy).then_inc(
                        *did("scalar", ("utok", g, t), ("read", "u", g, t)))

            def pooled_hi(g):
                for c in range(0, 4, 2):
                    act.wait_ge(*after("pooled", g, c))
                    copy(phi[:, c:c + 2, :], src("pooled", g, c).rearrange("p (a b) -> p a b", a=2), ACT.Copy).then_inc(
                        *did("scalar", ("phi", g, c)))

            def y_hi(g):
                for e in range(4):
                    act.wait_ge(*after("ymul", g * 4 + e))
                    copy(yhi[:, g * 4 + e, :], sgate[:, g * 4 + e, :], ACT.Copy).then_inc(
                        *did("scalar", ("yhi", g * 4 + e)))

            for g in range(4):
                u_copy(g)
                if g == 1:
                    pooled_hi(0)
                if g:
                    split_to(("grp", g - 1))
                    y_hi(g - 1)
                    pooled_hi(g)
            split_to(("grp", 3))
            y_hi(3)
            for r, name in enumerate(("ln_g", "ln_b")):
                act.dma_start(lnrow_a[:, r, :], rows_to_all(T[name], 0, D)).then_inc(loads["lna"], 16)
            for n in range(2):
                for kh in range(2):
                    split_to(("outa", n, kh))
            split_features("f1", 2)
            split_to(("k", 0, 0), 0)

            def exps(i, it):
                kind, l, h, t = it
                parts, kt, _ = item_info(it)
                e = e1 if kind == "first" else EE[l]
                act.wait_ge(*after("max", it))
                if kind in "AB":
                    if i >= 3:
                        act.wait_ge(*after("t", items[i - 3], 0))
                    for j, n in parts:
                        labels = [("read", "s", it, j)]
                        if j == len(parts) - 1:
                            labels.append(("exp", it))
                            if kind == "A":
                                labels.append(("probs", it))
                        copy(e[:, i % 3, j * 512:j * 512 + n], src("s", it, j)[:, 0:n], ACT.Exp,
                             bias=nmax[:, i % 4, j:j + 1], accum_out=rsum[:, i % 4, j:j + 1]).then_inc(*did("scalar", *labels))
                    return
                n = kt * P
                if kind == "C":
                    copy(esink[:, i % 4:i % 4 + 1], sinkr[:, h:h + 1], ACT.Exp, bias=nmax[:, i % 4, 0:1]).then_inc(
                        *did("scalar", ("esink", it)))
                copy(e[:, i % 3, 0:n], e[:, i % 3, 0:n], ACT.Exp, bias=nmax[:, i % 4, 0:1],
                     accum_out=rsum[:, i % 4, 0:1]).then_inc(*did("scalar", ("exp", it), ("probs", it)))

            def prob_copy(i, it):
                _, kt, _ = item_info(it)
                p = p1 if it[0] == "first" else PP[it[1]]
                for b in range(0, kt, 4):
                    n = min(kt - b, 4) * P
                    act.wait_ge(*after("t", it, b))
                    if i >= 2:
                        act.wait_ge(*after("o", items[i - 2]))
                    copy(p[:, i % 2, b * P:b * P + n], src("t", it, b)[:, 0:n], ACT.Copy).then_inc(
                        *did("scalar", ("pT", it, b), ("read", "t", it, b)))

            def save_mod(l, j):
                act.wait_ge(*after("read", "mod", l, j))
                act.dma_start(modd[l, :, j * NW:(j + 1) * NW], modrow[:, :]).then_inc(loads["modsave"], 16)

            def attend(items, mods):
                for i in range(len(items) + 3):
                    if i < len(items):
                        exps(i, items[i])
                    for m in mods_at(i, items, mods):
                        save_mod(*m)
                    if 0 <= i - 2 < len(items):
                        prob_copy(i - 2, items[i - 2])

            def load_mods(l):
                act.wait_ge(loads["modsave"], 16 * 12 * (l + 1))
                act.dma_start(modc[:, :], modd[l].rearrange("v (r p) -> (v r) p", p=P)).then_inc(loads[f"modc{l}"], 16)

            def save_gates(l):
                act.wait_ge(*after("growc", l))
                act.dma_start(gated[l].rearrange("v (r p) -> (v r) p", p=P), grow[:, :]).then_inc(loads["gsave"], 16)

            def load_gates(l, which):
                act.wait_ge(loads["gsave"], 16 * (l + 1))
                for v in range(2 - l):
                    act.dma_start(gates[:, v, :], rows_to_all(gated, (l * 4 + which * 2 + v) * D, D)).then_inc(
                        loads[f"g{l}{which}"], 16)

            act.wait_ge(*after("ln", 0, 1))
            act.dma_start(dist[:, :, :], T["t_dist"].rearrange("p (g t) -> p g t", g=NG)).then_inc(loads["dist"], 16)
            for r, name in enumerate(("ln_g", "ln_b")):
                act.dma_start(lnrow_b[:, r, :], rows_to_all(T[name], D, D)).then_inc(loads["lnb"], 16)
            for hf in range(2):
                for g in range(NG):
                    split_to(("k", hf, g))
                    for e in range(4):
                        act.wait_ge(*after("k", hf, g, e))
                        copy(kT1[:, g * 4 + e, :], src("k", hf, g, e)[:, 0:S], ACT.Copy).then_inc(
                            *did("scalar", ("k1", hf, g, e), ("read", "k", hf, g, e)))
                for g in range(NG):
                    split_to(("q", hf, g))
                    for e in range(4):
                        act.wait_ge(*after("q", hf, g, e))
                        copy(qT1[:, g * 4 + e, :], src("q", hf, g, e)[:, 0:S], ACT.Copy, scale=QSCALE).then_inc(
                            *did("scalar", ("q1", hf, g, e), ("read", "q", hf, g, e)))
                for g in range(NG):
                    split_to(("v", hf, g))
                    for t in range(XT):
                        act.wait_ge(*after("v", hf, g, t))
                        copy(v1[:, t, g, :], src("v", hf, g, t), ACT.Copy).then_inc(
                            *did("scalar", ("v1", hf, g, t), ("read", "v", hf, g, t)))
                for t in range(XT):
                    act.wait_ge(*after("gb", hf, t))
                    copy(gb[:, t, hf * NW:(hf + 1) * NW], src("gb", hf, t), ACT.Silu).then_inc(
                        *did("scalar", ("gbs", hf, t), ("read", "gb", hf, t)))
                items = items_first(hf)
                attend(items, mods_first(hf))
                split_to(("gb", hf), 2)
            load_mods(0)
            act.dma_start(hc[:, :, :], T["ctx_2"].rearrange("a (t p) d -> p (a t) d", p=P)).then_inc(loads["ctx"], 16)
            split_features("fo1", 2)
            split_to(("outb", 1), 1)
            save_gates(0)

            def squares(label, t):
                copy(mix[:, t, :], H(t), ACT.Square, accum_out=sumsq[:, t:t + 1]).then_inc(*did("scalar", label))

            def square_halves(l, which, t):
                for n in range(2):
                    k = ("sqh", l, which, t, n)
                    if t:
                        act.wait_ge(*after("sqh", l, which, t - 1, n))
                    copy(htmp[:, n, :], mix[:, t, n * NW:(n + 1) * NW], ACT.Square, accum_out=sumh[:, t, n:n + 1]).then_inc(
                        *did("scalar", k))

            for l in range(2):
                nt = 4 if l == 0 else 2
                for t in TILES[l]:
                    if l == 0 and t == 2:
                        act.wait_ge(loads["ctx"], 16)
                    if l == 0 and t < XT:
                        act.wait_ge(*after("ln", 1, t))
                    if l == 1:
                        act.wait_ge(*after("resid", 0, 1, t))
                    squares(("sq", l, 0, t), t)
                if l == 0:
                    act.wait_ge(*after("ln", 1, 1))
                    act.dma_start(rope[:, :, :, :], T["t_rope"].rearrange("p (a t d) -> p a t d", a=2, t=2)).then_inc(
                        loads["ropes"], 16)
                    act.dma_start(qkg[:, :, :], rows_to_all(T["qk_norm_a_2"], 0, 2 * DH)).then_inc(loads["ropes"], 16)
                    act.dma_start(sublng[:, :], rows_to_all(T["diff_subln_2"], 0, P)).then_inc(loads["ropes"], 16)
                    act.dma_start(lamrow[:, :, :], rows_to_all(T["diff_lambda_2"], 0, 4 * DH)).then_inc(loads["ropes"], 16)
                    split_to(("outb", 1), 2)
                else:
                    split_to(("q2", 1, 0), 1)
                split_features(("n1", l), 4, (l, 0))
                if l == 0:
                    act.wait_ge(*after("lam sums"))
                    copy(lam[:, 0:2], lam[:, 0:2], ACT.Exp).then_inc(*did("scalar", ("lam exp",)))
                else:
                    act.wait_ge(*after(("n1", 1), 7))
                    for h in range(8):
                        for r in range(4):
                            rows = bass.AP(tensor=T["rpb_rows"].tensor,
                                           offset=T["rpb_rows"].offset + (h * 7 + 3 - r) * GRID * P + GRID - 1,
                                           ap=[[P - 1, GRID], [GRID * P, 4], [1, GRID]])
                            b = bias_d(h, r // 2)[r % 2 * GRID:(r % 2 + 1) * GRID, :]
                            act.dma_start(b.rearrange("p (a b) -> p a b", a=4), rows).then_inc(loads["bias"], 16)
                for part in range(2):
                    if l == 1 and part == 1:
                        split_to(("q2", l, 1))
                        for e in range(4):
                            act.wait_ge(*after("q2", l, 1, e))
                            copy(QT[l][:, e, 0:S], src("q2", l, 1, e)[:, 0:S], ACT.Copy, scale=QSCALE).then_inc(
                                *did("scalar", *([("qT", l, 1, t) for t in range(2)] if e == 3 else []), ("read", "q2", l, 1, e)))
                        split_to(("k2", l, 1))
                        for e in range(4):
                            act.wait_ge(*after("k2", l, 1, e))
                            copy(KT[l][:, e, :], src("k2", l, 1, e), ACT.Copy).then_inc(
                                *did("scalar", *([("kT", l, 1, t) for t in range(4)] if e == 3 else []), ("read", "k2", l, 1, e)))
                    else:
                        sets = (("q", range(nt)), ("k", range(4)))
                        for what, tiles in sets:
                            small = what == "k" and part == 0
                            split_to((what + "2", l, part), 0 if small and l == 0 else 1)
                            w = P if small else NW
                            for t in tiles:
                                key = (what, l, part, t)
                                a = src(what + "2", l, part, t)
                                act.wait_ge(*after(what + "2", l, part, t))
                                if small:
                                    copy(VV[l][:, t, 0:P], a[:, P:2 * P], ACT.Copy).then_inc(*did("scalar", ("vv", l, part, t)))
                                normed = l == 0 and part == 0
                                if (normed or (t >= XT and not small)) and STAGE_BEFORE[key]:
                                    act.wait_ge(*after(*STAGE_BEFORE[key]))
                                if normed:
                                    copy(EE[l][:, STAGE[key], 512:512 + w], a[:, 0:w], ACT.Square).then_inc(
                                        *did("scalar", ("squared",) + key))
                                elif t >= XT and not small:
                                    copy(EE[l][:, STAGE[key], 0:w], a[:, 0:w], ACT.Copy).then_inc(
                                        *did("scalar", ("staged",) + key, ("read", what + "2", l, part, t)))
                        for what, tiles in sets:
                            n = 2 if what == "k" and part == 0 else 4
                            dst = (QT if what == "q" else KT)[l]
                            for t in tiles:
                                act.wait_ge(*after(what + "turn", l, part, t))
                                copy(dst[:, 0:n, t * P:t * P + P],
                                     src(what + "turn", l, part, t)[:, 0:n * P].rearrange("p (a b) -> p a b", a=n),
                                     ACT.Copy, scale=QSCALE if what == "q" else 1.0).then_inc(
                                    *did("scalar", (what + "T", l, part, t), ("read", what + "turn", l, part, t)))
                    if part == 1:
                        split_to(("v2", l, 1), l)
                        for t in range(4):
                            act.wait_ge(*after("v2", l, 1, t))
                            copy(VV[l][:, t, :], src("v2", l, 1, t), ACT.Copy).then_inc(
                                *did("scalar", ("vv", l, 1, t), ("read", "v2", l, 1, t)))
                    items = items_second(l, part)
                    if l == 1 and part == 0:
                        act.wait_ge(loads["odd"], 64)
                    attend(items, mods_second(l, part))
                    split_to(("q2", l, 1) if part == 0 else ("out2", l, 0), 1)
                if l == 0:
                    load_mods(1)
                    save_gates(1)
                for t in range(nt):
                    act.wait_ge(*after("mixed out", l, t))
                load_gates(l, 0)
                split_features(("fo", l), nt)
                for n in range(2):
                    split_to(("out2", l, n))
                    for t in range(nt):
                        act.wait_ge(*after("out2", l, n, t))
                        copy(mix[:, t, n * NW:(n + 1) * NW], src("out2", l, n, t), ACT.Copy).then_inc(
                            *did("scalar", ("out copied", l, n, t), ("read", "out2", l, n, t)))
                split_to(("in", l, 0), 1)
                for t in range(nt):
                    act.wait_ge(*after("out copied", l, 1, t))
                    square_halves(l, 0, t)
                for t in range(nt):
                    act.wait_ge(*after("resid", l, 0, t))
                    squares(("sq", l, 1, t), t)
                load_gates(l, 1)
                split_features(("n2", l), nt, (l, 1))
                for j in range(9):
                    if j < 8:
                        split_to(("in", l, j))
                        for e in range(4):
                            act.wait_ge(*after("in", l, j, e))
                            n = j * 4 + e
                            if n >= 2:
                                act.wait_ge(*after("hidden", l, (n - 2) // 4, (n - 2) % 4))
                            copy(htmp[:, e % 2, 0:nt * P], src("in", l, j, e)[:, 0:nt * P], ACT.Relu).then_inc(
                                *did("scalar", ("relu", l, j, e), ("read", "in", l, j, e)))
                            act.wait_ge(*after("squared", l, j, e))
                            if j >= 2:
                                act.wait_ge(*after("used", UNIT[("out", l, j - 2)].wn))
                            copy(hhi[:, j % 2, e, 0:nt * P], htmp[:, e % 2, 0:nt * P], ACT.Copy).then_inc(
                                *did("scalar", ("hhi", l, j, e)))
                    if j:
                        split_to(("out", l, j - 1))
                for t in range(nt):
                    act.wait_ge(*after("summed", l, t))
                    square_halves(l, 1, t)
                if l == 0:
                    act.wait_ge(*after("resid", 0, 1, 3))
                    act.dma_start(rope_b[:, :, :, :], T["t_rope"].rearrange("p (a t d) -> p a t d", a=2, t=2)).then_inc(
                        loads["odd"], 16)
                    act.dma_start(sinkr[:, :], rows_to_all(T["sink_c_2"], 0, 8)).then_inc(loads["odd"], 16)
                    act.dma_start(band[:, :, :], T["t_band"].rearrange("p (a b) -> p a b", a=2)).then_inc(loads["odd"], 16)
                    act.dma_start(colmask[:, :], T["t_cols"]).then_inc(loads["odd"], 16)

        @block.vector
        def _(dve):
            v = nc.vector
            st = [0]

            def split_to(name, ahead=1):
                split_lo(dve, v, UNIT[name].wn + ahead, st, 1)

            def link(ins, *labels):
                ins.then_inc(*did("vector", *labels))
                dve.wait_ge(counts.sems["vector"], counts.now["vector"])

            def src(*label):
                return ps[:, counts.bank(*label), :]

            def low_features(name, nt):
                per = 4 // nt
                for j in range(KD // per):
                    dve.wait_ge(*after("fhi", name, j))
                    dst = flo[:, j * per:(j + 1) * per, 0:nt * P]
                    hi = fhi[:, j * per:(j + 1) * per, 0:nt * P].bitcast(F32)
                    v.tensor_tensor(dst, src(name, j).rearrange("p (a b) -> p a b", a=per), hi, ALU.subtract).then_inc(
                        *did("vector", ("split", name, j), ("read", name, j)))

            def modulate(name, nt, l, which):
                per = 4 // nt
                for j in range(KD // per):
                    dve.wait_ge(*after(name, j))
                    if j >= 2:
                        dve.wait_ge(*after("split", name, j - 2))
                    for q in range(2):
                        k, vec = (j, q) if nt == 4 else (2 * j + q, 0)
                        ins = v.tensor_scalar(ftmp(l, which, j)[:, q * S:(q + 1) * S], src(name, j)[:, q * S:(q + 1) * S],
                                              modA[:, l, which, vec, k:k + 1], modB[:, l, which, vec, k:k + 1], ALU.mult, ALU.add)
                    ins.then_inc(*did("vector", ("modulated", name, j), ("read", name, j)))

            def rsqrt(out_, in_, n, eps):
                w = out_.shape[-1]
                x, t = newton[:, 0, 0:w], newton[:, 1, 0:w]
                link(v.tensor_scalar(x, in_, 1.0 / n, eps, ALU.mult, ALU.add))
                link(v.tensor_scalar(out_.bitcast(I32), x.bitcast(I32), -0.5, RSQRT_START, ALU.mult, ALU.add))
                for _ in range(NEWTON_STEPS):
                    link(v.tensor_tensor(t, out_, out_, ALU.mult))
                    link(v.tensor_tensor(t, t, x, ALU.mult))
                    link(v.tensor_scalar(t, t, -0.5, 1.5, ALU.mult, ALU.add))
                    link(v.tensor_tensor(out_, out_, t, ALU.mult))

            low_features("fx", 2)
            split_lo(dve, v, 1, st, 1)
            for g in range(4):
                split_to(("gate", g))

            def pooled_lo(g):
                for c in range(0, 4, 2):
                    dve.wait_ge(*after("phi", g, c))
                    v.tensor_tensor(plo[:, c:c + 2, :], src("pooled", g, c).rearrange("p (a b) -> p a b", a=2),
                                    phi[:, c:c + 2, :].bitcast(F32), ALU.subtract).then_inc(
                        *did("vector", ("pooled split", g, c), ("read", "pooled", g, c)))

            def gate_mixed(g):
                for e in range(4):
                    i = g * 4 + e
                    dve.wait_ge(*after("mixed", g, e))
                    dve.wait_ge(*after("sgate", i))
                    v.scalar_tensor_tensor(out=sgate[:, i, :], in0=src("mixed", g, e)[:, 0:S], scalar=scol[:, i:i + 1],
                                           in1=sgate[:, i, :], op0=ALU.mult, op1=ALU.mult).then_inc(
                        *did("vector", ("ymul", i), ("read", "mixed", g, e)))
                for e in range(4):
                    i = g * 4 + e
                    dve.wait_ge(*after("yhi", i))
                    v.tensor_tensor(ylo[:, i, :], sgate[:, i, :], yhi[:, i, :].bitcast(F32), ALU.subtract).then_inc(
                        *did("vector", ("y", i)))

            dve.wait_ge(loads["scol"], 16)
            for g in range(4):
                split_to(("u", g))
                if g == 1:
                    pooled_lo(0)
                if g:
                    split_to(("grp", g - 1))
                    gate_mixed(g - 1)
                    pooled_lo(g)
            split_to(("grp", 3))
            gate_mixed(3)

            def add_residual(name, n, t):
                dve.wait_ge(*after(name, n, t))
                hh = hx[:, t, n * NW:(n + 1) * NW]
                v.scalar_tensor_tensor(out=hh, in0=hh, scalar=ALPHA, in1=src(name, n, t), op0=ALU.mult, op1=ALU.add).then_inc(
                    *did("vector", ("read", name, n, t)))

            def layer_norm(i, rows, name, count):
                for t in range(XT):
                    for n in range(2):
                        dve.wait_ge(*after("read", name, n, t))
                        link(v.bn_stats(stats[:, t, n, :], hx[:, t, n * NW:(n + 1) * NW]))
                    link(v.bn_aggr(mv[:, t, :], stats[:, t, :, :].rearrange("p a b -> p (a b)")))
                    rsqrt(rstd[:, t:t + 1], mv[:, t, 1:2], 1, LN_EPS)
                    link(v.tensor_scalar(hx[:, t, :], hx[:, t, :], mv[:, t, 0:1], rstd[:, t:t + 1], ALU.subtract, ALU.mult))
                    dve.wait_ge(loads[count], 32)
                    link(v.tensor_tensor(hx[:, t, :], hx[:, t, :], rows[:, 0, :], ALU.mult))
                    link(v.tensor_tensor(hx[:, t, :], hx[:, t, :], rows[:, 1, :], ALU.add), ("ln", i, t))

            for n in range(2):
                for kh in range(2):
                    split_to(("outa", n, kh))
                for t in range(XT):
                    add_residual("outa", n, t)
            layer_norm(0, lnrow_a, "outa", "lna")
            low_features("f1", 2)
            split_to(("k", 0, 0), 0)

            def mod_row(l, j):
                dve.wait_ge(*after("mod", l, j))
                if l or j:
                    dve.wait_ge(loads["modsave"], 16 * (12 * l + j))
                v.tensor_copy(modrow[:, :], src("mod", l, j)[0:2, :]).then_inc(*did("vector", ("read", "mod", l, j)))

            def maxima(i, it):
                kind, l, h, t = it
                parts, kt, _ = item_info(it)
                dve.wait_ge(*after("s", it))
                if kind in "AB":
                    for j, n in parts:
                        ins = v.reduce_max(nmax[:, i % 4, j:j + 1], src("s", it, j)[:, 0:n], AX_X, negate=True)
                    ins.then_inc(*did("vector", ("max", it)))
                    return
                if i >= 3:
                    _, kb, _ = item_info(items[i - 3])
                    dve.wait_ge(*after("t", items[i - 3], (kb - 1) // 4 * 4))
                e = (e1 if kind == "first" else EE[l])[:, i % 3, :]
                if kind == "first":
                    n = parts[0][1]
                    for g in range(NG):
                        bank = 0 if not t or g < 2 else 1
                        a = src("s", it, bank)[:, (0 if bank else g * n):(0 if bank else g * n) + n]
                        labels = []
                        if (t and g >= 1) or g == 2:
                            labels.append(("read", "s", it, bank))
                        ins = v.scalar_tensor_tensor(out=e[:, g * n:(g + 1) * n], in0=dist[:, g, 256 - n:256],
                                                     scalar=-SLOPES[g][l * 8 + h], in1=a, op0=ALU.mult, op1=ALU.add)
                        if labels and g < 2:
                            ins.then_inc(*did("vector", *labels))
                    link(ins, *labels)
                else:
                    a = src("s", it, 0)
                    v.tensor_tensor(e[:, 0:S], a[:, 0:S], band[:, t, :] if kind == "C" else bias_d(h, t), ALU.add).then_inc(
                        *did("vector", ("biased", it)))
                    link(v.tensor_copy(e[:, S:2 * S], a[:, S:2 * S]), ("read", "s", it, 0))
                ins = v.reduce_max(nmax[:, i % 4, 0:1], e[:, 0:kt * P], AX_X, negate=True)
                if kind == "C":
                    link(ins)
                    ins = v.tensor_tensor(nmax[:, i % 4, 0:1], nmax[:, i % 4, 0:1], nsink[:, h:h + 1], ALU.min)
                ins.then_inc(*did("vector", ("max", it)))

            def combine(i, it):
                _, kt, _ = item_info(it)
                n = kt * P
                e = EE[0][:, i % 3, :]
                dve.wait_ge(*after("exp", it))
                link(v.reciprocal(rinv[:, i % 4, :], rsum[:, i % 4, :]))
                link(v.tensor_scalar(rinv[:, i % 4, 1:2], rinv[:, i % 4, 1:2], lam[:, 3:4], None, ALU.mult))
                link(v.tensor_scalar(e[:, 512:512 + n], e[:, 512:512 + n], rinv[:, i % 4, 1:2], None, ALU.mult))
                v.scalar_tensor_tensor(out=e[:, 0:n], in0=e[:, 0:n], scalar=rinv[:, i % 4, 0:1], in1=e[:, 512:512 + n],
                                       op0=ALU.mult, op1=ALU.add).then_inc(*did("vector", ("probs", it)))

            def outputs(i, it):
                kind, l, h, t = it
                dve.wait_ge(*after("o", it))
                if kind != "B":
                    dve.wait_ge(*after("exp", it))
                    if kind == "C":
                        link(v.tensor_tensor(rsum[:, i % 4, 0:1], rsum[:, i % 4, 0:1], esink[:, i % 4:i % 4 + 1], ALU.add))
                    link(v.reciprocal(rinv[:, i % 4, 0:1], rsum[:, i % 4, 0:1]))
                if kind == "first":
                    g = gb[:, t, (l * 8 + h) * DH:(l * 8 + h + 1) * DH]
                    dve.wait_ge(*after("gbs", l, t))
                    v.scalar_tensor_tensor(out=g, in0=src("o", it)[:, 0:DH], scalar=rinv[:, i % 4, 0:1], in1=g,
                                           op0=ALU.mult, op1=ALU.mult).then_inc(*did("vector", ("gated", it), ("read", "o", it)))
                elif kind == "B":
                    v.tensor_copy(mix[:, t, NW + h * P:NW + (h + 1) * P], src("o", it)[:, 0:P]).then_inc(
                        *did("vector", ("read", "o", it)))
                else:
                    at = (NW if kind == "D" else 0) + h * DH
                    v.tensor_scalar(mix[:, t, at:at + DH], src("o", it)[:, 0:DH], rinv[:, i % 4, 0:1], None, ALU.mult).then_inc(
                        *did("vector", ("read", "o", it), *([("mixed out", 1, t)] if kind == "D" and h == 7 else [])))

            def attend(items, mods):
                for i in range(len(items) + 3):
                    if i < len(items):
                        maxima(i, items[i])
                    for m in mods_at(i, items, mods):
                        mod_row(*m)
                    if items[0][0] == "B" and 0 <= i - 1 < len(items):
                        combine(i - 1, items[i - 1])
                    if 0 <= i - 3 < len(items):
                        outputs(i - 3, items[i - 3])

            def mod_columns(l):
                dve.wait_ge(*after("modT", l))
                dve.wait_ge(loads["modb"], 16)
                dve.wait_ge(loads["normc"], 16)
                link(v.tensor_tensor(modT[:, :, :], src("modT", l)[:, 0:96].rearrange("p (a b) -> p a b", a=2),
                                     heads_view(modb[:, l, :], (0, 2), (1, 48)), ALU.add), ("read", "modT", l))
                for which in range(2):
                    base = 3 * which * KD
                    gain = heads_view(normc[:, l, 2 * which, :], (0, 2), (1, KD))
                    v.tensor_copy(modB[:, l, which, :, :], modT[:, :, base:base + KD]).then_inc(*did("vector"))
                    v.scalar_tensor_tensor(out=modA[:, l, which, :, :], in0=modT[:, :, base + KD:base + 2 * KD], scalar=1.0,
                                           in1=gain, op0=ALU.add, op1=ALU.mult).then_inc(*did("vector"))
                    gain = heads_view(normc[:, l, 2 * which + 1, :], (0, 2), (1, KD))
                    ins = v.tensor_tensor(gcol[:, which, :, :], modT[:, :, base + 2 * KD:base + 3 * KD], gain, ALU.mult)
                    ins.then_inc(*did("vector", *([("gcol", l)] if which else [])))
                dve.wait_ge(*after("grow", l))
                if l:
                    dve.wait_ge(loads["gsave"], 16 * l)
                v.tensor_copy(grow[:, :], src("grow", l)[0:32, 0:P]).then_inc(*did("vector", ("growc", l), ("read", "grow", l)))

            dve.wait_ge(loads["dist"], 16)
            for hf in range(2):
                for what in ("k", "q", "v"):
                    for g in range(NG):
                        split_to((what, hf, g))
                items = items_first(hf)
                attend(items, mods_first(hf))
                split_to(("gb", hf), 2)
            low_features("fo1", 2)
            split_to(("outb", 1), 1)
            for n in range(2):
                for t in range(XT):
                    add_residual("outb", n, t)
            mod_columns(0)
            layer_norm(1, lnrow_b, "outb", "lnb")

            def normed(l, which, t):
                dve.wait_ge(*after("sq", l, which, t))
                rsqrt(rstd[:, t:t + 1], sumsq[:, t:t + 1], D, EPS)
                v.tensor_scalar(mix[:, t, :], H(t), rstd[:, t:t + 1], None, ALU.mult).then_inc(
                    *did("vector", ("xn", l, which, t)))

            def residual(l, which, t):
                vec = 0 if t < XT else 1
                if t == 0:
                    dve.wait_ge(loads[f"g{l}{which}"], 16 * (2 - l))
                dve.wait_ge(*after("sqh", l, which, t, 1))
                link(v.tensor_tensor(rstd[:, 4 + t:5 + t], sumh[:, t, 0:1], sumh[:, t, 1:2], ALU.add))
                rsqrt(rstd[:, 4 + t:5 + t], rstd[:, 4 + t:5 + t], D, EPS)
                link(v.scalar_tensor_tensor(out=mix[:, t, :], in0=mix[:, t, :], scalar=rstd[:, 4 + t:5 + t],
                                            in1=gates[:, vec, :], op0=ALU.mult, op1=ALU.mult))
                labels = [("resid", l, which, t)] + ([("final", t)] if l and which else [])
                link(v.tensor_tensor(H(t), H(t), mix[:, t, :], ALU.add), *labels)

            def stage(what, l, part, t):
                key = (what, l, part, t)
                small = what == "k" and part == 0
                norm = l == 0 and part == 0
                if t >= XT and not norm and not small:
                    return
                w = P if small else NW
                nh = w // DH
                r = STAGE[key]
                a = src(what + "2", l, part, t)
                e = EE[l][:, r, :]
                i = 0 if what == "q" else 1
                dve.wait_ge(*after(what + "2", l, part, t))
                if STAGE_BEFORE[key]:
                    dve.wait_ge(*after(*STAGE_BEFORE[key]))
                if norm:
                    dve.wait_ge(*after("squared", *key))
                    link(v.reduce_sum(hss[:, r, 0:nh], e[:, 512:512 + w].rearrange("p (h d) -> p h d", d=DH), AX_X))
                    rsqrt(hrs[:, r, 0:nh], hss[:, r, 0:nh], DH, EPS)
                elif small:
                    dve.wait_ge(*after("vv", l, part, t))
                read = ("read", what + "2", l, part, t)
                heads = lambda ap: ap.rearrange("p (h d) -> p h d", d=DH)
                if t < XT:
                    cos = ropeg[:, i, 0, t, :] if norm else RO[l][:, 0, t, :]
                    sin = ropeg[:, i, 1, t, :] if norm else RO[l][:, 1, t, :]
                    v.tensor_tensor(heads(e[:, 512:512 + w]), heads(a[:, 0:w]), heads_view(cos, (0, nh), (1, DH)), ALU.mult).then_inc(
                        *did("vector"))
                    for half in range(2):
                        out_ = e[:, 0:w].rearrange("p (h x f d) -> p h x f d", x=2, f=2, d=16)[:, :, :, half, :]
                        in_ = a[:, 0:w].rearrange("p (h x f d) -> p h x f d", x=2, f=2, d=16)[:, :, :, 1 - half, :]
                        ins = v.tensor_tensor(out_, in_, heads_view(sin[:, half * 16:], (0, nh), (32, 2), (1, 16)), ALU.mult)
                        if half == 0:
                            ins.then_inc(*did("vector"))
                    link(ins, read)
                    if norm:
                        link(v.tensor_tensor(e[:, 0:w], e[:, 0:w], e[:, 512:512 + w], ALU.add))
                elif norm:
                    link(v.tensor_tensor(heads(e[:, 0:w]), heads(a[:, 0:w]), heads_view(qkg[:, i, :], (0, nh), (1, DH)), ALU.mult), read)
                if small:
                    dup = lambda ap: heads_view(ap, (DH, 2), (0, 2), (1, DH))
                    dst = e[:, 256:512].rearrange("p (h c d) -> p h c d", h=2, c=2)
                    if norm:
                        ins = v.tensor_tensor(dst, dup(e[:, 0:w]), heads_view(hrs[:, r, 0:2], (1, 2), (0, 2), (0, DH)), ALU.mult)
                    elif t < XT:
                        ins = v.tensor_tensor(dst, dup(e[:, 0:w]), dup(e[:, 512:512 + w]), ALU.add)
                    else:
                        v.tensor_copy(dst, dup(a[:, 0:w])).then_inc(*did("vector", ("staged",) + key, read))
                        return
                elif norm:
                    ins = v.tensor_tensor(heads(e[:, 0:w]), heads(e[:, 0:w]), heads_view(hrs[:, r, 0:nh], (1, nh), (0, DH)), ALU.mult)
                else:
                    ins = v.tensor_tensor(e[:, 0:w], e[:, 0:w], e[:, 512:512 + w], ALU.add)
                ins.then_inc(*did("vector", ("staged",) + key))

            for l in range(2):
                nt = 4 if l == 0 else 2
                for t in TILES[l]:
                    normed(l, 0, t)
                split_to(*((("outb", 1), 2) if l == 0 else (("q2", 1, 0), 1)))
                if l == 0:
                    dve.wait_ge(loads["ropes"], 64)
                    for i in range(2):
                        v.tensor_tensor_reduce(lamrow[:, 2 * i, :], lamrow[:, 2 * i, :], lamrow[:, 2 * i + 1, :], 1.0, 0.0,
                                               ALU.mult, ALU.add, lam[:, i:i + 1]).then_inc(
                            *did("vector", *([("lam sums",)] if i else [])))
                modulate(("n1", l), 4, l, 0)
                if l == 0:
                    dve.wait_ge(*after("lam exp"))
                    link(v.tensor_tensor(lam[:, 2:3], lam[:, 1:2], lam[:, 0:1], ALU.subtract))
                    link(v.tensor_scalar(lam[:, 3:4], lam[:, 2:3], -LAM0, None, ALU.add))
                    link(v.tensor_scalar(sublng[:, :], sublng[:, :], 1.0 - LAM0, None, ALU.mult))
                    for i in range(2):
                        v.tensor_tensor(ropeg[:, i, 0, :, :], rope[:, 0, :, :], heads_view(qkg[:, i, :], (0, 2), (1, DH)),
                                        ALU.mult).then_inc(*did("vector"))
                        for half in range(2):
                            halves = lambda ap: ap.rearrange("p t (x f d) -> p t x f d", x=2, f=2)[:, :, :, half, :]
                            link(v.tensor_tensor(halves(ropeg[:, i, 1, :, :]), halves(rope[:, 1, :, :]),
                                                 heads_view(qkg[:, i, 16 * (1 - half):], (0, 2), (32, 2), (1, 16)), ALU.mult))
                else:
                    dve.wait_ge(loads["odd"], 64)
                    link(v.tensor_scalar(nsink[:, :], sinkr[:, :], -1.0, None, ALU.mult))
                for part in range(2):
                    if l == 1 and part == 1:
                        split_to(("q2", l, 1))
                        split_to(("k2", l, 1))
                    else:
                        for what, tiles in (("q", range(nt)), ("k", range(4))):
                            split_to((what + "2", l, part), 0 if what == "k" and part == 0 and l == 0 else 1)
                            for t in tiles:
                                stage(what, l, part, t)
                    if part == 1:
                        split_to(("v2", l, 1), l)
                    if l == 1 and part == 1:
                        dve.wait_ge(loads["bias"], 16 * 32)
                        for h in range(8):
                            for t in range(2):
                                b = bias_d(h, t)
                                ins = v.tensor_tensor(b, b, colmask[:, :], ALU.add)
                                ins.then_inc(*did("vector"))
                        dve.wait_ge(counts.sems["vector"], counts.now["vector"])
                    items = items_second(l, part)
                    attend(items, mods_second(l, part))
                    split_to(("q2", l, 1) if part == 0 else ("out2", l, 0), 1)
                if l == 0:
                    for t in range(4):
                        m = mix[:, t, NW:2 * NW].rearrange("p (h d) -> p h d", d=P)
                        e = e2[:, t % 3, 0:NW].rearrange("p (h d) -> p h d", d=P)
                        dve.wait_ge(counts.sems["vector"], counts.now["vector"])
                        link(v.tensor_tensor(e, m, m, ALU.mult))
                        link(v.reduce_sum(hss[:, 0, 0:4], e, AX_X))
                        rsqrt(hrs[:, 0, 0:4], hss[:, 0, 0:4], P, EPS)
                        link(v.tensor_tensor(m, m, heads_view(hrs[:, 0, 0:4], (1, 4), (0, P)), ALU.mult))
                        link(v.tensor_tensor(m, m, heads_view(sublng[:, :], (0, 4), (1, P)), ALU.mult), ("mixed out", 0, t))
                    mod_columns(1)
                low_features(("fo", l), nt)
                for n in range(2):
                    split_to(("out2", l, n))
                split_to(("in", l, 0), 1)
                for t in range(nt):
                    residual(l, 0, t)
                for t in range(nt):
                    normed(l, 1, t)
                modulate(("n2", l), nt, l, 1)
                for j in range(9):
                    if j < 8:
                        split_to(("in", l, j))
                        for e in range(4):
                            h = htmp[:, e % 2, 0:nt * P]
                            dve.wait_ge(*after("relu", l, j, e))
                            v.tensor_tensor(h, h, h, ALU.mult).then_inc(*did("vector", ("squared", l, j, e)))
                    if j:
                        split_to(("out", l, j - 1))
                        if l == 0 or j == 8:
                            for n in range(2):
                                for t in range(nt):
                                    m = mix[:, t, n * NW:(n + 1) * NW]
                                    key = ("acc", t, n) if l else ("acc", j - 1, t, n)
                                    dve.wait_ge(*after(*key))
                                    if l == 0 and j > 1:
                                        dve.wait_ge(*after("read", "acc", j - 2, t, n))
                                        ins = v.tensor_tensor(m, src(*key), m, ALU.add)
                                    else:
                                        ins = v.tensor_copy(m, src(*key))
                                    ins.then_inc(*did("vector", ("read",) + key, *([("summed", l, t)] if j == 8 and n else [])))
                for t in range(nt):
                    residual(l, 1, t)

        @block.gpsimd
        def _(pool):
            p = nc.gpsimd
            st = [0]

            def split_to(name, ahead=1):
                split_lo(pool, p, UNIT[name].wn + ahead, st, 0)

            def low_modulated(name, nt, l, which):
                per = 4 // nt
                for j in range(KD // per):
                    pool.wait_ge(*after("fhi", name, j))
                    dst = flo[:, j * per:(j + 1) * per, 0:nt * P]
                    hi = fhi[:, j * per:(j + 1) * per, 0:nt * P].bitcast(F32)
                    p.tensor_tensor(dst, ftmp(l, which, j).rearrange("p (a b) -> p a b", a=per), hi, ALU.subtract).then_inc(
                        *did("pool", ("split", name, j)))

            for l in range(2):
                nt = 4 if l == 0 else 2
                split_to(*((("outb", 1), 2) if l == 0 else (("q2", 1, 0), 1)))
                low_modulated(("n1", l), 4, l, 0)
                split_to(("in", l, 0), 1)
                low_modulated(("n2", l), nt, l, 1)
                for j in range(9):
                    if j < 8:
                        split_to(("in", l, j))
                        for e in range(4):
                            pool.wait_ge(*after("hhi", l, j, e))
                            p.tensor_tensor(hlo[:, j % 2, e, 0:nt * P], htmp[:, e % 2, 0:nt * P],
                                            hhi[:, j % 2, e, 0:nt * P].bitcast(F32), ALU.subtract).then_inc(
                                *did("pool", ("hidden", l, j, e)))
                    if j:
                        split_to(("out", l, j - 1))


def kernel(**inputs):
    import numpy as _np
    import concourse.bacc as _bacc
    from concourse import mybir as _mybir
    from concourse.bass_utils import run_bass_kernel_spmd as _run

    a = {k: _np.asarray(x) for k, x in inputs.items()}
    f32 = _np.float32
    stream = _np.empty((CHUNKS, P, CHUNK), f32)
    n = 0
    for u in UNITS:
        for name, idx, row, col in u.pieces:
            block = a[name][idx][row:row + u.nk * P, col:col + u.width]
            stream[n] = block.reshape(u.nk, P, u.width).transpose(1, 0, 2).reshape(P, CHUNK)
            n += 1

    def cols(x):
        y = x.reshape(x.shape[:-1] + (x.shape[-1] // P, P))
        return _np.ascontiguousarray(_np.moveaxis(y, -1, 0))

    rows = _np.zeros((8, 7, P), f32)
    rows[:, :, GRID - 16:GRID + 15] = a["rpb_d_2"][0, :, 4:11, :]
    arrays = {
        "wstream": stream,
        "x": a["x"], "ctx_2": a["ctx_2"],
        "cond": _np.ascontiguousarray(_np.moveaxis(cols(_np.stack([a["c_2"][0], a["c_ctx_2"]])), 1, 2)),
        "scale_cols": cols(a["scale_a"][0]),
        "b_mod_cols": cols(a["b_mod_2"]), "norm_cols": cols(a["norm_g_2"]),
        "ln_g": a["ln_g"], "ln_b": a["ln_b"],
        "qk_norm_a_2": a["qk_norm_a_2"], "diff_lambda_2": a["diff_lambda_2"],
        "diff_subln_2": a["diff_subln_2"], "sink_c_2": a["sink_c_2"],
        "rpb_rows": _np.ascontiguousarray(_np.broadcast_to(rows[:, :, None, :], (8, 7, GRID, P))),
        **constants(),
    }
    arrays = {k: _np.ascontiguousarray(x) for k, x in arrays.items()}

    counts = None
    for _ in range(2):
        nc = _bacc.Bacc("TRN2", target_bir_lowering=False, num_devices=1)
        T = {k: nc.dram_tensor("in_" + k, x.shape, _mybir.dt.float32, kind="ExternalInput").ap() for k, x in arrays.items()}
        out = nc.dram_tensor("out", (1, S, D), _mybir.dt.float32, kind="ExternalOutput").ap()
        counts = Counts(counts)
        build(nc, T, out, counts)
    r = _run(nc, [{"in_" + k: x for k, x in arrays.items()}], core_ids=[0])
    return r.results[0]["out"]
```

```python
from contextlib import ExitStack

import concourse.bass as bass
import numpy as np
from concourse import mybir

F32 = mybir.dt.float32
F32R = mybir.dt.float32r
I32 = mybir.dt.int32
ALU = mybir.AluOpType
ACT = mybir.ActivationFunctionType
AX_X = mybir.AxisListType.X

P = 128
D = 1024
KD = D // P
S = 256
XT = S // P
NW = 512
D_A = 2 * D
POOL_WINDOWS = (2, 4, 8, 16)
PAIRS = ((128, 1), (512, 4), (2048, 16))
NG = len(PAIRS)
HEADS = 16
DH = 64
ALPHA = 4.0 ** 0.25
LN_EPS = 1e-5
EPS = 1e-6
LAM0 = 0.8 - 0.6
QSCALE = DH ** -0.5
GRID = 64
MASKED = -1e30
RSQRT_START = float(0x5F3759DF)
NEWTON_STEPS = 3
FAR = 3e32
SLOPES = [[2.0 ** (-8.0 * (g * HEADS + h + 1) / (NG * HEADS)) for h in range(HEADS)] for g in range(NG)]

CHUNK = 2048
RAW_SLOTS = 3
SPLIT_SLOTS = 4
ETILE = 1024


class Unit:

    def __init__(self, name, kind, nk, width, pieces):
        self.name, self.kind, self.nk, self.width, self.pieces = name, kind, nk, width, pieces


MODS = {
    ("k", 0, 0): [(0, j) for j in range(0, 2)],
    ("k", 1, 0): [(0, j) for j in range(2, 5)],
    ("outb", 0): [(0, j) for j in range(5, 8)],
    ("q2", 0, 0): [(0, j) for j in range(8, 12)],
    ("q2", 0, 1): [(1, j) for j in range(0, 3)],
    ("out2", 0, 0): [(1, j) for j in range(3, 5)],
    ("in", 0, 0): [(1, j) for j in range(5, 7)],
    ("q2", 1, 0): [(1, j) for j in range(7, 10)],
    ("q2", 1, 1): [(1, j) for j in range(10, 12)],
}


def plan_units():
    units = []

    def std(name, src, idx, row, col, kind="w"):
        units.append(Unit(name, kind, 4, NW, [(src, idx, row, col), (src, idx, row + 512, col)]))


    for g in range(4):
        std(("gate", g), "w_in_a", (0,), 0, D_A + g * NW)
    grp = [Unit(("grp", g), "w", 4, NW, [("w_grp_a", (0, g), 0, 0)]) for g in range(4)]
    for g in range(4):
        std(("u", g), "w_in_a", (0,), 0, g * NW)
        if g:
            units.append(grp[g - 1])
    units.append(grp[3])
    for n in range(2):
        for kh in range(2):
            std(("outa", n, kh), "w_out_a", (0,), kh * D, n * NW)
    for hf in range(2):
        for g in range(NG):
            std(("k", hf, g), "w_kv", (), 0, g * D + hf * NW)
        for g in range(NG):
            std(("q", hf, g), "w_in_b", (0,), 0, g * D + hf * NW)
        for g in range(NG):
            std(("v", hf, g), "w_kv", (), 0, (NG + g) * D + hf * NW)
        std(("gb", hf), "w_in_b", (0,), 0, NG * D + hf * NW)
    for n in range(2):
        std(("outb", n), "w_out_b", (0,), 0, n * NW)
    for l in range(2):
        std(("q2", l, 0), "w_in_2", (l,), 0, 0)
        units.append(Unit(("k2", l, 0), "w", 8, 256, [("w_in_2", (l,), 0, 512)]))
        std(("q2", l, 1), "w_in_2", (l,), 0, 768)
        std(("k2", l, 1), "w_in_2", (l,), 0, 1280)
        std(("v2", l, 1), "w_in_2", (l,), 0, 1792)
        for n in range(2):
            std(("out2", l, n), "w_out_2", (l,), 0, n * NW)
        for j in range(9):
            if j < 8:
                std(("in", l, j), "w_mlp_in_2", (l,), 0, j * NW)
            if j:
                units.append(Unit(("out", l, j - 1), "w", 4, NW,
                                  [("w_mlp_out_2", (l,), (j - 1) * NW, n * NW) for n in range(2)]))
    weights, units = units, []
    for u in weights:
        units.append(u)
        for layer, j in MODS.get(u.name, []):
            std(("mod", layer, j), "w_mod_2", (layer,), 0, j * NW, "mod")
    c = w = 0
    for n, u in enumerate(units):
        u.at, u.c0, u.w0 = n, c, w
        c += len(u.pieces)
        if u.kind == "w":
            w += len(u.pieces)
    return units


UNITS = plan_units()
UNIT = {u.name: u for u in UNITS}
CHUNKS = sum(len(u.pieces) for u in UNITS)
assert CHUNKS % RAW_SLOTS == 0
SPLIT = [(u.c0 + i, u) for u in UNITS if u.kind == "w" for i in range(len(u.pieces))]
WUNITS = [u for u in UNITS if u.kind == "w"]
for _n, _u in enumerate(WUNITS):
    _u.wn = _n


def constants():
    s = np.arange(S)
    pool = np.zeros((P, 4, 272), np.float32)
    for g, w in enumerate(POOL_WINDOWS):
        m = np.zeros((S, S))
        for t in range(S):
            m[t, max(0, t - w + 1):t + 1] = 1.0 / min(t + 1, w)
            m[t, t] -= 1.0
        pool[:, g, :144] = m[:144, :P].T
        pool[:, g, 144:] = m[P:, P:].T
    dist = np.zeros((P, NG, 256), np.float32)
    for g, (window, dilation) in enumerate(PAIRS):
        rel = P + np.arange(P)[:, None] - np.arange(256)[None, :]
        ok = (rel >= 0) & (rel <= window) & (rel % dilation == 0)
        dist[:, g] = np.where(ok, rel, FAR)
    pos = np.stack([s // GRID, s % GRID], -1).astype(np.float32)
    inv = (np.float32(10000.0) ** (-np.arange(16, dtype=np.float32) / np.float32(16))).astype(np.float32)
    ang = pos[..., None] * inv
    cos, sin = np.cos(ang), np.sin(ang)
    rc = np.stack([cos, cos], 2).reshape(2, P, DH).transpose(1, 0, 2)
    rs = np.stack([-sin, sin], 2).reshape(2, P, DH).transpose(1, 0, 2)
    band = np.zeros((P, 2, S), np.float32)
    for qt in range(2):
        band[:, qt] = np.where(np.abs(qt * P + np.arange(P)[:, None] - s[None]) <= P, 0.0, MASKED)
    cq = (np.arange(P) % GRID)[:, None]
    ck = (s % GRID)[None]
    start = np.clip(cq - 8, 0, GRID - 16)
    cols = np.where((ck >= start) & (ck < start + 16), 0.0, MASKED)
    out = {"t_ident": np.eye(P), "t_pool": pool.reshape(P, -1), "t_dist": dist.reshape(P, -1),
           "t_rope": np.stack([rc, rs], 1).reshape(P, -1), "t_band": band.reshape(P, -1), "t_cols": cols}
    return {k: np.ascontiguousarray(v, dtype=np.float32) for k, v in out.items()}


def plan_stage():
    slot, before = {}, {}
    for l in range(2):
        for part in range(2 - l):
            tiles = [("q", l, part, t) for t in range(4 if l == 0 else 2)] + [("k", l, part, t) for t in range(4)]
            for n, key in enumerate(tiles):
                slot[key] = n % 3
                before[key] = (tiles[n - 3][0] + "turn",) + tiles[n - 3][1:] if n >= 3 else None
    return slot, before


STAGE, STAGE_BEFORE = plan_stage()


class Counts:

    def __init__(self, known=None):
        self.known, self.now, self.marks, self.banks = known, {}, {}, {}
        self.sems = {}

    def did(self, sem, *labels):
        n = self.now[sem] = self.now.get(sem, 0) + 1
        for label in labels:
            assert label not in self.marks, label
            self.marks[label] = (sem, n)
        return self.sems[sem], 1

    def used(self, c, *labels):
        sem, n = f"raw_used{c % RAW_SLOTS}", c // RAW_SLOTS + 1
        for label in labels:
            self.marks[label] = (sem, n)
        return self.sems[sem], 1

    def after(self, *label):
        if self.known is None:
            return self.sems["tensor"], 1
        sem, n = self.known.marks[label]
        return self.sems[sem], n

    def bank(self, *label):
        return 0 if self.known is None else self.known.banks[label]


def heads_view(ap, *dims):
    return bass.AP(tensor=ap.tensor, offset=ap.offset, ap=[list(ap.ap[0])] + [list(d) for d in dims])


def rows_to_all(ap, offset, n):
    return bass.AP(tensor=ap.tensor, offset=ap.offset + offset, ap=[[0, P], [1, n]])


def build(nc, T, out, counts):
    did, after = counts.did, counts.after
    with ExitStack() as ctx:
        def sem(name):
            s = ctx.enter_context(nc.semaphore(name))
            counts.sems[name] = s
            return s

        def tile(stack, name, shape, dt=F32):
            return stack.enter_context(nc.sbuf_tensor(name, shape, dt))

        raw = tile(ctx, "raw", [P, RAW_SLOTS, CHUNK])
        whi = tile(ctx, "whi", [P, SPLIT_SLOTS, CHUNK], F32R)
        wlo = tile(ctx, "wlo", [P, SPLIT_SLOTS, CHUNK], F32R)
        fhi = tile(ctx, "fhi", [P, KD, 512], F32R)
        flo = tile(ctx, "flo", [P, KD, 512], F32R)
        hx = tile(ctx, "hx", [P, XT, D])
        ident = tile(ctx, "ident", [P, P])
        cond = tile(ctx, "cond", [P, KD, 2])
        modrow = tile(ctx, "modrow", [2, NW])
        modc = tile(ctx, "modc", [64, P])
        lncol = tile(ctx, "lncol", [P, 2, KD])
        eps = tile(ctx, "eps", [P, 2])
        modb = tile(ctx, "modb", [P, 2, 48])
        normc = tile(ctx, "normc", [P, 2, 4, KD])
        modT = tile(ctx, "modT", [P, 2, 32])
        modA = tile(ctx, "modA", [P, 2, 2, 2, KD])
        modB = tile(ctx, "modB", [P, 2, 2, 2, KD])
        gcol = tile(ctx, "gcol", [P, 2, 2, KD])
        grow = tile(ctx, "grow", [32, P])
        scol = tile(ctx, "scol", [P, 16])
        stats = tile(ctx, "stats", [P, XT, 2, 6])
        mv = tile(ctx, "mv", [P, XT, 2])
        rstd = tile(ctx, "rstd", [P, 8])
        dev = tile(ctx, "dev", [P, 8])
        sumsq = tile(ctx, "sumsq", [P, 4])
        sumh = tile(ctx, "sumh", [P, 4, 2])
        newton = tile(ctx, "newton", [P, 2, 8])
        hss = tile(ctx, "hss", [P, 3, 8])
        hrs = tile(ctx, "hrs", [P, 3, 8])
        nmax = tile(ctx, "nmax", [P, 4, 2])
        rsum = tile(ctx, "rsum", [P, 4, 2])
        rinv = tile(ctx, "rinv", [P, 4, 2])
        esink = tile(ctx, "esink", [P, 4])
        lam = tile(ctx, "lam", [P, 4])

        one = ExitStack()
        gsil_a = ExitStack()
        sgate = tile(gsil_a, "sgate", [P, 16, S])
        yhi = tile(gsil_a, "yhi", [P, 16, S], F32R)
        ylo = tile(gsil_a, "ylo", [P, 16, S], F32R)
        sub = ExitStack()
        utok = tile(sub, "utok", [P, XT, NW])
        phi = tile(sub, "phi", [P, 4, S], F32R)
        plo = tile(sub, "plo", [P, 4, S], F32R)
        poolT = tile(sub, "poolT", [P, 4, 272])
        sub.close()
        gsil_a.close()
        kT1 = tile(one, "kT1", [P, NG * 4, S])
        qT1 = tile(one, "qT1", [P, NG * 4, S])
        v1 = tile(one, "v1", [P, XT, NG, NW])
        gb = tile(one, "gb", [P, XT, D])
        e1 = tile(one, "e1", [P, 3, 768])
        p1 = tile(one, "p1", [P, 2, 768])
        dist = tile(one, "dist", [P, NG, 256])
        lnrow = tile(one, "lnrow", [P, 2, D])
        one.close()
        hc = tile(ctx, "hc", [P, XT, D])
        mix = tile(ctx, "mix", [P, 4, D])
        att = ExitStack()
        kT = tile(att, "kT", [P, 4, 512])
        qT = tile(att, "qT", [P, 4, 512])
        vv = tile(att, "vv", [P, 4, 512])
        e2 = tile(att, "e2", [P, 3, ETILE])
        p2 = tile(att, "p2", [P, 2, 512])
        rope = tile(att, "rope", [P, 2, 2, DH])
        ropeg = tile(att, "ropeg", [P, 2, 2, 2, DH])
        qkg = tile(att, "qkg", [P, 2, DH])
        sublng = tile(att, "sublng", [P, P])
        lamrow = tile(att, "lamrow", [P, 4, DH])
        subtmp = tile(att, "subtmp", [P, NW])
        att.close()
        ffn = ExitStack()
        hhi = tile(ffn, "hhi", [P, 2, 4, 512], F32R)
        hlo = tile(ffn, "hlo", [P, 2, 4, 512], F32R)
        htmp = tile(ffn, "htmp", [P, 2, 512])
        gates = tile(ffn, "gates", [P, 2, D])
        ffn.close()
        att_b = ExitStack()
        kT_b = tile(att_b, "kT_b", [P, 4, 512])
        qT_b = tile(att_b, "qT_b", [P, 4, 512])
        vv_b = tile(att_b, "vv_b", [P, 4, 512])
        e2_b = tile(att_b, "e2_b", [P, 3, ETILE])
        p2_b = tile(att_b, "p2_b", [P, 2, 512])
        rope_b = tile(att_b, "rope_b", [P, 2, 2, DH])
        band = tile(att_b, "band", [P, 2, S])
        colmask = tile(att_b, "colmask", [P, S])
        sinkr = tile(att_b, "sinkr", [P, 8])
        nsink = tile(att_b, "nsink", [P, 8])
        att_b.close()
        KT, QT, VV, EE, PP, RO = (kT, kT_b), (qT, qT_b), (vv, vv_b), (e2, e2_b), (p2, p2_b), (rope, rope_b)

        ps = ctx.enter_context(nc.psum_tensor("ps", [P, 8, 512], F32))
        modd = nc.dram_tensor("modd", (2, 2, 6 * D), F32, kind="Internal").ap()
        gated = nc.dram_tensor("gated", (2, 4, D), F32, kind="Internal").ap()

        for name in ("tensor", "scalar", "vector", "pool"):
            sem(name)
        raw_in = [sem(f"raw_in{i}") for i in range(RAW_SLOTS)]
        for i in range(RAW_SLOTS):
            sem(f"raw_used{i}")
        loads = {}

        def H(t):
            return hx[:, t, :] if t < XT else hc[:, t - XT, :]

        def bias_d(h, t):
            return mix[:, XT + h // 2, (h % 2 * 2 + t) * S:(h % 2 * 2 + t + 1) * S] if h < 4 else \
                hc[:, h // 2 - 2, (h % 2 * 2 + t) * S:(h % 2 * 2 + t + 1) * S]

        def load_sem(name):
            if name not in loads:
                loads[name] = sem("in_" + name)
            return loads[name]

        for name in ("x", "ident", "cond", "pool", "scol", "modb", "normc", "lncol", "lna", "lnb", "dist", "ctx",
                     "ropes", "modsave", "modc00", "modc01", "modc10", "modc11", "gsave", "out",
                     "g00", "g01", "g10", "g11", "bias", "odd"):
            load_sem(name)

        def whalf(which, u, k, c0, c1):
            w = u.w0 + k // u.nk
            base = (k % u.nk) * u.width
            return which[:, w % SPLIT_SLOTS, base + c0:base + c1]

        def items_first(hf):
            return [("first", hf, h, qt) for h in range(8) for qt in range(2)]

        def items_second(l, part):
            if l == 0 and part == 0:
                return [("A", 0, h, t) for h in range(8) for t in range(4)]
            if l == 0:
                return [("B", 0, h, t) for t in range(4) for h in range(4)]
            return [("C" if part == 0 else "D", 1, h, t) for h in range(8) for t in range(2)]

        def mods_first(hf):
            return MODS[("outb", 0) if hf else ("k", 1, 0)]

        def mods_second(l, part):
            return MODS.get(("out2", l, 0) if part else ("q2", l, 1), [])

        def mods_at(i, items, mods):
            every = max(1, len(items) // (len(mods) + 1))
            return [mods[i // every - 1]] if i and i % every == 0 and i // every <= len(mods) else []

        def item_info(it):
            kind, _, h, t = it
            if kind == "first":
                n = 128 * (t + 1)
                return [(g, n) for g in range(NG)], NG * (t + 1), DH
            n = 512 if t < XT else 256
            return [(j, n) for j in range(2 if kind == "B" else 1)], n // P, (P if kind == "B" else DH)

        def key_tile(it, j):
            if it[0] == "first":
                nt = it[3] + 1
                return j // nt, j % nt
            return 0, j + (0 if it[3] < XT else XT)

        block = ctx.enter_context(nc.Block())

        @block.sync
        def _(sp):
            sp.dma_start(hx[:, :, :], T["x"].rearrange("a (t p) d -> p (a t) d", p=P)).then_inc(loads["x"], 16)
            sp.dma_start(ident[:, :], T["t_ident"]).then_inc(loads["ident"], 16)
            for s in range(RAW_SLOTS):
                sp.dma_start(raw[:, s, :], T["wstream"][s]).then_inc(raw_in[s], 16)
            with sp.Fori(1, CHUNKS // RAW_SLOTS) as i:
                for s in range(RAW_SLOTS):
                    sp.wait_ge(counts.sems[f"raw_used{s}"], i)
                    sp.dma_start(raw[:, s, :], T["wstream"][i * RAW_SLOTS + s]).then_inc(raw_in[s], 16)
            for t in range(XT):
                sp.wait_ge(*after("final", t))
                sp.dma_start(out.rearrange("a (t p) d -> t p (a d)", p=P)[t], hx[:, t, :]).then_inc(loads["out"], 16)
            sp.wait_ge(loads["out"], 16 * XT)

        def wait_raw(eng, c):
            eng.wait_ge(raw_in[c % RAW_SLOTS], 16 * (c // RAW_SLOTS + 1))

        @block.tensor
        def _(pe):
            mm = nc.tensor.matmul
            last = {}
            turn = [0]
            state = {"banks": list(range(8))}

            def job(*label):
                banks = state["banks"]
                b = banks[turn[0] % len(banks)]
                turn[0] += 1
                if b in last:
                    pe.wait_ge(*after("read", *last[b]))
                last[b] = label
                counts.banks[label] = b
                return ps[:, b, :]

            def mm3(o, lh, ll, rh, rl, start, stop):
                mm(o, lh, rh, start=start, stop=False)
                mm(o, lh, rl, start=False, stop=False)
                return mm(o, ll, rh, start=False, stop=stop)

            def wait_weights(u):
                for i in range(len(u.pieces)):
                    pe.wait_ge(*after("lo", u.w0 + i))

            def wait_feature(feat, k):
                name, nt = feat
                per = 4 // nt
                if k % per == 0:
                    pe.wait_ge(*after("split", name, k // per))

            def by_token(u, name, tiles, kt=KD, width=NW, feat=None):
                wait_weights(u)
                for t in tiles:
                    o = job(*name, t)
                    for k in range(kt):
                        if feat and t == tiles[0]:
                            wait_feature(feat, k)
                        ins = mm3(o[:, 0:width], fhi[:, k, t * P:t * P + P], flo[:, k, t * P:t * P + P],
                                  whalf(whi, u, k, 0, width), whalf(wlo, u, k, 0, width), k == 0, k == kt - 1)
                    labels = [name + (t,)] + ([("used", u.wn)] if t == tiles[-1] else [])
                    ins.then_inc(*did("tensor", *labels))

            def by_feature(u, name, c0, c1, feat=None):
                wait_weights(u)
                for e in range(4):
                    o = job(*name, e)
                    for k in range(KD):
                        if feat and e == 0:
                            wait_feature(feat, k)
                        ins = mm3(o[:, 0:c1 - c0], whalf(whi, u, k, e * P, e * P + P), whalf(wlo, u, k, e * P, e * P + P),
                                  fhi[:, k, c0:c1], flo[:, k, c0:c1], k == 0, k == KD - 1)
                    labels = [name + (e,)] + ([("used", u.wn)] if e == 3 else [])
                    ins.then_inc(*did("tensor", *labels))

            def turn_features(name, src, nt, ready):
                per = 4 // nt
                for j in range(KD // per):
                    o = job(name, j)
                    if j == 0:
                        for r in ready:
                            pe.wait_ge(*after(*r))
                    for q in range(per):
                        for t in range(nt):
                            k = j * per + q
                            c = (q * nt + t) * P
                            ins = nc.tensor.transpose(o[:, c:c + P], src(t)[:, k * P:k * P + P], ident[:, :])
                    ins.then_inc(*did("tensor", (name, j)))

            def mod(l, j):
                u = UNIT[("mod", l, j)]
                o = job("mod", l, j)
                if l == 0 and j == 0:
                    pe.wait_ge(*after("cond"))
                for i in range(2):
                    c = u.c0 + i
                    wait_raw(pe, c)
                    for k in range(4):
                        ins = mm(o[0:2, :], cond[:, i * 4 + k, :], raw[:, c % RAW_SLOTS, k * NW:k * NW + NW],
                                 start=i + k == 0, stop=i == 1 and k == 3)
                    ins.then_inc(*counts.used(c, *([("mod", l, j)] if i else [])))

            def mod_columns(l, r):
                n = 32 * (r + 1)
                o = job("modT", l, r)
                pe.wait_ge(loads[f"modc{l}{r}"], 32)
                nc.tensor.transpose(o[:, 0:n], modc[0:n, :], ident[0:n, 0:n]).then_inc(*did("tensor", ("modT", l, r)))

            def gate_rows(l):
                o = job("grow", l)
                pe.wait_ge(*after("gcol", l))
                nc.tensor.transpose(o[0:32, 0:P], gcol[:, :, :, :].rearrange("p a b c -> p (a b c)"),
                                    ident[:, :]).then_inc(*did("tensor", ("grow", l)))

            def mods_before(name):
                for m in MODS.get(name, []):
                    mod(*m)

            def scores(it):
                kind, l, h, t = it
                parts, _, _ = item_info(it)
                if kind == "first":
                    po, tq = (h % 2) * DH, h // 2
                    n = parts[0][1]
                    o = job("s", it, 0)
                    o2 = job("s", it, 1) if t else None
                    if h == 0 and t == 0:
                        for g in range(NG):
                            for e in range(4):
                                pe.wait_ge(*after("k1", l, g, e))
                                pe.wait_ge(*after("q1", l, g, e))
                    for g in range(NG):
                        dst = o[:, g * n:(g + 1) * n] if not t or g < 2 else o2[:, 0:n]
                        ins = mm(dst, qT1[po:po + DH, g * 4 + tq, t * P:t * P + P], kT1[po:po + DH, g * 4 + tq, 0:n],
                                 start=True, stop=True)
                else:
                    part = {"A": 0, "B": 1, "C": 0, "D": 1}[kind]
                    if h == 0 and t == 0:
                        for tt in range(4):
                            pe.wait_ge(*after("kT", l, part, tt))
                        for tt in range(4 if l == 0 else 2):
                            pe.wait_ge(*after("qT", l, part, tt))
                    k0, k1 = (0, 512) if t < XT else (256, 512)
                    for j, n in parts:
                        head = 2 * h + j if kind == "B" else h
                        po, tq = (head % 2) * DH, head // 2
                        tk = tq if kind in "BD" else h // 4
                        o = job("s", it, j)
                        ins = mm(o[:, 0:n], QT[l][po:po + DH, tq, t * P:t * P + P], KT[l][po:po + DH, tk, k0:k1],
                                 start=True, stop=True)
                ins.then_inc(*did("tensor", ("s", it)))

            def turns(i, it):
                _, kt, _ = item_info(it)
                e = e1 if it[0] == "first" else EE[it[1]]
                pe.wait_ge(*after("probs", it))
                for b in range(0, kt, 4):
                    o = job("t", it, b)
                    for j in range(b, min(kt, b + 4)):
                        ins = nc.tensor.transpose(o[:, (j - b) * P:(j - b + 1) * P], e[:, i % 3, j * P:j * P + P], ident[:, :])
                    ins.then_inc(*did("tensor", ("t", it, b)))

            def values(i, it):
                kind, l, h, t = it
                _, kt, dv = item_info(it)
                p = p1 if kind == "first" else PP[l]
                o = job("o", it)
                if h == 0 and t == 0:
                    for tt in range(2 if kind == "first" else 4):
                        for g in range(NG if kind == "first" else 1):
                            pe.wait_ge(*(after("v1", l, g, tt) if kind == "first"
                                         else after("vv", l, {"A": 0, "B": 1, "C": 0, "D": 1}[kind], tt)))
                for b in range(0, kt, 4):
                    pe.wait_ge(*after("pT", it, b))
                for j in range(kt):
                    g, tt = key_tile(it, j)
                    if kind == "first":
                        v = v1[:, tt, g, h * DH:(h + 1) * DH]
                    elif kind in "AC":
                        v = VV[l][:, tt, (h // 4) * DH:(h // 4 + 1) * DH]
                    else:
                        v = VV[l][:, tt, h * dv:(h + 1) * dv]
                    ins = mm(o[:, 0:dv], p[:, i % 2, j * P:j * P + P], v, start=j == 0, stop=j == kt - 1)
                ins.then_inc(*did("tensor", ("o", it)))

            def attend(items, mods):
                for i in range(len(items) + 3):
                    if i < len(items):
                        scores(items[i])
                    for m in mods_at(i, items, mods):
                        mod(*m)
                    if 0 <= i - 2 < len(items):
                        turns(i - 2, items[i - 2])
                    if 0 <= i - 3 < len(items):
                        values(i - 3, items[i - 3])

            pe.wait_ge(loads["x"], 16)
            pe.wait_ge(loads["ident"], 16)
            turn_features("fx", lambda t: hx[:, t, :], 2, [])
            for g in range(4):
                by_feature(UNIT[("gate", g)], ("gate", g), 0, S, feat=None if g else ("fx", 2))

            def pool(g):
                if g == 0:
                    pe.wait_ge(loads["pool"], 16)
                for t in range(XT):
                    pe.wait_ge(*after("utok", g, t))
                for c in range(0, 4, 2):
                    o = job("pooled", g, c)
                    for q in range(2):
                        cc = slice((c + q) * P, (c + q + 1) * P)
                        r = o[:, q * S:(q + 1) * S]
                        mm(r[:, 0:144], utok[:, 0, cc], poolT[:, g, 0:144], start=q == 0, stop=False, skip_group_check=True)
                        ins = mm(r[:, 128:256], utok[:, 1, cc], poolT[:, g, 144:272], start=False, stop=True,
                                 skip_group_check=True)
                    ins.then_inc(*did("tensor", ("pooled", g, c)))

            def group(g):
                u = UNIT[("grp", g)]
                wait_weights(u)
                for c in range(0, 4, 2):
                    pe.wait_ge(*after("pooled split", g, c))
                for e in range(4):
                    o = job("mixed", g, e)
                    for k in range(4):
                        ins = mm3(o[:, 0:S], whalf(whi, u, k, e * P, e * P + P), whalf(wlo, u, k, e * P, e * P + P),
                                  phi[:, k, :], plo[:, k, :], k == 0, k == 3)
                    labels = [("mixed", g, e)] + ([("used", u.wn)] if e == 3 else [])
                    ins.then_inc(*did("tensor", *labels))

            for g in range(4):
                by_token(UNIT[("u", g)], ("u", g), range(XT))
                if g:
                    pool(g - 1) if g == 1 else None
                    group(g - 1)
                    pool(g)
            group(3)

            for n in range(2):
                outs = []
                for kh in range(2):
                    u = UNIT[("outa", n, kh)]
                    wait_weights(u)
                    for t in range(XT):
                        if kh == 0:
                            outs.append(job("outa", n, t))
                        for k in range(KD):
                            kk = kh * KD + k
                            if n == 0 and t == 0:
                                pe.wait_ge(*after("y", kk))
                            ins = mm3(outs[t], yhi[:, kk, t * P:t * P + P], ylo[:, kk, t * P:t * P + P],
                                      whalf(whi, u, k, 0, NW), whalf(wlo, u, k, 0, NW), kk == 0, kk == 15)
                        labels = ([("outa", n, t)] if kh else []) + ([("used", u.wn)] if t == 1 else [])
                        if labels:
                            ins.then_inc(*did("tensor", *labels))
            mods_before(("k", 0, 0))
            turn_features("f1", lambda t: hx[:, t, :], 2, [("ln", 0, 0), ("ln", 0, 1)])
            for hf in range(2):
                for g in range(NG):
                    by_feature(UNIT[("k", hf, g)], ("k", hf, g), 0, S, feat=("f1", 2) if hf == g == 0 else None)
                for g in range(NG):
                    by_feature(UNIT[("q", hf, g)], ("q", hf, g), 0, S)
                for g in range(NG):
                    by_token(UNIT[("v", hf, g)], ("v", hf, g), range(XT))
                by_token(UNIT[("gb", hf)], ("gb", hf), range(XT))
                attend(items_first(hf), mods_first(hf))
            turn_features("fo1", lambda t: gb[:, t, :], 2, [("gated", items_first(1)[-1])])
            for n in range(2):
                by_token(UNIT[("outb", n)], ("outb", n), range(XT), feat=None if n else ("fo1", 2))

            for l in range(2):
                nt = 4 if l == 0 else 2
                mod_columns(l, 0)
                mods_before(("q2", l, 0))
                turn_features(("n1", l), lambda t: mix[:, t, :], 4, [("xn", l, 0, t) for t in range(4)])
                if l == 0:
                    mod_columns(0, 1)

                def turn_heads(what, part, tiles, ntile):
                    for t in tiles:
                        r = STAGE[(what, l, part, t)]
                        o = job(what + "turn", l, part, t)
                        pe.wait_ge(*after("staged", what, l, part, t))
                        off = 256 if what == "k" and part == 0 else 0
                        for j in range(ntile):
                            ins = nc.tensor.transpose(o[:, j * P:(j + 1) * P], EE[l][:, r, off + j * P:off + j * P + P], ident[:, :])
                        ins.then_inc(*did("tensor", (what + "turn", l, part, t)))

                for part in range(2):
                    if l == 1 and part == 1:
                        by_feature(UNIT[("q2", l, 1)], ("q2", l, 1), 0, S)
                        by_feature(UNIT[("k2", l, 1)], ("k2", l, 1), 0, 512)
                    else:
                        by_token(UNIT[("q2", l, part)], ("q2", l, part), range(nt), feat=None if part else (("n1", l), 4))
                        by_token(UNIT[("k2", l, part)], ("k2", l, part), range(4), width=256 if part == 0 else NW)
                        turn_heads("q", part, range(nt), 4)
                        turn_heads("k", part, range(4), 2 if part == 0 else 4)
                        if l == 0 and part == 0:
                            gate_rows(0)
                    if part == 1:
                        by_token(UNIT[("v2", l, 1)], ("v2", l, 1), range(4))
                    if l == 1 and part == 1:
                        gate_rows(1)
                    attend(items_second(l, part), mods_second(l, part))
                    if l == 1 and part == 0:
                        mod_columns(1, 1)
                turn_features(("fo", l), lambda t: mix[:, t, :], nt, [("mixed out", l, t) for t in range(nt)])
                for n in range(2):
                    by_token(UNIT[("out2", l, n)], ("out2", l, n), range(nt), feat=None if n else (("fo", l), nt))
                mods_before(("in", l, 0))
                turn_features(("n2", l), lambda t: mix[:, t, :], nt, [("xn", l, 1, t) for t in range(nt)])
                if l == 1:
                    held = {}
                    for t in range(XT):
                        for n in range(2):
                            held[t, n] = job("acc", t, n)
                    state["banks"] = [b for b in range(8) if b not in [counts.banks[("acc", t, n)] for t in range(2) for n in range(2)]]
                for j in range(9):
                    if j < 8:
                        by_feature(UNIT[("in", l, j)], ("in", l, j), 0, nt * P, feat=None if j else (("n2", l), nt))
                    if j:
                        u = UNIT[("out", l, j - 1)]
                        wait_weights(u)
                        for e in range(4):
                            pe.wait_ge(*after("hidden", l, j - 1, e))
                        b = (j - 1) % 2
                        for n in range(2):
                            w = (u.w0 + n) % SPLIT_SLOTS
                            for t in range(nt):
                                o = held[t, n] if l else job("acc", j - 1, t, n)
                                for k in range(4):
                                    first, stop = (k == 0, k == 3) if l == 0 else (j == 1 and k == 0, j == 8 and k == 3)
                                    ins = mm3(o, hhi[:, b, k, t * P:t * P + P], hlo[:, b, k, t * P:t * P + P],
                                              whi[:, w, k * NW:(k + 1) * NW], wlo[:, w, k * NW:(k + 1) * NW], first, stop)
                                labels = [("used", u.wn)] if n == 1 and t == nt - 1 else []
                                if l == 0:
                                    labels.append(("acc", j - 1, t, n))
                                elif j == 8:
                                    labels.append(("acc", t, n))
                                if labels:
                                    ins.then_inc(*did("tensor", *labels))

        def split_hi(act, upto, state):
            while state[0] < len(SPLIT) and SPLIT[state[0]][1].wn <= upto:
                w = state[0]
                c, _ = SPLIT[w]
                wait_raw(act, c)
                if w >= SPLIT_SLOTS:
                    act.wait_ge(*after("used", SPLIT[w - SPLIT_SLOTS][1].wn))
                nc.scalar.activation(whi[:, w % SPLIT_SLOTS, :], raw[:, c % RAW_SLOTS, :], ACT.Copy).then_inc(
                    *did("scalar", ("hi", w)))
                state[0] += 1

        def split_lo(eng, ops, upto, state, mine):
            while state[0] < len(SPLIT) and SPLIT[state[0]][1].wn <= upto:
                w = state[0]
                c, _ = SPLIT[w]
                if w % 2 == mine:
                    eng.wait_ge(*after("hi", w))
                    ops.tensor_tensor(wlo[:, w % SPLIT_SLOTS, :], raw[:, c % RAW_SLOTS, :],
                                      whi[:, w % SPLIT_SLOTS, :].bitcast(F32), ALU.subtract).then_inc(
                        *counts.used(c, ("lo", w)))
                state[0] += 1

        def ftmp(l, which, j):
            if l < 0:
                return e1[:, j % 2, 0:512]
            return EE[l][:, j % 2, 0:512] if which == 0 else htmp[:, j % 2, :]

        TILES = {0: (2, 3, 0, 1), 1: (0, 1, 2, 3)}

        @block.scalar
        def _(act):
            copy = nc.scalar.activation
            st = [0]
            act.dma_start(cond[:, :, :], T["cond"]).then_inc(loads["cond"], 16)
            act.dma_start(poolT[:, :, :], T["t_pool"].rearrange("p (g t) -> p g t", g=4)).then_inc(loads["pool"], 16)
            act.dma_start(scol[:, :], T["scale_cols"]).then_inc(loads["scol"], 16)
            act.dma_start(modb[:, :, :], T["b_mod_cols"]).then_inc(loads["modb"], 16)
            act.dma_start(normc[:, :, :, :], T["norm_cols"]).then_inc(loads["normc"], 16)
            act.dma_start(lncol[:, :, :], T["ln_cols"]).then_inc(loads["lncol"], 16)

            def split_to(name, ahead=1):
                split_hi(act, UNIT[name].wn + ahead, st)

            def src(*label):
                return ps[:, counts.bank(*label), :]

            def split_features(name, nt, tmp=None):
                per = 4 // nt
                for j in range(KD // per):
                    dst = fhi[:, j * per:(j + 1) * per, 0:nt * P]
                    if tmp is None:
                        act.wait_ge(*after(name, j))
                        got = src(name, j)
                    else:
                        act.wait_ge(*after("modulated", name, j))
                        got = ftmp(*tmp, j)
                    copy(dst, got.rearrange("p (a b) -> p a b", a=per), ACT.Copy).then_inc(
                        *did("scalar", ("fhi", name, j)))

            def save_mod(l, j):
                act.wait_ge(*after("read", "mod", l, j))
                act.dma_start(modd[l, :, j * NW:(j + 1) * NW], modrow[:, :]).then_inc(loads["modsave"], 16)

            act.wait_ge(loads["cond"], 16)
            copy(cond[:, :, :], cond[:, :, :], ACT.Silu).then_inc(*did("scalar", ("cond",)))
            split_features("fx", 2)
            split_hi(act, 1, st)
            for g in range(4):
                split_to(("gate", g))
                for e in range(4):
                    act.wait_ge(*after("gate", g, e))
                    copy(sgate[:, g * 4 + e, :], src("gate", g, e)[:, 0:S], ACT.Silu).then_inc(
                        *did("scalar", ("sgate", g * 4 + e), ("read", "gate", g, e)))

            def u_copy(g):
                split_to(("u", g))
                for t in range(XT):
                    act.wait_ge(*after("u", g, t))
                    if g:
                        act.wait_ge(*after("pooled", g - 1, 2))
                    copy(utok[:, t, :], src("u", g, t), ACT.Copy).then_inc(
                        *did("scalar", ("utok", g, t), ("read", "u", g, t)))

            def pooled_hi(g):
                for c in range(0, 4, 2):
                    act.wait_ge(*after("pooled", g, c))
                    copy(phi[:, c:c + 2, :], src("pooled", g, c).rearrange("p (a b) -> p a b", a=2), ACT.Copy).then_inc(
                        *did("scalar", ("phi", g, c)))

            def y_hi(g):
                for e in range(4):
                    act.wait_ge(*after("ymul", g * 4 + e))
                    copy(yhi[:, g * 4 + e, :], sgate[:, g * 4 + e, :], ACT.Copy).then_inc(
                        *did("scalar", ("yhi", g * 4 + e)))

            for g in range(4):
                u_copy(g)
                if g == 1:
                    pooled_hi(0)
                if g:
                    split_to(("grp", g - 1))
                    y_hi(g - 1)
                    pooled_hi(g)
            split_to(("grp", 3))
            y_hi(3)
            act.wait_ge(*after("y", 15))
            act.wait_ge(*after("mixed", 3, 3))
            for r, name in enumerate(("ln_g", "ln_b")):
                act.dma_start(lnrow[:, r, :], rows_to_all(T[name], 0, D)).then_inc(loads["lna"], 16)
            act.dma_start(dist[:, :, :], T["t_dist"].rearrange("p (g t) -> p g t", g=NG)).then_inc(loads["dist"], 16)
            for n in range(2):
                for kh in range(2):
                    split_to(("outa", n, kh))

            def root(out_, in_, n, e, *label):
                copy(out_, in_, ACT.Sqrt, scale=1.0 / n, bias=eps[:, e:e + 1]).then_inc(*did("scalar", label))

            for t in range(XT):
                act.wait_ge(*after("var", 0, t))
                root(rstd[:, t:t + 1], mv[:, t, 1:2], 1, 1, "root", "ln", 0, t)
            for m in MODS[("k", 0, 0)]:
                save_mod(*m)
            split_features("f1", 2, (-1, 0))

            def exps(i, it):
                kind, l, h, t = it
                parts, kt, _ = item_info(it)
                e = e1 if kind == "first" else EE[l]
                act.wait_ge(*after("max", it))
                if kind in "AB":
                    if i >= 3:
                        act.wait_ge(*after("t", items[i - 3], 0))
                    for j, n in parts:
                        labels = [("read", "s", it, j)]
                        if j == len(parts) - 1:
                            labels.append(("exp", it))
                            if kind == "A":
                                labels.append(("probs", it))
                        copy(e[:, i % 3, j * 512:j * 512 + n], src("s", it, j)[:, 0:n], ACT.Exp,
                             bias=nmax[:, i % 4, j:j + 1], accum_out=rsum[:, i % 4, j:j + 1]).then_inc(*did("scalar", *labels))
                    return
                n = kt * P
                if kind == "C":
                    copy(esink[:, i % 4:i % 4 + 1], sinkr[:, h:h + 1], ACT.Exp, bias=nmax[:, i % 4, 0:1]).then_inc(
                        *did("scalar", ("esink", it)))
                copy(e[:, i % 3, 0:n], e[:, i % 3, 0:n], ACT.Exp, bias=nmax[:, i % 4, 0:1],
                     accum_out=rsum[:, i % 4, 0:1]).then_inc(*did("scalar", ("exp", it), ("probs", it)))

            def prob_copy(i, it):
                _, kt, _ = item_info(it)
                p = p1 if it[0] == "first" else PP[it[1]]
                for b in range(0, kt, 4):
                    n = min(kt - b, 4) * P
                    act.wait_ge(*after("t", it, b))
                    if i >= 2:
                        act.wait_ge(*after("o", items[i - 2]))
                    copy(p[:, i % 2, b * P:b * P + n], src("t", it, b)[:, 0:n], ACT.Copy).then_inc(
                        *did("scalar", ("pT", it, b), ("read", "t", it, b)))

            def attend(items, mods):
                for i in range(len(items) + 3):
                    if i < len(items):
                        exps(i, items[i])
                    for m in mods_at(i, items, mods):
                        save_mod(*m)
                    if 0 <= i - 2 < len(items):
                        prob_copy(i - 2, items[i - 2])

            def load_mods(l, r):
                act.wait_ge(loads["modsave"], 16 * (12 * l + (12 if r else 4)))
                if l or r:
                    act.wait_ge(*after("modT", *((l, 0) if r else (l - 1, 1))))
                n = 16 * (r + 1)
                for vec in range(2):
                    rows = modd[l, vec, (4 * NW if r else 0):(12 if r else 4) * NW].rearrange("(r p) -> r p", p=P)
                    act.dma_start(modc[vec * n:(vec + 1) * n, :], rows).then_inc(loads[f"modc{l}{r}"], 16)

            def save_gates(l):
                act.wait_ge(*after("growc", l))
                act.dma_start(gated[l].rearrange("v (r p) -> (v r) p", p=P), grow[:, :]).then_inc(loads["gsave"], 16)

            def load_gates(l, which):
                act.wait_ge(loads["gsave"], 16 * (l + 1))
                for v in range(2 - l):
                    act.dma_start(gates[:, v, :], rows_to_all(gated, (l * 4 + which * 2 + v) * D, D)).then_inc(
                        loads[f"g{l}{which}"], 16)

            for hf in range(2):
                for g in range(NG):
                    split_to(("k", hf, g))
                    for e in range(4):
                        act.wait_ge(*after("k", hf, g, e))
                        copy(kT1[:, g * 4 + e, :], src("k", hf, g, e)[:, 0:S], ACT.Copy).then_inc(
                            *did("scalar", ("k1", hf, g, e), ("read", "k", hf, g, e)))
                for g in range(NG):
                    split_to(("q", hf, g))
                    for e in range(4):
                        act.wait_ge(*after("q", hf, g, e))
                        copy(qT1[:, g * 4 + e, :], src("q", hf, g, e)[:, 0:S], ACT.Copy, scale=QSCALE).then_inc(
                            *did("scalar", ("q1", hf, g, e), ("read", "q", hf, g, e)))
                for g in range(NG):
                    split_to(("v", hf, g))
                    for t in range(XT):
                        act.wait_ge(*after("v", hf, g, t))
                        copy(v1[:, t, g, :], src("v", hf, g, t), ACT.Copy).then_inc(
                            *did("scalar", ("v1", hf, g, t), ("read", "v", hf, g, t)))
                split_to(("gb", hf))
                for t in range(XT):
                    act.wait_ge(*after("gb", hf, t))
                    copy(gb[:, t, hf * NW:(hf + 1) * NW], src("gb", hf, t), ACT.Silu).then_inc(
                        *did("scalar", ("gbs", hf, t), ("read", "gb", hf, t)))
                if hf == 0:
                    act.wait_ge(*after("h1", 1))
                    for r, name in enumerate(("ln_g", "ln_b")):
                        act.dma_start(lnrow[:, r, :], rows_to_all(T[name], D, D)).then_inc(loads["lnb"], 16)
                items = items_first(hf)
                attend(items, mods_first(hf))
            load_mods(0, 0)
            act.dma_start(hc[:, :, :], T["ctx_2"].rearrange("a (t p) d -> p (a t) d", p=P)).then_inc(loads["ctx"], 16)
            split_features("fo1", 2)
            for n in range(2):
                split_to(("outb", n))

            def squares(label, t):
                copy(mix[:, t, :], H(t), ACT.Square, accum_out=sumsq[:, t:t + 1]).then_inc(*did("scalar", label))

            def half_square(l, which, t, n):
                if (t, n) != (0, 0):
                    act.wait_ge(counts.sems["scalar"], counts.now["scalar"])
                if which == 0:
                    act.wait_ge(*after("out2", l, n, t))
                    got = src("out2", l, n, t)
                elif l == 0:
                    act.wait_ge(*after("summed", t, n))
                    got = mix[:, t, n * NW:(n + 1) * NW]
                else:
                    act.wait_ge(*after("acc", t, n))
                    got = src("acc", t, n)
                copy(htmp[:, n, :], got, ACT.Square, accum_out=sumh[:, t, n:n + 1]).then_inc(
                    *did("scalar", ("sqh", l, which, t, n)))

            def mixer_root(l, which, t):
                act.wait_ge(*after("sumh", l, which, t))
                root(rstd[:, 4 + t:5 + t], sumh[:, t, 0:1], D, 0, "mixer root", l, which, t)

            def stream_root(l, which, t):
                if which or l:
                    act.wait_ge(*after("resid", *((l, 0) if which else (0, 1)), t))
                squares(("sq", l, which, t), t)
                act.wait_ge(counts.sems["scalar"], counts.now["scalar"])
                root(rstd[:, t:t + 1], sumsq[:, t:t + 1], D, 0, "stream root", l, which, t)

            for t in range(XT):
                act.wait_ge(*after("var", 1, t))
                root(rstd[:, t:t + 1], mv[:, t, 1:2], 1, 1, "root", "ln", 1, t)

            for l in range(2):
                nt = 4 if l == 0 else 2
                if l == 0:
                    for t in TILES[0]:
                        if t == 2:
                            act.wait_ge(loads["ctx"], 16)
                        if t < XT:
                            act.wait_ge(*after("ln", 1, t))
                        stream_root(0, 0, t)
                    act.wait_ge(*after("ln", 1, 1))
                    act.dma_start(rope[:, :, :, :], T["t_rope"].rearrange("p (a t d) -> p a t d", a=2, t=2)).then_inc(
                        loads["ropes"], 16)
                    act.dma_start(qkg[:, :, :], rows_to_all(T["qk_norm_a_2"], 0, 2 * DH)).then_inc(loads["ropes"], 16)
                    act.dma_start(sublng[:, :], rows_to_all(T["diff_subln_2"], 0, P)).then_inc(loads["ropes"], 16)
                    act.dma_start(lamrow[:, :, :], rows_to_all(T["diff_lambda_2"], 0, 4 * DH)).then_inc(loads["ropes"], 16)
                for m in MODS[("q2", l, 0)]:
                    save_mod(*m)
                if l == 0:
                    load_mods(0, 1)
                split_features(("n1", l), 4, (l, 0))
                if l == 0:
                    act.wait_ge(*after("lam sums"))
                    copy(lam[:, 0:2], lam[:, 0:2], ACT.Exp).then_inc(*did("scalar", ("lam exp",)))
                else:
                    act.wait_ge(*after(("n1", 1), 7))
                    for h in range(8):
                        for r in range(4):
                            rows = bass.AP(tensor=T["rpb_rows"].tensor,
                                           offset=T["rpb_rows"].offset + (h * 7 + 3 - r) * GRID * P + GRID - 1,
                                           ap=[[P - 1, GRID], [GRID * P, 4], [1, GRID]])
                            b = bias_d(h, r // 2)[r % 2 * GRID:(r % 2 + 1) * GRID, :]
                            act.dma_start(b.rearrange("p (a b) -> p a b", a=4), rows).then_inc(loads["bias"], 16)
                for part in range(2):
                    if l == 1 and part == 1:
                        split_to(("q2", l, 1))
                        for e in range(4):
                            act.wait_ge(*after("q2", l, 1, e))
                            copy(QT[l][:, e, 0:S], src("q2", l, 1, e)[:, 0:S], ACT.Copy, scale=QSCALE).then_inc(
                                *did("scalar", *([("qT", l, 1, t) for t in range(2)] if e == 3 else []), ("read", "q2", l, 1, e)))
                        split_to(("k2", l, 1))
                        for e in range(4):
                            act.wait_ge(*after("k2", l, 1, e))
                            copy(KT[l][:, e, :], src("k2", l, 1, e), ACT.Copy).then_inc(
                                *did("scalar", *([("kT", l, 1, t) for t in range(4)] if e == 3 else []), ("read", "k2", l, 1, e)))
                    else:
                        sets = (("q", range(nt)), ("k", range(4)))
                        for what, tiles in sets:
                            small = what == "k" and part == 0
                            split_to((what + "2", l, part))
                            w = P if small else NW
                            for t in tiles:
                                key = (what, l, part, t)
                                a = src(what + "2", l, part, t)
                                act.wait_ge(*after(what + "2", l, part, t))
                                if small:
                                    copy(VV[l][:, t, 0:P], a[:, P:2 * P], ACT.Copy).then_inc(*did("scalar", ("vv", l, part, t)))
                                normed = l == 0 and part == 0
                                if (normed or (t >= XT and not small)) and STAGE_BEFORE[key]:
                                    act.wait_ge(*after(*STAGE_BEFORE[key]))
                                if normed:
                                    copy(EE[l][:, STAGE[key], 512:512 + w], a[:, 0:w], ACT.Square).then_inc(
                                        *did("scalar", ("squared",) + key))
                                elif t >= XT and not small:
                                    copy(EE[l][:, STAGE[key], 0:w], a[:, 0:w], ACT.Copy).then_inc(
                                        *did("scalar", ("staged",) + key, ("read", what + "2", l, part, t)))
                        for what, tiles in sets:
                            n = 2 if what == "k" and part == 0 else 4
                            dst = (QT if what == "q" else KT)[l]
                            for t in tiles:
                                act.wait_ge(*after(what + "turn", l, part, t))
                                copy(dst[:, 0:n, t * P:t * P + P],
                                     src(what + "turn", l, part, t)[:, 0:n * P].rearrange("p (a b) -> p a b", a=n),
                                     ACT.Copy, scale=QSCALE if what == "q" else 1.0).then_inc(
                                    *did("scalar", (what + "T", l, part, t), ("read", what + "turn", l, part, t)))
                        if l == 0 and part == 0:
                            save_gates(0)
                    if part == 1:
                        split_to(("v2", l, 1))
                        for t in range(4):
                            act.wait_ge(*after("v2", l, 1, t))
                            copy(VV[l][:, t, :], src("v2", l, 1, t), ACT.Copy).then_inc(
                                *did("scalar", ("vv", l, 1, t), ("read", "v2", l, 1, t)))
                    items = items_second(l, part)
                    if l == 1 and part == 0:
                        act.wait_ge(loads["odd"], 64)
                    if l == 1 and part == 1:
                        save_gates(1)
                    attend(items, mods_second(l, part))
                    if l == 1 and part == 0:
                        load_mods(1, 1)
                for t in range(nt):
                    act.wait_ge(*after("mixed out", l, t))
                load_gates(l, 0)
                split_features(("fo", l), nt)
                for n in range(2):
                    split_to(("out2", l, n))
                    if n == 0:
                        for t in range(nt):
                            half_square(l, 0, t, 0)
                for i in range(nt + 2):
                    if i < nt:
                        half_square(l, 0, i, 1)
                    if 0 <= i - 1 < nt:
                        mixer_root(l, 0, i - 1)
                    if 0 <= i - 2 < nt:
                        stream_root(l, 1, i - 2)
                for m in MODS.get(("in", l, 0), []):
                    save_mod(*m)
                load_gates(l, 1)
                if l == 0:
                    load_mods(1, 0)
                split_features(("n2", l), nt, (l, 1))
                for j in range(9):
                    if j < 8:
                        split_to(("in", l, j))
                        for e in range(4):
                            act.wait_ge(*after("in", l, j, e))
                            n = j * 4 + e
                            if n >= 2:
                                act.wait_ge(*after("hidden", l, (n - 2) // 4, (n - 2) % 4))
                            copy(htmp[:, e % 2, 0:nt * P], src("in", l, j, e)[:, 0:nt * P], ACT.Relu).then_inc(
                                *did("scalar", ("relu", l, j, e), ("read", "in", l, j, e)))
                            act.wait_ge(*after("squared", l, j, e))
                            if j >= 2:
                                act.wait_ge(*after("used", UNIT[("out", l, j - 2)].wn))
                            copy(hhi[:, j % 2, e, 0:nt * P], htmp[:, e % 2, 0:nt * P], ACT.Copy).then_inc(
                                *did("scalar", ("hhi", l, j, e)))
                    if j:
                        split_to(("out", l, j - 1))
                for t in range(nt):
                    half_square(l, 1, t, 0)
                for i in range(nt + 2):
                    if i < nt:
                        half_square(l, 1, i, 1)
                    if 0 <= i - 1 < nt:
                        mixer_root(l, 1, i - 1)
                    if l == 0 and 0 <= i - 2 < nt:
                        stream_root(1, 0, i - 2)
                if l == 0:
                    act.wait_ge(*after("resid", 0, 1, 3))
                    act.dma_start(rope_b[:, :, :, :], T["t_rope"].rearrange("p (a t d) -> p a t d", a=2, t=2)).then_inc(
                        loads["odd"], 16)
                    act.dma_start(sinkr[:, :], rows_to_all(T["sink_c_2"], 0, 8)).then_inc(loads["odd"], 16)
                    act.dma_start(band[:, :, :], T["t_band"].rearrange("p (a b) -> p a b", a=2)).then_inc(loads["odd"], 16)
                    act.dma_start(colmask[:, :], T["t_cols"]).then_inc(loads["odd"], 16)

        @block.vector
        def _(dve):
            v = nc.vector
            st = [0]

            def split_to(name, ahead=1):
                split_lo(dve, v, UNIT[name].wn + ahead, st, 1)

            def link(ins, *labels):
                ins.then_inc(*did("vector", *labels))
                dve.wait_ge(counts.sems["vector"], counts.now["vector"])

            def src(*label):
                return ps[:, counts.bank(*label), :]

            def low_features(name, nt):
                per = 4 // nt
                for j in range(KD // per):
                    dve.wait_ge(*after("fhi", name, j))
                    dst = flo[:, j * per:(j + 1) * per, 0:nt * P]
                    hi = fhi[:, j * per:(j + 1) * per, 0:nt * P].bitcast(F32)
                    v.tensor_tensor(dst, src(name, j).rearrange("p (a b) -> p a b", a=per), hi, ALU.subtract).then_inc(
                        *did("vector", ("split", name, j), ("read", name, j)))

            def modulate(name, nt, l, which, A=None, B=None):
                per = 4 // nt
                for j in range(KD // per):
                    dve.wait_ge(*after(name, j))
                    if j >= 2:
                        dve.wait_ge(*after("split", name, j - 2))
                    for q in range(2):
                        k, vec = (j, q) if nt == 4 else (2 * j + q, 0)
                        factor = A[:, k:k + 1] if A is not None else modA[:, l, which, vec, k:k + 1]
                        shift = B[:, k:k + 1] if B is not None else modB[:, l, which, vec, k:k + 1]
                        ins = v.tensor_scalar(ftmp(l, which, j)[:, q * S:(q + 1) * S], src(name, j)[:, q * S:(q + 1) * S],
                                              factor, shift, ALU.mult, ALU.add)
                    ins.then_inc(*did("vector", ("modulated", name, j), ("read", name, j)))

            def rsqrt(out_, in_, n, e):
                w = out_.shape[-1]
                x, t = newton[:, 0, 0:w], newton[:, 1, 0:w]
                link(v.tensor_scalar(x, in_, 1.0 / n, e, ALU.mult, ALU.add))
                link(v.tensor_scalar(out_.bitcast(I32), x.bitcast(I32), -0.5, RSQRT_START, ALU.mult, ALU.add))
                for _ in range(NEWTON_STEPS):
                    link(v.tensor_tensor(t, out_, out_, ALU.mult))
                    link(v.scalar_tensor_tensor(out=t, in0=t, scalar=-0.5, in1=x, op0=ALU.mult, op1=ALU.mult))
                    link(v.scalar_tensor_tensor(out=out_, in0=t, scalar=1.5, in1=out_, op0=ALU.add, op1=ALU.mult))

            def deviation(col, in_, n, e):
                link(v.tensor_scalar(dev[:, col:col + 1], in_, 1.0 / n, e, ALU.mult, ALU.add))

            def refined(col, fold=False):
                y, x, t = rstd[:, col:col + 1], dev[:, col:col + 1], newton[:, 0, col:col + 1]
                link(v.reciprocal(y, y))
                link(v.scalar_tensor_tensor(out=t, in0=y, scalar=y, in1=x, op0=ALU.mult, op1=ALU.mult))
                link(v.tensor_scalar(t, t, -0.5, 1.5, ALU.mult, ALU.add))
                if not fold:
                    link(v.tensor_tensor(y, y, t, ALU.mult))
                return y, t

            v.memset(eps[:, 0:1], EPS).then_inc(*did("vector"))
            v.memset(eps[:, 1:2], LN_EPS).then_inc(*did("vector"))

            low_features("fx", 2)
            split_lo(dve, v, 1, st, 1)
            for g in range(4):
                split_to(("gate", g))

            def pooled_lo(g):
                for c in range(0, 4, 2):
                    dve.wait_ge(*after("phi", g, c))
                    v.tensor_tensor(plo[:, c:c + 2, :], src("pooled", g, c).rearrange("p (a b) -> p a b", a=2),
                                    phi[:, c:c + 2, :].bitcast(F32), ALU.subtract).then_inc(
                        *did("vector", ("pooled split", g, c), ("read", "pooled", g, c)))

            def gate_mixed(g):
                for e in range(4):
                    i = g * 4 + e
                    dve.wait_ge(*after("mixed", g, e))
                    dve.wait_ge(*after("sgate", i))
                    v.scalar_tensor_tensor(out=sgate[:, i, :], in0=src("mixed", g, e)[:, 0:S], scalar=scol[:, i:i + 1],
                                           in1=sgate[:, i, :], op0=ALU.mult, op1=ALU.mult).then_inc(
                        *did("vector", ("ymul", i), ("read", "mixed", g, e)))
                for e in range(4):
                    i = g * 4 + e
                    dve.wait_ge(*after("yhi", i))
                    v.tensor_tensor(ylo[:, i, :], sgate[:, i, :], yhi[:, i, :].bitcast(F32), ALU.subtract).then_inc(
                        *did("vector", ("y", i)))

            dve.wait_ge(loads["scol"], 16)
            for g in range(4):
                split_to(("u", g))
                if g == 1:
                    pooled_lo(0)
                if g:
                    split_to(("grp", g - 1))
                    gate_mixed(g - 1)
                    pooled_lo(g)
            split_to(("grp", 3))
            gate_mixed(3)

            def add_residual(name, n, t):
                dve.wait_ge(*after(name, n, t))
                hh = hx[:, t, n * NW:(n + 1) * NW]
                v.scalar_tensor_tensor(out=hh, in0=hh, scalar=ALPHA, in1=src(name, n, t), op0=ALU.mult, op1=ALU.add).then_inc(
                    *did("vector", ("read", name, n, t)))

            def layer_norm(i, name):
                for t in range(XT):
                    for n in range(2):
                        dve.wait_ge(*after("read", name, n, t))
                        link(v.bn_stats(stats[:, t, n, :], hx[:, t, n * NW:(n + 1) * NW]))
                    link(v.bn_aggr(mv[:, t, :], stats[:, t, :, :].rearrange("p a b -> p (a b)")), ("var", i, t))
                    deviation(t, mv[:, t, 1:2], 1, LN_EPS)
                for t in range(XT):
                    dve.wait_ge(*after("root", "ln", i, t))
                    refined(t)
                    h = hx[:, t, :]
                    labels = [("ln", i, t)] if i == 0 else [("centred", t)]
                    link(v.tensor_scalar(h, h, mv[:, t, 0:1], rstd[:, t:t + 1], ALU.subtract, ALU.mult), *labels)

            def mod_row(l, j):
                dve.wait_ge(*after("mod", l, j))
                if l or j:
                    dve.wait_ge(loads["modsave"], 16 * (12 * l + j))
                v.tensor_copy(modrow[:, :], src("mod", l, j)[0:2, :]).then_inc(*did("vector", ("read", "mod", l, j)))

            for n in range(2):
                for kh in range(2):
                    split_to(("outa", n, kh))
                for t in range(XT):
                    add_residual("outa", n, t)
            layer_norm(0, "outa")
            for m in MODS[("k", 0, 0)]:
                mod_row(*m)
            dve.wait_ge(loads["lncol"], 16)
            modulate("f1", 2, -1, 0, lncol[:, 0, :], lncol[:, 1, :])

            def maxima(i, it):
                kind, l, h, t = it
                parts, kt, _ = item_info(it)
                dve.wait_ge(*after("s", it))
                if kind in "AB":
                    for j, n in parts:
                        ins = v.reduce_max(nmax[:, i % 4, j:j + 1], src("s", it, j)[:, 0:n], AX_X, negate=True)
                    ins.then_inc(*did("vector", ("max", it)))
                    return
                if i >= 3:
                    _, kb, _ = item_info(items[i - 3])
                    dve.wait_ge(*after("t", items[i - 3], (kb - 1) // 4 * 4))
                e = (e1 if kind == "first" else EE[l])[:, i % 3, :]
                if kind == "first":
                    n = parts[0][1]
                    for g in range(NG):
                        bank = 0 if not t or g < 2 else 1
                        a = src("s", it, bank)[:, (0 if bank else g * n):(0 if bank else g * n) + n]
                        labels = []
                        if (t and g >= 1) or g == 2:
                            labels.append(("read", "s", it, bank))
                        ins = v.scalar_tensor_tensor(out=e[:, g * n:(g + 1) * n], in0=dist[:, g, 256 - n:256],
                                                     scalar=-SLOPES[g][l * 8 + h], in1=a, op0=ALU.mult, op1=ALU.add)
                        if labels and g < 2:
                            ins.then_inc(*did("vector", *labels))
                    link(ins, *labels)
                else:
                    a = src("s", it, 0)
                    v.tensor_tensor(e[:, 0:S], a[:, 0:S], band[:, t, :] if kind == "C" else bias_d(h, t), ALU.add).then_inc(
                        *did("vector", ("biased", it)))
                    link(v.tensor_copy(e[:, S:2 * S], a[:, S:2 * S]), ("read", "s", it, 0))
                ins = v.reduce_max(nmax[:, i % 4, 0:1], e[:, 0:kt * P], AX_X, negate=True)
                if kind == "C":
                    link(ins)
                    ins = v.tensor_tensor(nmax[:, i % 4, 0:1], nmax[:, i % 4, 0:1], nsink[:, h:h + 1], ALU.min)
                ins.then_inc(*did("vector", ("max", it)))

            def combine(i, it):
                _, kt, _ = item_info(it)
                n = kt * P
                e = EE[0][:, i % 3, :]
                dve.wait_ge(*after("exp", it))
                link(v.reciprocal(rinv[:, i % 4, :], rsum[:, i % 4, :]))
                link(v.tensor_scalar(rinv[:, i % 4, 1:2], rinv[:, i % 4, 1:2], lam[:, 3:4], None, ALU.mult))
                link(v.tensor_scalar(e[:, 512:512 + n], e[:, 512:512 + n], rinv[:, i % 4, 1:2], None, ALU.mult))
                v.scalar_tensor_tensor(out=e[:, 0:n], in0=e[:, 0:n], scalar=rinv[:, i % 4, 0:1], in1=e[:, 512:512 + n],
                                       op0=ALU.mult, op1=ALU.add).then_inc(*did("vector", ("probs", it)))

            def outputs(i, it):
                kind, l, h, t = it
                dve.wait_ge(*after("o", it))
                if kind != "B":
                    dve.wait_ge(*after("exp", it))
                    if kind == "C":
                        link(v.tensor_tensor(rsum[:, i % 4, 0:1], rsum[:, i % 4, 0:1], esink[:, i % 4:i % 4 + 1], ALU.add))
                    link(v.reciprocal(rinv[:, i % 4, 0:1], rsum[:, i % 4, 0:1]))
                if kind == "first":
                    g = gb[:, t, (l * 8 + h) * DH:(l * 8 + h + 1) * DH]
                    dve.wait_ge(*after("gbs", l, t))
                    v.scalar_tensor_tensor(out=g, in0=src("o", it)[:, 0:DH], scalar=rinv[:, i % 4, 0:1], in1=g,
                                           op0=ALU.mult, op1=ALU.mult).then_inc(*did("vector", ("gated", it), ("read", "o", it)))
                elif kind == "B":
                    link(v.tensor_copy(mix[:, t, NW + h * P:NW + (h + 1) * P], src("o", it)[:, 0:P]), ("read", "o", it))
                    if h == 3:
                        pair_norm(t)
                else:
                    at = (NW if kind == "D" else 0) + h * DH
                    v.tensor_scalar(mix[:, t, at:at + DH], src("o", it)[:, 0:DH], rinv[:, i % 4, 0:1], None, ALU.mult).then_inc(
                        *did("vector", ("read", "o", it), *([("mixed out", 1, t)] if kind == "D" and h == 7 else [])))

            def pair_norm(t):
                m = mix[:, t, NW:2 * NW].rearrange("p (h d) -> p h d", d=P)
                e = subtmp[:, :].rearrange("p (h d) -> p h d", d=P)
                link(v.tensor_tensor(e, m, m, ALU.mult))
                link(v.reduce_sum(hss[:, 0, 0:4], e, AX_X))
                rsqrt(hrs[:, 0, 0:4], hss[:, 0, 0:4], P, EPS)
                link(v.tensor_tensor(m, m, heads_view(hrs[:, 0, 0:4], (1, 4), (0, P)), ALU.mult))
                link(v.tensor_tensor(m, m, heads_view(sublng[:, :], (0, 4), (1, P)), ALU.mult), ("mixed out", 0, t))

            def attend(items, mods):
                for i in range(len(items) + 3):
                    if i < len(items):
                        maxima(i, items[i])
                    for m in mods_at(i, items, mods):
                        mod_row(*m)
                    if items[0][0] == "B" and 0 <= i - 1 < len(items):
                        combine(i - 1, items[i - 1])
                    if 0 <= i - 3 < len(items):
                        outputs(i - 3, items[i - 3])

            def mod_columns(l, r):
                n = 16 * (r + 1)
                dve.wait_ge(*after("modT", l, r))
                dve.wait_ge(loads["modb"], 16)
                dve.wait_ge(loads["normc"], 16)
                link(v.tensor_tensor(modT[:, :, 0:n], src("modT", l, r)[:, 0:2 * n].rearrange("p (a b) -> p a b", a=2),
                                     heads_view(modb[:, l, 16 * r:], (0, 2), (1, n)), ALU.add), ("read", "modT", l, r))
                at = 8 * r
                gain = heads_view(normc[:, l, 2 * r, :], (0, 2), (1, KD))
                v.tensor_copy(modB[:, l, r, :, :], modT[:, :, at:at + KD]).then_inc(*did("vector"))
                link(v.scalar_tensor_tensor(out=modA[:, l, r, :, :], in0=modT[:, :, at + KD:at + 2 * KD], scalar=1.0,
                                            in1=gain, op0=ALU.add, op1=ALU.mult))
                if r:
                    for which in range(2):
                        gain = heads_view(normc[:, l, 2 * which + 1, :], (0, 2), (1, KD))
                        ins = v.tensor_tensor(gcol[:, which, :, :], modT[:, :, 24 * which:24 * which + KD], gain, ALU.mult)
                        ins.then_inc(*did("vector", *([("gcol", l)] if which else [])))

            def gate_rows(l):
                dve.wait_ge(*after("grow", l))
                if l:
                    dve.wait_ge(loads["gsave"], 16 * l)
                v.tensor_copy(grow[:, :], src("grow", l)[0:32, 0:P]).then_inc(*did("vector", ("growc", l), ("read", "grow", l)))

            dve.wait_ge(loads["dist"], 16)
            for hf in range(2):
                for what in ("k", "q", "v"):
                    for g in range(NG):
                        split_to((what, hf, g))
                split_to(("gb", hf))
                items = items_first(hf)
                attend(items, mods_first(hf))
            low_features("fo1", 2)
            for n in range(2):
                split_to(("outb", n))
                for t in range(XT):
                    if n == 0:
                        dve.wait_ge(*after("h1", t))
                    add_residual("outb", n, t)
            layer_norm(1, "outb")
            dve.wait_ge(loads["lnb"], 32)
            link(v.tensor_tensor(hx[:, 0, :], hx[:, 0, :], lnrow[:, 0, :], ALU.mult))
            link(v.tensor_tensor(hx[:, 0, :], hx[:, 0, :], lnrow[:, 1, :], ALU.add), ("ln", 1, 0))

            def normed(l, which, t):
                dve.wait_ge(*after("sq", l, which, t))
                deviation(t, sumsq[:, t:t + 1], D, EPS)
                dve.wait_ge(*after("stream root", l, which, t))
                y, factor = refined(t, fold=True)
                v.tensor_scalar(mix[:, t, :], H(t), y, factor, ALU.mult, ALU.mult).then_inc(
                    *did("vector", ("xn", l, which, t)))

            def gated_half(l, which, t, n):
                vec = 0 if t < XT else 1
                if (t, n) == (0, 0):
                    dve.wait_ge(loads[f"g{l}{which}"], 16 * (2 - l))
                dve.wait_ge(*after("sqh", l, which, t, n))
                key = ("out2", l, n, t) if which == 0 else ("acc", t, n)
                v.tensor_tensor(mix[:, t, n * NW:(n + 1) * NW], src(*key), gates[:, vec, n * NW:(n + 1) * NW], ALU.mult).then_inc(
                    *did("vector", ("read",) + key, ("gated half", l, which, t, n)))

            def sum_halves(l, which, t):
                dve.wait_ge(*after("sqh", l, which, t, 1))
                link(v.tensor_tensor(sumh[:, t, 0:1], sumh[:, t, 0:1], sumh[:, t, 1:2], ALU.add), ("sumh", l, which, t))
                deviation(4 + t, sumh[:, t, 0:1], D, EPS)

            def residual(l, which, t):
                dve.wait_ge(*after("mixer root", l, which, t))
                refined(4 + t)
                for n in range(2):
                    dve.wait_ge(*after("gated half", l, which, t, n))
                labels = [("resid", l, which, t)] + ([("final", t)] if l and which else [])
                link(v.scalar_tensor_tensor(out=H(t), in0=mix[:, t, :], scalar=rstd[:, 4 + t:5 + t], in1=H(t),
                                            op0=ALU.mult, op1=ALU.add), *labels)

            def stage(what, l, part, t):
                key = (what, l, part, t)
                small = what == "k" and part == 0
                norm = l == 0 and part == 0
                if t >= XT and not norm and not small:
                    return
                w = P if small else NW
                nh = w // DH
                r = STAGE[key]
                a = src(what + "2", l, part, t)
                e = EE[l][:, r, :]
                i = 0 if what == "q" else 1
                dve.wait_ge(*after(what + "2", l, part, t))
                if STAGE_BEFORE[key]:
                    dve.wait_ge(*after(*STAGE_BEFORE[key]))
                if norm:
                    dve.wait_ge(*after("squared", *key))
                    link(v.reduce_sum(hss[:, r, 0:nh], e[:, 512:512 + w].rearrange("p (h d) -> p h d", d=DH), AX_X))
                    rsqrt(hrs[:, r, 0:nh], hss[:, r, 0:nh], DH, EPS)
                elif small:
                    dve.wait_ge(*after("vv", l, part, t))
                read = ("read", what + "2", l, part, t)
                heads = lambda ap: ap.rearrange("p (h d) -> p h d", d=DH)
                if t < XT:
                    cos = ropeg[:, i, 0, t, :] if norm else RO[l][:, 0, t, :]
                    sin = ropeg[:, i, 1, t, :] if norm else RO[l][:, 1, t, :]
                    v.tensor_tensor(heads(e[:, 512:512 + w]), heads(a[:, 0:w]), heads_view(cos, (0, nh), (1, DH)), ALU.mult).then_inc(
                        *did("vector"))
                    for half in range(2):
                        out_ = e[:, 0:w].rearrange("p (h x f d) -> p h x f d", x=2, f=2, d=16)[:, :, :, half, :]
                        in_ = a[:, 0:w].rearrange("p (h x f d) -> p h x f d", x=2, f=2, d=16)[:, :, :, 1 - half, :]
                        ins = v.tensor_tensor(out_, in_, heads_view(sin[:, half * 16:], (0, nh), (32, 2), (1, 16)), ALU.mult)
                        if half == 0:
                            ins.then_inc(*did("vector"))
                    link(ins, read)
                    if norm:
                        link(v.tensor_tensor(e[:, 0:w], e[:, 0:w], e[:, 512:512 + w], ALU.add))
                elif norm:
                    link(v.tensor_tensor(heads(e[:, 0:w]), heads(a[:, 0:w]), heads_view(qkg[:, i, :], (0, nh), (1, DH)), ALU.mult), read)
                if small:
                    dup = lambda ap: heads_view(ap, (DH, 2), (0, 2), (1, DH))
                    dst = e[:, 256:512].rearrange("p (h c d) -> p h c d", h=2, c=2)
                    if norm:
                        ins = v.tensor_tensor(dst, dup(e[:, 0:w]), heads_view(hrs[:, r, 0:2], (1, 2), (0, 2), (0, DH)), ALU.mult)
                    elif t < XT:
                        ins = v.tensor_tensor(dst, dup(e[:, 0:w]), dup(e[:, 512:512 + w]), ALU.add)
                    else:
                        v.tensor_copy(dst, dup(a[:, 0:w])).then_inc(*did("vector", ("staged",) + key, read))
                        return
                elif norm:
                    ins = v.tensor_tensor(heads(e[:, 0:w]), heads(e[:, 0:w]), heads_view(hrs[:, r, 0:nh], (1, nh), (0, DH)), ALU.mult)
                else:
                    ins = v.tensor_tensor(e[:, 0:w], e[:, 0:w], e[:, 512:512 + w], ALU.add)
                ins.then_inc(*did("vector", ("staged",) + key))

            for l in range(2):
                nt = 4 if l == 0 else 2
                if l == 0:
                    for t in TILES[0]:
                        normed(0, 0, t)
                mod_columns(l, 0)
                for m in MODS[("q2", l, 0)]:
                    mod_row(*m)
                if l == 0:
                    dve.wait_ge(loads["ropes"], 64)
                    for i in range(2):
                        v.tensor_tensor_reduce(lamrow[:, 2 * i, :], lamrow[:, 2 * i, :], lamrow[:, 2 * i + 1, :], 1.0, 0.0,
                                               ALU.mult, ALU.add, lam[:, i:i + 1]).then_inc(
                            *did("vector", *([("lam sums",)] if i else [])))
                modulate(("n1", l), 4, l, 0)
                if l == 0:
                    mod_columns(0, 1)
                if l == 0:
                    dve.wait_ge(*after("lam exp"))
                    link(v.tensor_tensor(lam[:, 2:3], lam[:, 1:2], lam[:, 0:1], ALU.subtract))
                    link(v.tensor_scalar(lam[:, 3:4], lam[:, 2:3], -LAM0, None, ALU.add))
                    link(v.tensor_scalar(sublng[:, :], sublng[:, :], 1.0 - LAM0, None, ALU.mult))
                    for i in range(2):
                        v.tensor_tensor(ropeg[:, i, 0, :, :], rope[:, 0, :, :], heads_view(qkg[:, i, :], (0, 2), (1, DH)),
                                        ALU.mult).then_inc(*did("vector"))
                        for half in range(2):
                            halves = lambda ap: ap.rearrange("p t (x f d) -> p t x f d", x=2, f=2)[:, :, :, half, :]
                            link(v.tensor_tensor(halves(ropeg[:, i, 1, :, :]), halves(rope[:, 1, :, :]),
                                                 heads_view(qkg[:, i, 16 * (1 - half):], (0, 2), (32, 2), (1, 16)), ALU.mult))
                else:
                    dve.wait_ge(loads["odd"], 64)
                    link(v.tensor_scalar(nsink[:, :], sinkr[:, :], -1.0, None, ALU.mult))
                for part in range(2):
                    if l == 1 and part == 1:
                        split_to(("q2", l, 1))
                        split_to(("k2", l, 1))
                    else:
                        for what, tiles in (("q", range(nt)), ("k", range(4))):
                            split_to((what + "2", l, part))
                            for t in tiles:
                                stage(what, l, part, t)
                        if l == 0 and part == 0:
                            gate_rows(0)
                    if part == 1:
                        split_to(("v2", l, 1))
                        if l == 1:
                            gate_rows(1)
                    if l == 1 and part == 1:
                        dve.wait_ge(loads["bias"], 16 * 32)
                        for h in range(8):
                            for t in range(2):
                                b = bias_d(h, t)
                                ins = v.tensor_tensor(b, b, colmask[:, :], ALU.add)
                                ins.then_inc(*did("vector"))
                        dve.wait_ge(counts.sems["vector"], counts.now["vector"])
                    items = items_second(l, part)
                    attend(items, mods_second(l, part))
                    if l == 1 and part == 0:
                        mod_columns(1, 1)
                low_features(("fo", l), nt)
                for n in range(2):
                    split_to(("out2", l, n))
                    if n == 0:
                        for t in range(nt):
                            gated_half(l, 0, t, 0)
                for i in range(nt + 2):
                    if i < nt:
                        sum_halves(l, 0, i)
                        gated_half(l, 0, i, 1)
                    if 0 <= i - 1 < nt:
                        residual(l, 0, i - 1)
                    if 0 <= i - 2 < nt:
                        normed(l, 1, i - 2)
                for m in MODS.get(("in", l, 0), []):
                    mod_row(*m)
                modulate(("n2", l), nt, l, 1)
                for j in range(9):
                    if j < 8:
                        split_to(("in", l, j))
                        for e in range(4):
                            h = htmp[:, e % 2, 0:nt * P]
                            dve.wait_ge(*after("relu", l, j, e))
                            v.tensor_tensor(h, h, h, ALU.mult).then_inc(*did("vector", ("squared", l, j, e)))
                    if j:
                        split_to(("out", l, j - 1))
                        if l == 0:
                            for n in range(2):
                                for t in range(nt):
                                    m = mix[:, t, n * NW:(n + 1) * NW]
                                    key = ("acc", j - 1, t, n)
                                    dve.wait_ge(*after(*key))
                                    if j > 1:
                                        dve.wait_ge(*after("read", "acc", j - 2, t, n))
                                        ins = v.tensor_tensor(m, src(*key), m, ALU.add)
                                    else:
                                        ins = v.tensor_copy(m, src(*key))
                                    ins.then_inc(*did("vector", ("read",) + key, *([("summed", t, n)] if j == 8 else [])))
                if l == 1:
                    for t in range(nt):
                        gated_half(l, 1, t, 0)
                for i in range(nt + 2):
                    if i < nt:
                        sum_halves(l, 1, i)
                        if l == 1:
                            gated_half(l, 1, i, 1)
                    if 0 <= i - 1 < nt:
                        residual(l, 1, i - 1)
                    if l == 0 and 0 <= i - 2 < nt:
                        normed(1, 0, i - 2)

        @block.gpsimd
        def _(pool):
            p = nc.gpsimd
            st = [0]

            def split_to(name, ahead=1):
                split_lo(pool, p, UNIT[name].wn + ahead, st, 0)

            def low_modulated(name, nt, l, which):
                per = 4 // nt
                for j in range(KD // per):
                    pool.wait_ge(*after("fhi", name, j))
                    dst = flo[:, j * per:(j + 1) * per, 0:nt * P]
                    hi = fhi[:, j * per:(j + 1) * per, 0:nt * P].bitcast(F32)
                    p.tensor_tensor(dst, ftmp(l, which, j).rearrange("p (a b) -> p a b", a=per), hi, ALU.subtract).then_inc(
                        *did("pool", ("split", name, j)))

            def gain_shift(t, *label):
                h = hx[:, t, :]
                p.tensor_tensor(h, h, lnrow[:, 0, :], ALU.mult).then_inc(*did("pool"))
                pool.wait_ge(counts.sems["pool"], counts.now["pool"])
                p.tensor_tensor(h, h, lnrow[:, 1, :], ALU.add).then_inc(*did("pool", label))

            split_to(("k", 0, 0), 0)
            low_modulated("f1", 2, -1, 0)
            pool.wait_ge(*after("f1", 3))
            pool.wait_ge(loads["lna"], 32)
            for t in range(XT):
                gain_shift(t, "h1", t)
            split_to(("outb", 1), 1)
            pool.wait_ge(loads["lnb"], 32)
            pool.wait_ge(*after("centred", 1))
            gain_shift(1, "ln", 1, 1)

            for l in range(2):
                nt = 4 if l == 0 else 2
                low_modulated(("n1", l), 4, l, 0)
                split_to(("in", l, 0), 0)
                low_modulated(("n2", l), nt, l, 1)
                for j in range(9):
                    if j < 8:
                        split_to(("in", l, j))
                        for e in range(4):
                            pool.wait_ge(*after("hhi", l, j, e))
                            p.tensor_tensor(hlo[:, j % 2, e, 0:nt * P], htmp[:, e % 2, 0:nt * P],
                                            hhi[:, j % 2, e, 0:nt * P].bitcast(F32), ALU.subtract).then_inc(
                                *did("pool", ("hidden", l, j, e)))
                    if j:
                        split_to(("out", l, j - 1))
                if l == 0:
                    pool.wait_ge(loads["g01"], 32)
                    for t, n in [(t, 0) for t in range(4)] + [(t, 1) for t in range(4)]:
                        pool.wait_ge(*after("sqh", 0, 1, t, n))
                        m = mix[:, t, n * NW:(n + 1) * NW]
                        p.tensor_tensor(m, m, gates[:, 0 if t < XT else 1, n * NW:(n + 1) * NW], ALU.mult).then_inc(
                            *did("pool", ("gated half", 0, 1, t, n)))


def kernel(**inputs):
    import numpy as _np
    import concourse.bacc as _bacc
    from concourse import mybir as _mybir
    from concourse.bass_utils import run_bass_kernel_spmd as _run

    a = {k: _np.asarray(x) for k, x in inputs.items()}
    f32 = _np.float32
    stream = _np.empty((CHUNKS, P, CHUNK), f32)
    n = 0
    for u in UNITS:
        for name, idx, row, col in u.pieces:
            block = a[name][idx][row:row + u.nk * P, col:col + u.width]
            stream[n] = block.reshape(u.nk, P, u.width).transpose(1, 0, 2).reshape(P, CHUNK)
            n += 1

    def cols(x):
        y = x.reshape(x.shape[:-1] + (x.shape[-1] // P, P))
        return _np.ascontiguousarray(_np.moveaxis(y, -1, 0))

    rows = _np.zeros((8, 7, P), f32)
    rows[:, :, GRID - 16:GRID + 15] = a["rpb_d_2"][0, :, 4:11, :]
    arrays = {
        "wstream": stream,
        "x": a["x"], "ctx_2": a["ctx_2"],
        "cond": _np.ascontiguousarray(_np.moveaxis(cols(_np.stack([a["c_2"][0], a["c_ctx_2"]])), 1, 2)),
        "scale_cols": cols(a["scale_a"][0]),
        "b_mod_cols": cols(a["b_mod_2"]), "norm_cols": cols(a["norm_g_2"]),
        "ln_g": a["ln_g"], "ln_b": a["ln_b"],
        "ln_cols": cols(_np.stack([a["ln_g"][0], a["ln_b"][0]])),
        "qk_norm_a_2": a["qk_norm_a_2"], "diff_lambda_2": a["diff_lambda_2"],
        "diff_subln_2": a["diff_subln_2"], "sink_c_2": a["sink_c_2"],
        "rpb_rows": _np.ascontiguousarray(_np.broadcast_to(rows[:, :, None, :], (8, 7, GRID, P))),
        **constants(),
    }
    arrays = {k: _np.ascontiguousarray(x) for k, x in arrays.items()}

    counts = None
    for _ in range(2):
        nc = _bacc.Bacc("TRN2", target_bir_lowering=False, num_devices=1)
        T = {k: nc.dram_tensor("in_" + k, x.shape, _mybir.dt.float32, kind="ExternalInput").ap() for k, x in arrays.items()}
        out = nc.dram_tensor("out", (1, S, D), _mybir.dt.float32, kind="ExternalOutput").ap()
        counts = Counts(counts)
        build(nc, T, out, counts)
    r = _run(nc, [{"in_" + k: x for k, x in arrays.items()}], core_ids=[0])
    return r.results[0]["out"]
```

```python
from contextlib import ExitStack

import concourse.bass as bass
import numpy as np
from concourse import mybir

F32 = mybir.dt.float32
F32R = mybir.dt.float32r
I32 = mybir.dt.int32
ALU = mybir.AluOpType
ACT = mybir.ActivationFunctionType
AX_X = mybir.AxisListType.X

P = 128
D = 1024
KD = D // P
S = 256
XT = S // P
NW = 512
QW = D // 4
D_A = 2 * D
POOL_WINDOWS = (2, 4, 8, 16)
PAIRS = ((128, 1), (512, 4), (2048, 16))
NG = len(PAIRS)
HEADS = 16
DH = 64
ALPHA = 4.0 ** 0.25
LN_EPS = 1e-5
EPS = 1e-6
LAM0 = 0.8 - 0.6
QSCALE = DH ** -0.5
GRID = 64
MASKED = -1e30
RSQRT_START = float(0x5F3759DF)
NEWTON_STEPS = 3
FAR = 3e32
SLOPES = [[2.0 ** (-8.0 * (g * HEADS + h + 1) / (NG * HEADS)) for h in range(HEADS)] for g in range(NG)]

CHUNK = 2048
RAW_SLOTS = 3
SPLIT_SLOTS = 4
ETILE = 1024
BIAS_LOADS = 9
ITEMS_KEPT = 8


class Unit:

    def __init__(self, name, nk, width, pieces):
        self.name, self.nk, self.width, self.pieces = name, nk, width, pieces


MODS = {
    ('k', 0, 0): [(0, 0), (0, 1)],
    ('side', 0): [(0, 2), (0, 3)],
    ('side', 1): [(0, 4), (0, 5)],
    ('side', 2): [(0, 6), (0, 7)],
    ('side', 3): [(0, 8), (0, 9), (0, 10), (0, 11)],
    ('q2', 0, 0): [(1, 0), (1, 1)],
    ('turn', 0, 0): [(1, 2)],
    ('q2', 0, 1): [(1, 3), (1, 4), (1, 5), (1, 6)],
    ('out2', 0, 0): [(1, 7)],
    ('fo', 0): [(1, 8)],
    ('in', 0, 0): [(1, 9), (1, 10)],
    ('q2', 1, 0): [(1, 11)],
}


def side_steps():
    placed = []
    for qr in range(4):
        mods = [("mod",) + m for m in MODS["side", qr]]
        if qr < 3:
            steps = []
            for what in "kqv":
                steps += [(what, qr + 1, g, n) for g in range(NG) for n in range(2)]
                steps += [mods.pop(0)] if what != "v" else mods
        else:
            steps = mods
        placed += [(8 * qr + n * 8 // len(steps), step) for n, step in enumerate(steps)]
    return placed


def plan_units():
    units = []

    def std(name, src, idx, row, col):
        units.append(Unit(name, 4, NW, [(src, idx, row, col), (src, idx, row + 512, col)]))


    for g in range(4):
        std(("gate", g), "w_in_a", (0,), 0, D_A + g * NW)
    grp = [Unit(("grp", g), 4, NW, [("w_grp_a", (0, g), 0, 0)]) for g in range(4)]
    for g in range(4):
        std(("u", g), "w_in_a", (0,), 0, g * NW)
        if g:
            units.append(grp[g - 1])
    units.append(grp[3])
    for n in range(2):
        for kh in range(2):
            std(("outa", n, kh), "w_out_a", (0,), kh * D, n * NW)
    def projection(what, qr, g):
        src, idx, first = {"k": ("w_kv", (), 0), "q": ("w_in_b", (0,), 0), "v": ("w_kv", (), NG)}[what]
        units.append(Unit((what, qr, g), 8, QW, [(src, idx, 0, (first + g) * D + qr * QW)]))

    for what in "kqv":
        for g in range(NG):
            projection(what, 0, g)
    for n in range(2):
        std(("gb", n), "w_in_b", (0,), 0, NG * D + n * NW)
    for _, step in side_steps():
        if step[0] == "mod":
            std(step, "w_mod_2", step[1:2], 0, step[2] * NW)
        elif step[3] == 0:
            projection(*step[:3])
    for n in range(2):
        std(("outb", n), "w_out_b", (0,), 0, n * NW)
    for l in range(2):
        std(("q2", l, 0), "w_in_2", (l,), 0, 0)
        units.append(Unit(("k2", l, 0), 8, 256, [("w_in_2", (l,), 0, 512)]))
        std(("q2", l, 1), "w_in_2", (l,), 0, 768)
        std(("k2", l, 1), "w_in_2", (l,), 0, 1280)
        std(("v2", l, 1), "w_in_2", (l,), 0, 1792)
        for n in range(2):
            std(("out2", l, n), "w_out_2", (l,), 0, n * NW)
        for j in range(9):
            if j < 8:
                std(("in", l, j), "w_mlp_in_2", (l,), 0, j * NW)
            if j:
                units.append(Unit(("out", l, j - 1), 4, NW,
                                  [("w_mlp_out_2", (l,), (j - 1) * NW, n * NW) for n in range(2)]))
    weights, units = units, []
    for u in weights:
        for layer, j in MODS.get(u.name, []) + (MODS["fo", 0] if u.name == ("out2", 0, 0) else []):
            std(("mod", layer, j), "w_mod_2", (layer,), 0, j * NW)
        units.append(u)
        if u.name[0] == "k2":
            for layer, j in MODS.get(("turn",) + u.name[1:], []):
                std(("mod", layer, j), "w_mod_2", (layer,), 0, j * NW)
    w = 0
    for n, u in enumerate(units):
        u.n, u.w0 = n, w
        w += len(u.pieces)
    return units


UNITS = plan_units()
UNIT = {u.name: u for u in UNITS}
CHUNKS = sum(len(u.pieces) for u in UNITS)
assert CHUNKS % RAW_SLOTS == 0
SPLIT = [u for u in UNITS for _ in u.pieces]
LOW_ON_GPSIMD = [("mod",) + m for name, ms in MODS.items() for m in ms
                 if name not in (("q2", 1, 0), ("side", 0), ("side", 1), ("side", 2))]


def low_on_gpsimd(w):
    name = SPLIT[w].name
    return name in LOW_ON_GPSIMD or (name[0] != "mod" and w > 1 and w % 2 == 0)


def constants():
    s = np.arange(S)
    pool = np.zeros((P, 4, 272), np.float32)
    for g, w in enumerate(POOL_WINDOWS):
        m = np.zeros((S, S))
        for t in range(S):
            m[t, max(0, t - w + 1):t + 1] = 1.0 / min(t + 1, w)
            m[t, t] -= 1.0
        pool[:, g, :144] = m[:144, :P].T
        pool[:, g, 144:] = m[P:, P:].T
    dist = np.zeros((P, NG, 256), np.float32)
    for g, (window, dilation) in enumerate(PAIRS):
        rel = P + np.arange(P)[:, None] - np.arange(256)[None, :]
        ok = (rel >= 0) & (rel <= window) & (rel % dilation == 0)
        dist[:, g] = np.where(ok, rel, FAR)
    pos = np.stack([s // GRID, s % GRID], -1).astype(np.float32)
    inv = (np.float32(10000.0) ** (-np.arange(16, dtype=np.float32) / np.float32(16))).astype(np.float32)
    ang = pos[..., None] * inv
    cos, sin = np.cos(ang), np.sin(ang)
    rc = np.stack([cos, cos], 2).reshape(2, P, DH).transpose(1, 0, 2)
    rs = np.stack([-sin, sin], 2).reshape(2, P, DH).transpose(1, 0, 2)
    band = np.zeros((P, 2, S), np.float32)
    for qt in range(2):
        band[:, qt] = np.where(np.abs(qt * P + np.arange(P)[:, None] - s[None]) <= P, 0.0, MASKED)
    cq = (np.arange(P) % GRID)[:, None]
    ck = (s % GRID)[None]
    start = np.clip(cq - 8, 0, GRID - 16)
    cols = np.where((ck >= start) & (ck < start + 16), 0.0, MASKED)
    out = {"t_ident": np.eye(P), "t_pool": pool.reshape(P, -1), "t_dist": dist.reshape(P, -1),
           "t_rope": np.stack([rc, rs], 1).reshape(P, -1), "t_band": band.reshape(P, -1), "t_cols": cols}
    return {k: np.ascontiguousarray(v, dtype=np.float32) for k, v in out.items()}


def plan_stage():
    slot, before = {}, {}
    for l in range(2):
        for part in range(2 - l):
            tiles = [("q", l, part, t) for t in range(4 if l == 0 else 2)] + [("k", l, part, t) for t in range(4)]
            for n, key in enumerate(tiles):
                slot[key] = n % 3
                before[key] = (tiles[n - 3][0] + "turn",) + tiles[n - 3][1:] if n >= 3 else None
    return slot, before


STAGE, STAGE_BEFORE = plan_stage()


class Counts:

    def __init__(self, known=None):
        self.known, self.now, self.marks, self.banks = known, {}, {}, {}
        self.sems = {}

    def did(self, sem, *labels):
        n = self.now[sem] = self.now.get(sem, 0) + 1
        for label in labels:
            assert label not in self.marks, label
            self.marks[label] = (sem, n)
        return self.sems[sem], 1

    def used(self, c, *labels):
        sem, n = f"raw_used{c % RAW_SLOTS}", c // RAW_SLOTS + 1
        for label in labels:
            self.marks[label] = (sem, n)
        return self.sems[sem], 1

    def after(self, *label):
        if self.known is None:
            return self.sems["tensor"], 1
        sem, n = self.known.marks[label]
        return self.sems[sem], n

    def bank(self, *label):
        return 0 if self.known is None else self.known.banks[label]


def heads_view(ap, *dims):
    return bass.AP(tensor=ap.tensor, offset=ap.offset, ap=[list(ap.ap[0])] + [list(d) for d in dims])


def rows_to_all(ap, offset, n):
    return bass.AP(tensor=ap.tensor, offset=ap.offset + offset, ap=[[0, P], [1, n]])


def build(nc, T, out, counts):
    did, after = counts.did, counts.after
    with ExitStack() as ctx:
        def sem(name):
            s = ctx.enter_context(nc.semaphore(name))
            counts.sems[name] = s
            return s

        def tile(stack, name, shape, dt=F32):
            return stack.enter_context(nc.sbuf_tensor(name, shape, dt))

        raw = tile(ctx, "raw", [P, RAW_SLOTS, CHUNK])
        whi = tile(ctx, "whi", [P, SPLIT_SLOTS, CHUNK], F32R)
        wlo = tile(ctx, "wlo", [P, SPLIT_SLOTS, CHUNK], F32R)
        fhi = tile(ctx, "fhi", [P, KD, 512], F32R)
        flo = tile(ctx, "flo", [P, KD, 512], F32R)
        hx = tile(ctx, "hx", [P, XT, D])
        ident = tile(ctx, "ident", [P, P])
        cond = tile(ctx, "cond", [P, KD, 2])
        condp = tile(ctx, "condp", [P, KD, 4], F32R)
        modrow = tile(ctx, "modrow", [P, NW])
        modc = tile(ctx, "modc", [P, P])
        lncol = tile(ctx, "lncol", [P, 2, KD])
        eps = tile(ctx, "eps", [P, 2])
        modb = tile(ctx, "modb", [P, 2, 48])
        normc = tile(ctx, "normc", [P, 2, 4, KD])
        modT = tile(ctx, "modT", [P, 2, 32])
        modA = tile(ctx, "modA", [P, 2, 2, 2, KD])
        modB = tile(ctx, "modB", [P, 2, 2, 2, KD])
        gcol = tile(ctx, "gcol", [P, 2, 2, KD])
        grow = tile(ctx, "grow", [32, P])
        scol = tile(ctx, "scol", [P, 16])
        stats = tile(ctx, "stats", [P, XT, 2, 6])
        mv = tile(ctx, "mv", [P, XT, 2])
        rstd = tile(ctx, "rstd", [P, 8])
        dev = tile(ctx, "dev", [P, 8])
        sumsq = tile(ctx, "sumsq", [P, 4])
        sumh = tile(ctx, "sumh", [P, 4, 2])
        newton = tile(ctx, "newton", [P, 2, 8])
        hss = tile(ctx, "hss", [P, 3, 8])
        hrs = tile(ctx, "hrs", [P, 3, 8])
        nmax = tile(ctx, "nmax", [P, ITEMS_KEPT, 2])
        rsum = tile(ctx, "rsum", [P, ITEMS_KEPT, 2])
        rinv = tile(ctx, "rinv", [P, ITEMS_KEPT, 2])
        esink = tile(ctx, "esink", [P, ITEMS_KEPT])
        lam = tile(ctx, "lam", [P, 4])

        one = ExitStack()
        gsil_a = ExitStack()
        sgate = tile(gsil_a, "sgate", [P, 16, S])
        yhi = tile(gsil_a, "yhi", [P, 16, S], F32R)
        ylo = tile(gsil_a, "ylo", [P, 16, S], F32R)
        sub = ExitStack()
        utok = tile(sub, "utok", [P, XT, NW])
        phi = tile(sub, "phi", [P, 4, S], F32R)
        plo = tile(sub, "plo", [P, 4, S], F32R)
        poolT = tile(sub, "poolT", [P, 4, 272])
        sub.close()
        gsil_a.close()
        kT1 = tile(one, "kT1", [P, 2, NG * 2, S])
        qT1 = tile(one, "qT1", [P, 2, NG * 2, S])
        v1 = tile(one, "v1", [P, 2, XT, NG, QW])
        gb = tile(one, "gb", [P, XT, D])
        e1 = tile(one, "e1", [P, 3, 768])
        p1 = tile(one, "p1", [P, 2, 768])
        dist = tile(one, "dist", [P, NG, 256])
        lnrow = tile(one, "lnrow", [P, 2, D])
        one.close()
        hc = tile(ctx, "hc", [P, XT, D])
        mix = tile(ctx, "mix", [P, 4, D])
        att = ExitStack()
        kT = tile(att, "kT", [P, 4, 512])
        qT = tile(att, "qT", [P, 4, 512])
        vv = tile(att, "vv", [P, 4, 512])
        e2 = tile(att, "e2", [P, 3, ETILE])
        p2 = tile(att, "p2", [P, 2, 512])
        rope = tile(att, "rope", [P, 2, 2, DH])
        ropeg = tile(att, "ropeg", [P, 2, 2, 2, DH])
        qkg = tile(att, "qkg", [P, 2, DH])
        sublng = tile(att, "sublng", [P, P])
        lamrow = tile(att, "lamrow", [P, 4, DH])
        subtmp = tile(att, "subtmp", [P, NW])
        att.close()
        ffn = ExitStack()
        hhi = tile(ffn, "hhi", [P, 2, 4, 512], F32R)
        hlo = tile(ffn, "hlo", [P, 2, 4, 512], F32R)
        htmp = tile(ffn, "htmp", [P, 2, 512])
        gates = tile(ffn, "gates", [P, 2, D])
        ffn.close()
        att_b = ExitStack()
        kT_b = tile(att_b, "kT_b", [P, 6, 512])
        qT_b = tile(att_b, "qT_b", [P, 4, 512])
        vv_b = tile(att_b, "vv_b", [P, 4, P + NW])
        e2_b = tile(att_b, "e2_b", [P, 3, ETILE])
        p2_b = tile(att_b, "p2_b", [P, 2, 512])
        rope_b = tile(att_b, "rope_b", [P, 2, 2, DH])
        band = tile(att_b, "band", [P, 2, S])
        sinkr = tile(att_b, "sinkr", [P, 8])
        nsink = tile(att_b, "nsink", [P, 8])
        att_b.close()
        KT, QT, VV, EE, PP, RO = (kT, kT_b), (qT, qT_b), (vv, vv_b), (e2, e2_b), (p2, p2_b), (rope, rope_b)

        ps = ctx.enter_context(nc.psum_tensor("ps", [P, 8, 512], F32))
        modd = nc.dram_tensor("modd", (2, 4, 6 * D), F32, kind="Internal").ap()
        gated = nc.dram_tensor("gated", (2, 4, D), F32, kind="Internal").ap()

        for name in ("tensor", "scalar", "vector", "pool"):
            sem(name)
        raw_in = [sem(f"raw_in{i}") for i in range(RAW_SLOTS)]
        for i in range(RAW_SLOTS):
            sem(f"raw_used{i}")
        loads = {}

        def H(t):
            return hx[:, t, :] if t < XT else hc[:, t - XT, :]

        colmask = mix[:, 0, NW:NW + S]

        def bias_d(h, t):
            return mix[:, XT + t, h * S:(h + 1) * S] if h < 4 else hc[:, t, (h - 4) * S:(h - 3) * S]

        def load_sem(name):
            if name not in loads:
                loads[name] = sem("in_" + name)
            return loads[name]

        for name in ("x", "ident", "cond", "pool", "scol", "modb", "normc", "lncol", "lna", "lnb", "dist", "ctx",
                     "ropes", "modsave0", "modsave1", "modsave2", "modsave3", "modc00", "modc01", "modc10", "modc11", "gsave", "out",
                     "g00", "g01", "g10", "g11", "bias", "odd"):
            load_sem(name)

        def whalf(which, u, k, c0, c1):
            w = u.w0 + k // u.nk
            base = (k % u.nk) * u.width
            return which[:, w % SPLIT_SLOTS, base + c0:base + c1]

        def items_first():
            return [("first", qr, h, qt) for qr in range(4) for h in range(4) for qt in range(2)]

        def first_of_unit(step):
            if step[0] == "bias":
                return None
            return step if step[0] == "mod" else step[:3] if step[3] == 0 else None

        def side_steps_last():
            steps = [(what, 1, 1, n) for what in ("q2", "k2", "v2") for n in range(4)]
            return [(n * 16 // len(steps), step) for n, step in enumerate(steps)] + [(n, ("bias", n)) for n in range(BIAS_LOADS)]

        def items_second(l, part):
            if l == 0 and part == 0:
                return [("A", 0, h, t) for h in range(8) for t in range(4)]
            if l == 0:
                return [("B", 0, h, t) for t in range(4) for h in range(4)]
            return [(kind, 1, h, t) for kind in "CD" for h in range(8) for t in range(2)]

        def mods_second(l, part):
            return [] if l else MODS["out2", 0, 0] if part else MODS["q2", 0, 1]

        def mods_at(i, items, mods):
            every = max(1, len(items) // (len(mods) + 1))
            return [mods[i // every - 1]] if i and i % every == 0 and i // every <= len(mods) else []

        def item_info(it):
            kind, _, h, t = it
            if kind == "first":
                n = 128 * (t + 1)
                return [(g, n) for g in range(NG)], NG * (t + 1), DH
            n = 512 if t < XT else 256
            return [(j, n) for j in range(2 if kind == "B" else 1)], n // P, (P if kind == "B" else DH)

        def key_tile(it, j):
            if it[0] == "first":
                nt = it[3] + 1
                return j // nt, j % nt
            return 0, j + (0 if it[3] < XT else XT)

        block = ctx.enter_context(nc.Block())

        @block.sync
        def _(sp):
            sp.dma_start(hx[:, :, :], T["x"].rearrange("a (t p) d -> p (a t) d", p=P)).then_inc(loads["x"], 16)
            sp.dma_start(ident[:, :], T["t_ident"]).then_inc(loads["ident"], 16)
            for s in range(RAW_SLOTS):
                sp.dma_start(raw[:, s, :], T["wstream"][s]).then_inc(raw_in[s], 16)
            with sp.Fori(1, CHUNKS // RAW_SLOTS) as i:
                for s in range(RAW_SLOTS):
                    sp.wait_ge(counts.sems[f"raw_used{s}"], i)
                    sp.dma_start(raw[:, s, :], T["wstream"][i * RAW_SLOTS + s]).then_inc(raw_in[s], 16)
            for t in range(XT):
                sp.wait_ge(*after("final", t))
                sp.dma_start(out.rearrange("a (t p) d -> t p (a d)", p=P)[t], hx[:, t, :]).then_inc(loads["out"], 16)
            sp.wait_ge(loads["out"], 16 * XT)

        def wait_raw(eng, c):
            eng.wait_ge(raw_in[c % RAW_SLOTS], 16 * (c // RAW_SLOTS + 1))

        @block.tensor
        def _(pe):
            mm = nc.tensor.matmul
            last = {}
            turn = [0, 0]
            state = {"banks": list(range(8))}

            def job(*label, side=0):
                banks = (6, 7) if side else state["banks"]
                b = banks[turn[side] % len(banks)]
                turn[side] += 1
                if b in last:
                    pe.wait_ge(*after("read", *last[b]))
                last[b] = label
                counts.banks[label] = b
                return ps[:, b, :]

            def mm3(o, lh, ll, rh, rl, start, stop):
                mm(o, lh, rh, start=start, stop=False)
                mm(o, lh, rl, start=False, stop=False)
                return mm(o, ll, rh, start=False, stop=stop)

            def wait_weights(u, k):
                if k % u.nk == 0:
                    pe.wait_ge(*after("lo", u.w0 + k // u.nk))

            def wait_feature(feat, k):
                name, nt = feat
                per = 4 // nt
                if k % per == 0:
                    pe.wait_ge(*after("split", name, k // per))

            def by_token(u, name, tiles, kt=KD, width=NW, feat=None, first=True, last=True, side=0):
                for t in tiles:
                    o = job(*name, t, side=side)
                    for k in range(kt):
                        if first and t == tiles[0]:
                            wait_weights(u, k)
                        if feat and t == tiles[0]:
                            wait_feature(feat, k)
                        ins = mm3(o[:, 0:width], fhi[:, k, t * P:t * P + P], flo[:, k, t * P:t * P + P],
                                  whalf(whi, u, k, 0, width), whalf(wlo, u, k, 0, width), k == 0, k == kt - 1)
                    labels = [name + (t,)] + ([("used", u.n)] if last and t == tiles[-1] else [])
                    ins.then_inc(*did("tensor", *labels))

            def by_feature(u, name, c0, c1, feat=None, tiles=range(4), side=0):
                for e in tiles:
                    o = job(*name, e, side=side)
                    for k in range(KD):
                        if e == 0:
                            wait_weights(u, k)
                        if feat and e == 0:
                            wait_feature(feat, k)
                        ins = mm3(o[:, 0:c1 - c0], whalf(whi, u, k, e * P, e * P + P), whalf(wlo, u, k, e * P, e * P + P),
                                  fhi[:, k, c0:c1], flo[:, k, c0:c1], k == 0, k == KD - 1)
                    labels = [name + (e,)] + ([("used", u.n)] if (e + 1) * P == u.width else [])
                    ins.then_inc(*did("tensor", *labels))

            def turn_features(name, src, nt, ready):
                per = 4 // nt
                for j in range(KD // per):
                    o = job(name, j)
                    if j == 0:
                        for r in ready:
                            pe.wait_ge(*after(*r))
                    for q in range(per):
                        for t in range(nt):
                            k = j * per + q
                            c = (q * nt + t) * P
                            ins = nc.tensor.transpose(o[:, c:c + P], src(t)[:, k * P:k * P + P], ident[:, :])
                    ins.then_inc(*did("tensor", (name, j)))

            def mod(l, j, side=0):
                u = UNIT[("mod", l, j)]
                o = job("mod", l, j, side=side)
                if l == 0 and j == 0:
                    pe.wait_ge(*after("cond"))
                for k in range(KD):
                    wait_weights(u, k)
                    mm(o[0:4, :], condp[:, k, :], whalf(whi, u, k, 0, NW), start=k == 0, stop=False)
                    ins = mm(o[0:4, :], condp[:, k, :], whalf(wlo, u, k, 0, NW), start=False, stop=k == KD - 1)
                ins.then_inc(*did("tensor", ("mod", l, j), ("used", u.n)))

            def mod_columns(l, r):
                n = 64 * (r + 1)
                o = job("modT", l, r)
                pe.wait_ge(loads[f"modc{l}{r}"], 64)
                nc.tensor.transpose(o[:, 0:n], modc[0:n, :], ident[0:n, 0:n]).then_inc(*did("tensor", ("modT", l, r)))

            def gate_rows(l):
                o = job("grow", l)
                pe.wait_ge(*after("gcol", l))
                nc.tensor.transpose(o[0:32, 0:P], gcol[:, :, :, :].rearrange("p a b c -> p (a b c)"),
                                    ident[:, :]).then_inc(*did("tensor", ("grow", l)))

            def mods_before(name):
                for m in MODS.get(name, []):
                    mod(*m)

            def scores(it):
                kind, l, h, t = it
                parts, _, _ = item_info(it)
                if kind == "first":
                    po, tq = (h % 2) * DH, h // 2
                    n = parts[0][1]
                    o = job("s", it, 0)
                    o2 = job("s", it, 1) if t else None
                    if h == 0 and t == 0:
                        for g in range(NG):
                            for e in range(2):
                                pe.wait_ge(*after("k1", l, g, e))
                                pe.wait_ge(*after("q1", l, g, e))
                    for g in range(NG):
                        dst = o[:, g * n:(g + 1) * n] if not t or g < 2 else o2[:, 0:n]
                        ins = mm(dst, qT1[po:po + DH, l % 2, g * 2 + tq, t * P:t * P + P],
                                 kT1[po:po + DH, l % 2, g * 2 + tq, 0:n],
                                 start=True, stop=True)
                else:
                    part = {"A": 0, "B": 1, "C": 0, "D": 1}[kind]
                    if h == 0 and t == 0:
                        for tt in range(4):
                            pe.wait_ge(*after("kT", l, part, tt))
                        for tt in range(4 if l == 0 else 2):
                            pe.wait_ge(*after("qT", l, part, tt))
                    k0, k1 = (0, 512) if t < XT else (256, 512)
                    for j, n in parts:
                        head = 2 * h + j if kind == "B" else h
                        po, tq = (head % 2) * DH, head // 2
                        tk = {"A": h // 4, "B": tq, "C": h // 4, "D": 2 + tq}[kind]
                        q0 = S if kind == "D" else 0
                        o = job("s", it, j)
                        ins = mm(o[:, 0:n], QT[l][po:po + DH, tq, q0 + t * P:q0 + t * P + P], KT[l][po:po + DH, tk, k0:k1],
                                 start=True, stop=True)
                ins.then_inc(*did("tensor", ("s", it)))

            def turns(i, it):
                _, kt, _ = item_info(it)
                e = e1 if it[0] == "first" else EE[it[1]]
                pe.wait_ge(*after("probs", it))
                for b in range(0, kt, 4):
                    o = job("t", it, b)
                    for j in range(b, min(kt, b + 4)):
                        ins = nc.tensor.transpose(o[:, (j - b) * P:(j - b + 1) * P], e[:, i % 3, j * P:j * P + P], ident[:, :])
                    ins.then_inc(*did("tensor", ("t", it, b)))

            def values(i, it):
                kind, l, h, t = it
                _, kt, dv = item_info(it)
                p = p1 if kind == "first" else PP[l]
                o = job("o", it)
                if h == 0 and t == 0:
                    for tt in range(2 if kind == "first" else 4):
                        for g in range(NG if kind == "first" else 1):
                            pe.wait_ge(*(after("v1", l, g, tt) if kind == "first"
                                         else after("vv", l, {"A": 0, "B": 1, "C": 0, "D": 1}[kind], tt)))
                for b in range(0, kt, 4):
                    pe.wait_ge(*after("pT", it, b))
                for j in range(kt):
                    g, tt = key_tile(it, j)
                    if kind == "first":
                        v = v1[:, l % 2, tt, g, h * DH:(h + 1) * DH]
                    elif kind in "AC":
                        v = VV[l][:, tt, (h // 4) * DH:(h // 4 + 1) * DH]
                    else:
                        v0 = P if kind == "D" else 0
                        v = VV[l][:, tt, v0 + h * dv:v0 + (h + 1) * dv]
                    ins = mm(o[:, 0:dv], p[:, i % 2, j * P:j * P + P], v, start=j == 0, stop=j == kt - 1)
                ins.then_inc(*did("tensor", ("o", it)))

            def attend(items, mods, steps=()):
                for i in range(len(items) + 3):
                    if i < len(items):
                        scores(items[i])
                    alone = items[0][0] in ("first", "C") and i >= len(items) - (8 if items[0][0] == "first" else 16)
                    if alone:
                        state["banks"] = list(range(8))
                    for at, step in steps:
                        if step[0] == "bias":
                            continue
                        if at == i and step[0] == "mod":
                            mod(*step[1:], side=0 if alone else 1)
                        elif at == i and step[0] == "v2":
                            by_token(UNIT[step[:3]], step[:3], [step[3]], last=step[3] == 3, first=step[3] == 0, side=1)
                        elif at == i and step[0] in ("q2", "k2"):
                            by_feature(UNIT[step[:3]], step[:3], 0, S if step[0] == "q2" else 2 * S, tiles=[step[3]], side=1)
                        elif at == i and step[0] == "v":
                            by_token(UNIT[step[:3]], step[:3], [step[3]], width=QW, last=step[3] == 1, first=step[3] == 0,
                                     side=1)
                        elif at == i:
                            by_feature(UNIT[step[:3]], step[:3], 0, S, tiles=[step[3]], side=1)
                    for m in mods_at(i, items, mods):
                        mod(*m)
                    if 0 <= i - 2 < len(items):
                        turns(i - 2, items[i - 2])
                    if 0 <= i - 3 < len(items):
                        values(i - 3, items[i - 3])

            pe.wait_ge(loads["x"], 16)
            pe.wait_ge(loads["ident"], 16)
            turn_features("fx", lambda t: hx[:, t, :], 2, [])
            for g in range(4):
                by_feature(UNIT[("gate", g)], ("gate", g), 0, S, feat=None if g else ("fx", 2))

            def pool(g):
                if g == 0:
                    pe.wait_ge(loads["pool"], 16)
                for t in range(XT):
                    pe.wait_ge(*after("utok", g, t))
                for c in range(0, 4, 2):
                    o = job("pooled", g, c)
                    for q in range(2):
                        cc = slice((c + q) * P, (c + q + 1) * P)
                        r = o[:, q * S:(q + 1) * S]
                        mm(r[:, 0:144], utok[:, 0, cc], poolT[:, g, 0:144], start=q == 0, stop=False, skip_group_check=True)
                        ins = mm(r[:, 128:256], utok[:, 1, cc], poolT[:, g, 144:272], start=False, stop=True,
                                 skip_group_check=True)
                    ins.then_inc(*did("tensor", ("pooled", g, c)))

            def group(g):
                u = UNIT[("grp", g)]
                wait_weights(u, 0)
                for c in range(0, 4, 2):
                    pe.wait_ge(*after("pooled split", g, c))
                for e in range(4):
                    o = job("mixed", g, e)
                    for k in range(4):
                        ins = mm3(o[:, 0:S], whalf(whi, u, k, e * P, e * P + P), whalf(wlo, u, k, e * P, e * P + P),
                                  phi[:, k, :], plo[:, k, :], k == 0, k == 3)
                    labels = [("mixed", g, e)] + ([("used", u.n)] if e == 3 else [])
                    ins.then_inc(*did("tensor", *labels))

            for g in range(4):
                by_token(UNIT[("u", g)], ("u", g), range(XT))
                if g:
                    pool(g - 1) if g == 1 else None
                    group(g - 1)
                    pool(g)
            group(3)

            for n in range(2):
                outs = []
                for kh in range(2):
                    u = UNIT[("outa", n, kh)]
                    for t in range(XT):
                        if kh == 0:
                            outs.append(job("outa", n, t))
                        for k in range(KD):
                            kk = kh * KD + k
                            if t == 0:
                                wait_weights(u, k)
                            if n == 0 and t == 0:
                                pe.wait_ge(*after("y", kk))
                            ins = mm3(outs[t], yhi[:, kk, t * P:t * P + P], ylo[:, kk, t * P:t * P + P],
                                      whalf(whi, u, k, 0, NW), whalf(wlo, u, k, 0, NW), kk == 0, kk == 15)
                        labels = ([("outa", n, t)] if kh else []) + ([("used", u.n)] if t == 1 else [])
                        if labels:
                            ins.then_inc(*did("tensor", *labels))
            mods_before(("k", 0, 0))
            turn_features("f1", lambda t: hx[:, t, :], 2, [("ln", 0, 0), ("ln", 0, 1)])
            for what in "kq":
                for g in range(NG):
                    by_feature(UNIT[what, 0, g], (what, 0, g), 0, S, feat=("f1", 2) if (what, g) == ("k", 0) else None,
                               tiles=range(2))
            for g in range(NG):
                by_token(UNIT["v", 0, g], ("v", 0, g), range(XT), width=QW)
            for n in range(2):
                by_token(UNIT["gb", n], ("gb", n), range(XT))
            state["banks"] = list(range(6))
            attend(items_first(), [], side_steps())
            turn_features("fo1", lambda t: gb[:, t, :], 2, [("gated", items_first()[-1])])
            for n in range(2):
                by_token(UNIT[("outb", n)], ("outb", n), range(XT), feat=None if n else ("fo1", 2))

            for l in range(2):
                nt = 4 if l == 0 else 2
                mods_before(("q2", l, 0))
                mod_columns(l, 0)
                turn_features(("n1", l), lambda t: mix[:, t, :], 4, [("xn", l, 0, t) for t in range(4)])

                def turn_heads(what, part, tiles, ntile):
                    for t in tiles:
                        r = STAGE[(what, l, part, t)]
                        o = job(what + "turn", l, part, t)
                        pe.wait_ge(*after("staged", what, l, part, t))
                        off = 256 if what == "k" and part == 0 else 0
                        for j in range(ntile):
                            ins = nc.tensor.transpose(o[:, j * P:(j + 1) * P], EE[l][:, r, off + j * P:off + j * P + P], ident[:, :])
                        ins.then_inc(*did("tensor", (what + "turn", l, part, t)))

                for part in range(2 - l):
                    by_token(UNIT[("q2", l, part)], ("q2", l, part), range(nt), feat=None if part else (("n1", l), 4))
                    by_token(UNIT[("k2", l, part)], ("k2", l, part), range(4), width=256 if part == 0 else NW)
                    if part == 1:
                        by_token(UNIT[("v2", l, 1)], ("v2", l, 1), range(2), last=False)
                    for m in MODS.get(("turn", l, part), [])[:-1]:
                        mod(*m)
                    turn_heads("q", part, range(nt), 4)
                    for m in MODS.get(("turn", l, part), [])[-1:]:
                        mod(*m)
                    turn_heads("k", part, range(4), 2 if part == 0 else 4)
                    if part == 1:
                        by_token(UNIT[("v2", l, 1)], ("v2", l, 1), range(2, 4))
                    if l == 0 and part == 0:
                        mod_columns(0, 1)
                        gate_rows(0)
                    beside = l == 1
                    if beside:
                        mod_columns(1, 1)
                        gate_rows(1)
                    if beside:
                        state["banks"] = list(range(6))
                    attend(items_second(l, part), mods_second(l, part), side_steps_last() if beside else ())
                    state["banks"] = list(range(8))
                mods_before(("fo", l))
                turn_features(("fo", l), lambda t: mix[:, t, :], nt, [("mixed out", l, t) for t in range(nt)])
                for n in range(2):
                    by_token(UNIT[("out2", l, n)], ("out2", l, n), range(nt), feat=None if n else (("fo", l), nt))
                mods_before(("in", l, 0))
                turn_features(("n2", l), lambda t: mix[:, t, :], nt, [("xn", l, 1, t) for t in range(nt)])
                if l == 1:
                    held = {}
                    for t in range(XT):
                        for n in range(2):
                            held[t, n] = job("acc", t, n)
                    state["banks"] = [b for b in range(8) if b not in [counts.banks[("acc", t, n)] for t in range(2) for n in range(2)]]
                for j in range(9):
                    if j < 8:
                        by_feature(UNIT[("in", l, j)], ("in", l, j), 0, nt * P, feat=None if j else (("n2", l), nt))
                    if j:
                        u = UNIT[("out", l, j - 1)]
                        for k in (0, 4):
                            wait_weights(u, k)
                        for e in range(4):
                            pe.wait_ge(*after("hidden", l, j - 1, e))
                        b = (j - 1) % 2
                        for n in range(2):
                            w = (u.w0 + n) % SPLIT_SLOTS
                            for t in range(nt):
                                o = held[t, n] if l else job("acc", j - 1, t, n)
                                for k in range(4):
                                    first, stop = (k == 0, k == 3) if l == 0 else (j == 1 and k == 0, j == 8 and k == 3)
                                    ins = mm3(o, hhi[:, b, k, t * P:t * P + P], hlo[:, b, k, t * P:t * P + P],
                                              whi[:, w, k * NW:(k + 1) * NW], wlo[:, w, k * NW:(k + 1) * NW], first, stop)
                                labels = [("used", u.n)] if n == 1 and t == nt - 1 else []
                                if l == 0:
                                    labels.append(("acc", j - 1, t, n))
                                elif j == 8:
                                    labels.append(("acc", t, n))
                                if labels:
                                    ins.then_inc(*did("tensor", *labels))

        def last_split(name, ahead):
            return UNIT[name].w0 + (SPLIT_SLOTS if ahead else len(UNIT[name].pieces)) - 1

        def split_hi(act, upto, state):
            while state[0] < min(CHUNKS, upto + 1):
                w = state[0]
                wait_raw(act, w)
                if w >= SPLIT_SLOTS:
                    act.wait_ge(*after("used", SPLIT[w - SPLIT_SLOTS].n))
                nc.scalar.activation(whi[:, w % SPLIT_SLOTS, :], raw[:, w % RAW_SLOTS, :], ACT.Copy).then_inc(
                    *did("scalar", ("hi", w)))
                state[0] += 1

        def split_lo(eng, ops, upto, state, gpsimd):
            while state[0] < min(CHUNKS, upto + 1):
                w = state[0]
                if low_on_gpsimd(w) == gpsimd:
                    eng.wait_ge(*after("hi", w))
                    ops.tensor_tensor(wlo[:, w % SPLIT_SLOTS, :], raw[:, w % RAW_SLOTS, :],
                                      whi[:, w % SPLIT_SLOTS, :].bitcast(F32), ALU.subtract).then_inc(
                        *counts.used(w, ("lo", w)))
                state[0] += 1

        def ftmp(l, which, j):
            if l < 0:
                return e1[:, j % 2, 0:512]
            return EE[l][:, j % 2, 0:512] if which == 0 else htmp[:, j % 2, :]

        GROUPS = (((0, 1), (2, 3)), ((0,), (1,)))
        STREAM_GROUPS = ((2, 3), (0, 1))

        @block.scalar
        def _(act):
            copy = nc.scalar.activation
            st = [0]
            act.dma_start(cond[:, :, :], T["cond"]).then_inc(loads["cond"], 16)
            act.dma_start(scol[:, :], T["scale_cols"]).then_inc(loads["scol"], 16)
            act.dma_start(modb[:, :, :], T["b_mod_cols"]).then_inc(loads["modb"], 16)
            act.dma_start(normc[:, :, :, :], T["norm_cols"]).then_inc(loads["normc"], 16)
            act.dma_start(lncol[:, :, :], T["ln_cols"]).then_inc(loads["lncol"], 16)

            def split_to(name, ahead=1):
                split_hi(act, last_split(name, ahead), st)

            def split_mods(name, i):
                if i < len(MODS.get(name, [])):
                    split_to(("mod",) + MODS[name][i])

            def src(*label):
                return ps[:, counts.bank(*label), :]

            def split_features(name, nt, tmp=None):
                per = 4 // nt
                for j in range(KD // per):
                    dst = fhi[:, j * per:(j + 1) * per, 0:nt * P]
                    if tmp is None:
                        act.wait_ge(*after(name, j))
                        got = src(name, j)
                    else:
                        act.wait_ge(*after("modulated", name, j))
                        got = ftmp(*tmp, j)
                    copy(dst, got.rearrange("p (a b) -> p a b", a=per), ACT.Copy).then_inc(
                        *did("scalar", ("fhi", name, j)))

            def save_mod(l, j):
                act.wait_ge(*after("read", "mod", l, j))
                q = j % 4 * 32
                act.dma_start(modd[l, :, j * NW:(j + 1) * NW], modrow[q:q + 4, :]).then_inc(
                    loads[f"modsave{j % 4}"], 16)

            act.wait_ge(loads["cond"], 16)
            copy(cond[:, :, :], cond[:, :, :], ACT.Silu).then_inc(*did("scalar", ("silu",)))
            act.wait_ge(*after("silu"))
            copy(condp[:, :, 0:2], cond[:, :, :], ACT.Copy).then_inc(*did("scalar", ("cond high",)))
            split_features("fx", 2)
            split_hi(act, 3, st)
            act.dma_start(poolT[:, :, :], T["t_pool"].rearrange("p (g t) -> p g t", g=4)).then_inc(loads["pool"], 16)
            for g in range(4):
                split_to(("gate", g))
                for e in range(4):
                    act.wait_ge(*after("gate", g, e))
                    copy(sgate[:, g * 4 + e, :], src("gate", g, e)[:, 0:S], ACT.Silu).then_inc(
                        *did("scalar", ("sgate", g * 4 + e), ("read", "gate", g, e)))

            def u_copy(g):
                split_to(("u", g))
                for t in range(XT):
                    act.wait_ge(*after("u", g, t))
                    if g:
                        act.wait_ge(*after("pooled", g - 1, 2))
                    copy(utok[:, t, :], src("u", g, t), ACT.Copy).then_inc(
                        *did("scalar", ("utok", g, t), ("read", "u", g, t)))

            def pooled_hi(g):
                for c in range(0, 4, 2):
                    act.wait_ge(*after("pooled", g, c))
                    copy(phi[:, c:c + 2, :], src("pooled", g, c).rearrange("p (a b) -> p a b", a=2), ACT.Copy).then_inc(
                        *did("scalar", ("phi", g, c)))

            def y_hi(g):
                for e in range(4):
                    act.wait_ge(*after("ymul", g * 4 + e))
                    copy(yhi[:, g * 4 + e, :], sgate[:, g * 4 + e, :], ACT.Copy).then_inc(
                        *did("scalar", ("yhi", g * 4 + e)))

            for g in range(4):
                u_copy(g)
                if g == 1:
                    pooled_hi(0)
                if g:
                    split_to(("grp", g - 1))
                    y_hi(g - 1)
                    pooled_hi(g)
            split_to(("grp", 3))
            y_hi(3)
            act.wait_ge(*after("y", 15))
            act.wait_ge(*after("mixed", 3, 3))
            for r, name in enumerate(("ln_g", "ln_b")):
                act.dma_start(lnrow[:, r, :], rows_to_all(T[name], 0, D)).then_inc(loads["lna"], 16)
            act.dma_start(dist[:, :, :], T["t_dist"].rearrange("p (g t) -> p g t", g=NG)).then_inc(loads["dist"], 16)
            for n in range(2):
                for kh in range(2):
                    split_to(("outa", n, kh))

            def root(out_, in_, n, e, *label):
                copy(out_, in_, ACT.Sqrt, scale=1.0 / n, bias=eps[:, e:e + 1]).then_inc(*did("scalar", label))

            for t in range(XT):
                split_mods(("k", 0, 0), t)
                act.wait_ge(*after("var", 0, t))
                root(rstd[:, t:t + 1], mv[:, t, 1:2], 1, 1, "root", "ln", 0, t)
            for m in MODS[("k", 0, 0)]:
                save_mod(*m)
            split_features("f1", 2, (-1, 0))

            def exps(i, it):
                kind, l, h, t = it
                parts, kt, _ = item_info(it)
                e = e1 if kind == "first" else EE[l]
                act.wait_ge(*after("max", it))
                if kind in "AB":
                    if i >= 3:
                        act.wait_ge(*after("t", items[i - 3], 0))
                    for j, n in parts:
                        labels = [("read", "s", it, j)]
                        if j == len(parts) - 1:
                            labels.append(("exp", it))
                            if kind == "A":
                                labels.append(("probs", it))
                        copy(e[:, i % 3, j * 512:j * 512 + n], src("s", it, j)[:, 0:n], ACT.Exp,
                             bias=nmax[:, i % ITEMS_KEPT, j:j + 1], accum_out=rsum[:, i % ITEMS_KEPT, j:j + 1]).then_inc(*did("scalar", *labels))
                    return
                n = kt * P
                if kind == "C":
                    copy(esink[:, i % ITEMS_KEPT:i % ITEMS_KEPT + 1], sinkr[:, h:h + 1], ACT.Exp, bias=nmax[:, i % ITEMS_KEPT, 0:1]).then_inc(
                        *did("scalar", ("esink", it)))
                copy(e[:, i % 3, 0:n], e[:, i % 3, 0:n], ACT.Exp, bias=nmax[:, i % ITEMS_KEPT, 0:1],
                     accum_out=rsum[:, i % ITEMS_KEPT, 0:1]).then_inc(*did("scalar", ("exp", it), ("probs", it)))

            def prob_copy(i, it):
                _, kt, _ = item_info(it)
                p = p1 if it[0] == "first" else PP[it[1]]
                for b in range(0, kt, 4):
                    n = min(kt - b, 4) * P
                    act.wait_ge(*after("t", it, b))
                    if i >= 2:
                        act.wait_ge(*after("o", items[i - 2]))
                    copy(p[:, i % 2, b * P:b * P + n], src("t", it, b)[:, 0:n], ACT.Copy).then_inc(
                        *did("scalar", ("pT", it, b), ("read", "t", it, b)))

            def projected_last(what, n):
                act.wait_ge(*after(what, 1, 1, n))
                dst = {"q2": qT_b[:, n, S:2 * S], "k2": kT_b[:, 2 + n, :], "v2": vv_b[:, n, P:P + NW]}[what]
                labels = [("vv", 1, 1, n)] if what == "v2" else [(what[0] + "T", 1, 1, t) for t in range(4)] if n == 3 else []
                copy(dst, src(what, 1, 1, n)[:, 0:S if what == "q2" else NW], ACT.Copy,
                     scale=QSCALE if what == "q2" else 1.0).then_inc(*did("scalar", ("read", what, 1, 1, n), *labels))

            def projected(what, qr, g, n):
                if what in ("q2", "k2", "v2"):
                    projected_last(what, n)
                    return
                act.wait_ge(*after(what, qr, g, n))
                dst = {"k": kT1[:, qr % 2, g * 2 + n, :], "q": qT1[:, qr % 2, g * 2 + n, :], "v": v1[:, qr % 2, n, g, :]}[what]
                copy(dst, src(what, qr, g, n)[:, 0:QW], ACT.Copy, scale=QSCALE if what == "q" else 1.0).then_inc(
                    *did("scalar", (what + "1", qr, g, n), ("read", what, qr, g, n)))

            def load_bias(n):
                if n == 0:
                    act.wait_ge(*after(("n1", 1), 7))
                    act.dma_start(colmask, T["t_cols"]).then_inc(loads["bias"], 16)
                    return
                h0, r = (n - 1) // 4 * 4, (n - 1) % 4
                rows = bass.AP(tensor=T["rpb_rows"].tensor,
                               offset=T["rpb_rows"].offset + (r * 8 + h0) * 4 * GRID * P + GRID - 1,
                               ap=[[P - 1, GRID], [GRID * P, 16], [1, GRID]])
                b = (hc[:, r // 2, :] if h0 else mix[:, XT + r // 2, :])[r % 2 * GRID:(r % 2 + 1) * GRID, :]
                act.dma_start(b.rearrange("p (a b) -> p a b", b=GRID), rows).then_inc(loads["bias"], 16)

            def pair_squares(t):
                act.wait_ge(*after("pairs", t))
                for h in range(4):
                    copy(subtmp[:, h * P:(h + 1) * P], mix[:, t, NW + h * P:NW + (h + 1) * P], ACT.Square,
                         accum_out=hss[:, 0, h:h + 1]).then_inc(*did("scalar", *([("pair squares", t)] if h == 3 else [])))

            def attend(items, mods, steps=()):
                for i in range(len(items) + 4):
                    if items[0][0] == "B" and 0 <= i - 2 < len(items):
                        prob_copy(i - 2, items[i - 2])
                    if i < len(items):
                        exps(i, items[i])
                    for m in mods_at(i, items, mods):
                        split_to(("mod",) + m)
                    for at, step in steps:
                        if at == i and first_of_unit(step):
                            split_to(first_of_unit(step))
                        if at == i and step[0] == "bias":
                            load_bias(step[1])
                        elif at == i and step[0] != "mod":
                            projected(*step)
                    if items[0][0] != "B" and 0 <= i - 2 < len(items):
                        prob_copy(i - 2, items[i - 2])
                    if 0 <= i - 4 < len(items) and items[i - 4][0] == "B" and items[i - 4][2] == 3:
                        pair_squares(items[i - 4][3])
                    for m in mods_at(i - 2, items, mods):
                        save_mod(*m)
                    for at, step in steps:
                        if at == i - 1 and step[0] == "mod":
                            save_mod(*step[1:])

            def load_mods(l, r):
                for q in range(4):
                    act.wait_ge(loads[f"modsave{q}"], 16 * (3 * l + (3 if r else 1)))
                if l or r:
                    act.wait_ge(*after("modT", *((l, 0) if r else (l - 1, 1))))
                n = 16 * (r + 1)
                for vec in range(4):
                    rows = modd[l, vec, (4 * NW if r else 0):(12 if r else 4) * NW].rearrange("(r p) -> r p", p=P)
                    act.dma_start(modc[vec * n:(vec + 1) * n, :], rows).then_inc(loads[f"modc{l}{r}"], 16)

            def save_gates(l):
                act.wait_ge(*after("growc", l))
                act.dma_start(gated[l].rearrange("v (r p) -> (v r) p", p=P), grow[:, :]).then_inc(loads["gsave"], 16)

            def load_gates(l, which):
                act.wait_ge(loads["gsave"], 16 * (l + 1))
                for v in range(2 - l):
                    act.dma_start(gates[:, v, :], rows_to_all(gated, (l * 4 + which * 2 + v) * D, D)).then_inc(
                        loads[f"g{l}{which}"], 16)

            for what in "kqv":
                for g in range(NG):
                    split_to((what, 0, g))
                    for n in range(2):
                        projected(what, 0, g, n)
            for n in range(2):
                split_to(("gb", n))
                for t in range(XT):
                    act.wait_ge(*after("gb", n, t))
                    copy(gb[:, t, n * NW:(n + 1) * NW], src("gb", n, t), ACT.Silu).then_inc(
                        *did("scalar", ("gbs", n, t), ("read", "gb", n, t)))
            act.wait_ge(*after("h1", 1))
            for r, name in enumerate(("ln_g", "ln_b")):
                act.dma_start(lnrow[:, r, :], rows_to_all(T[name], D, D)).then_inc(loads["lnb"], 16)
            items = items_first()
            attend(items, [], side_steps())
            load_mods(0, 0)
            act.dma_start(hc[:, :, :], T["ctx_2"].rearrange("a (t p) d -> p (a t) d", p=P)).then_inc(loads["ctx"], 16)
            split_features("fo1", 2)
            for n in range(2):
                split_to(("outb", n))

            def squares(label, t):
                copy(mix[:, t, :], H(t), ACT.Square, accum_out=sumsq[:, t:t + 1]).then_inc(*did("scalar", label))

            def half_square(l, which, t, n):
                if (t, n) != (0, 0):
                    act.wait_ge(counts.sems["scalar"], counts.now["scalar"])
                if which == 0:
                    act.wait_ge(*after("out2", l, n, t))
                    got = src("out2", l, n, t)
                elif l == 0:
                    act.wait_ge(*after("summed", t, n))
                    got = mix[:, t, n * NW:(n + 1) * NW]
                else:
                    act.wait_ge(*after("acc", t, n))
                    got = src("acc", t, n)
                copy(htmp[:, n, :], got, ACT.Square, accum_out=sumh[:, t, n:n + 1]).then_inc(
                    *did("scalar", ("sqh", l, which, t, n)))

            def mixer_root(l, which, group):
                t, n = group[0], len(group)
                act.wait_ge(*after("sumh", l, which, group))
                root(rstd[:, 4 + t:4 + t + n], sumh[:, t:t + n, 0], D, 0, "mixer root", l, which, group)

            def stream_root(l, which, group):
                if which or l:
                    act.wait_ge(*after("resid", *((l, 0) if which else (0, 1)), group))
                for t in group:
                    squares(("sq", l, which, t), t)
                act.wait_ge(counts.sems["scalar"], counts.now["scalar"])
                t, n = group[0], len(group)
                root(rstd[:, t:t + n], sumsq[:, t:t + n], D, 0, "stream root", l, which, group)

            split_mods(("q2", 0, 0), 0)
            for t in range(XT):
                act.wait_ge(*after("var", 1, t))
                root(rstd[:, t:t + 1], mv[:, t, 1:2], 1, 1, "root", "ln", 1, t)

            def values_copy(l, tiles):
                split_to(("v2", l, 1))
                for t in tiles:
                    act.wait_ge(*after("v2", l, 1, t))
                    copy(VV[l][:, t, :], src("v2", l, 1, t), ACT.Copy).then_inc(
                        *did("scalar", ("vv", l, 1, t), ("read", "v2", l, 1, t)))

            for l in range(2):
                nt = 4 if l == 0 else 2
                groups = GROUPS[l]
                if l == 0:
                    for i, group in enumerate(STREAM_GROUPS):
                        if i == 0:
                            act.wait_ge(loads["ctx"], 16)
                        else:
                            for t in group:
                                act.wait_ge(*after("ln", 1, t))
                        stream_root(0, 0, group)
                        split_mods(("q2", 0, 0), i + 1)
                    act.wait_ge(*after("ln", 1, 1))
                    act.dma_start(rope[:, :, :, :], T["t_rope"].rearrange("p (a t d) -> p a t d", a=2, t=2)).then_inc(
                        loads["ropes"], 16)
                    act.dma_start(qkg[:, :, :], rows_to_all(T["qk_norm_a_2"], 0, 2 * DH)).then_inc(loads["ropes"], 16)
                    act.dma_start(sublng[:, :], rows_to_all(T["diff_subln_2"], 0, P)).then_inc(loads["ropes"], 16)
                    act.dma_start(lamrow[:, :, :], rows_to_all(T["diff_lambda_2"], 0, 4 * DH)).then_inc(loads["ropes"], 16)
                for m in MODS[("q2", l, 0)]:
                    save_mod(*m)
                split_features(("n1", l), 4, (l, 0))
                load_mods(l, 1)
                if l == 0:
                    act.wait_ge(*after("lam sums"))
                    copy(lam[:, 0:2], lam[:, 0:2], ACT.Exp).then_inc(*did("scalar", ("lam exp",)))
                for part in range(2 - l):
                    sets = (("q", range(nt)), ("k", range(4)))
                    for what, tiles in sets:
                        small = what == "k" and part == 0
                        split_to((what + "2", l, part))
                        w = P if small else NW
                        for t in tiles:
                            key = (what, l, part, t)
                            a = src(what + "2", l, part, t)
                            act.wait_ge(*after(what + "2", l, part, t))
                            if small:
                                copy(VV[l][:, t, 0:P], a[:, P:2 * P], ACT.Copy).then_inc(*did("scalar", ("vv", l, part, t)))
                            if part == 1 and what == "q" and t == 3:
                                split_to(("k2", l, part))
                            normed = l == 0 and part == 0
                            if (normed or (t >= XT and not small)) and STAGE_BEFORE[key]:
                                act.wait_ge(*after(*STAGE_BEFORE[key]))
                            if normed:
                                copy(EE[l][:, STAGE[key], 512:512 + w], a[:, 0:w], ACT.Square).then_inc(
                                    *did("scalar", ("squared",) + key))
                            elif t >= XT and not small:
                                copy(EE[l][:, STAGE[key], 0:w], a[:, 0:w], ACT.Copy).then_inc(
                                    *did("scalar", ("staged",) + key, ("read", what + "2", l, part, t)))
                    split_mods(("turn", l, part), 0)
                    if part == 1:
                        values_copy(l, range(2))
                    for what, tiles in sets:
                        n = 2 if what == "k" and part == 0 else 4
                        dst = (QT if what == "q" else KT)[l]
                        for t in tiles:
                            act.wait_ge(*after(what + "turn", l, part, t))
                            copy(dst[:, 0:n, t * P:t * P + P],
                                 src(what + "turn", l, part, t)[:, 0:n * P].rearrange("p (a b) -> p a b", a=n),
                                 ACT.Copy, scale=QSCALE if what == "q" else 1.0).then_inc(
                                *did("scalar", (what + "T", l, part, t), ("read", what + "turn", l, part, t)))
                    for m in MODS.get(("turn", l, part), []):
                        save_mod(*m)
                    if l == 0 and part == 0:
                        save_gates(0)
                    if l == 0 and part == 1:
                        values_copy(l, range(2, 4))
                    items = items_second(l, part)
                    if l == 1:
                        act.wait_ge(loads["odd"], 48)
                        save_gates(1)
                    attend(items, mods_second(l, part), side_steps_last() if l else ())
                for m in MODS.get(("fo", l), []):
                    split_to(("mod",) + m)
                    save_mod(*m)
                for t in range(nt):
                    act.wait_ge(*after("mixed out", l, t))
                split_features(("fo", l), nt)
                load_gates(l, 0)
                for n in range(2):
                    split_to(("out2", l, n))
                    if n == 0:
                        for t in range(nt):
                            half_square(l, 0, t, 0)
                for i in range(4):
                    if i < 2:
                        for t in groups[i]:
                            half_square(l, 0, t, 1)
                    if 0 <= i - 1 < 2:
                        mixer_root(l, 0, groups[i - 1])
                    if 0 <= i - 2 < 2:
                        stream_root(l, 1, groups[i - 2])
                    if i != 1 and i != 2:
                        split_mods(("in", l, 0), i and 1)
                for m in MODS.get(("in", l, 0), []):
                    save_mod(*m)
                load_gates(l, 1)
                if l == 0:
                    load_mods(1, 0)
                split_features(("n2", l), nt, (l, 1))
                for j in range(9):
                    if j < 8:
                        split_to(("in", l, j))
                        for e in range(4):
                            act.wait_ge(*after("in", l, j, e))
                            n = j * 4 + e
                            if n >= 2:
                                act.wait_ge(*after("hidden", l, (n - 2) // 4, (n - 2) % 4))
                            copy(htmp[:, e % 2, 0:nt * P], src("in", l, j, e)[:, 0:nt * P], ACT.Relu).then_inc(
                                *did("scalar", ("relu", l, j, e), ("read", "in", l, j, e)))
                            act.wait_ge(*after("squared", l, j, e))
                            if j >= 2:
                                act.wait_ge(*after("used", UNIT[("out", l, j - 2)].n))
                            copy(hhi[:, j % 2, e, 0:nt * P], htmp[:, e % 2, 0:nt * P], ACT.Copy).then_inc(
                                *did("scalar", ("hhi", l, j, e)))
                    if j:
                        split_to(("out", l, j - 1))
                for t in range(nt):
                    half_square(l, 1, t, 0)
                for i in range(4):
                    if i < 2:
                        for t in groups[i]:
                            half_square(l, 1, t, 1)
                    if 0 <= i - 1 < 2:
                        mixer_root(l, 1, groups[i - 1])
                    if l == 0 and 0 <= i - 2 < 2:
                        stream_root(1, 0, groups[i - 2])
                    if l == 0 and i >= 2:
                        split_mods(("q2", 1, 0), i - 2)
                if l == 0:
                    act.wait_ge(*after("resid", 0, 1, (2, 3)))
                    act.dma_start(rope_b[:, :, :, :], T["t_rope"].rearrange("p (a t d) -> p a t d", a=2, t=2)).then_inc(
                        loads["odd"], 16)
                    act.dma_start(sinkr[:, :], rows_to_all(T["sink_c_2"], 0, 8)).then_inc(loads["odd"], 16)
                    act.dma_start(band[:, :, :], T["t_band"].rearrange("p (a b) -> p a b", a=2)).then_inc(loads["odd"], 16)

        @block.vector
        def _(dve):
            v = nc.vector
            st = [0]

            def split_to(name, ahead=1):
                split_lo(dve, v, last_split(name, ahead), st, False)

            def link(ins, *labels):
                ins.then_inc(*did("vector", *labels))
                dve.wait_ge(counts.sems["vector"], counts.now["vector"])

            def split_mods(name, i):
                if i < len(MODS.get(name, [])):
                    split_to(("mod",) + MODS[name][i])

            def src(*label):
                return ps[:, counts.bank(*label), :]

            def low_features(name, nt):
                per = 4 // nt
                for j in range(KD // per):
                    dve.wait_ge(*after("fhi", name, j))
                    dst = flo[:, j * per:(j + 1) * per, 0:nt * P]
                    hi = fhi[:, j * per:(j + 1) * per, 0:nt * P].bitcast(F32)
                    v.tensor_tensor(dst, src(name, j).rearrange("p (a b) -> p a b", a=per), hi, ALU.subtract).then_inc(
                        *did("vector", ("split", name, j), ("read", name, j)))

            def modulate(name, nt, l, which, A=None, B=None):
                per = 4 // nt
                for j in range(KD // per):
                    dve.wait_ge(*after(name, j))
                    if j >= 2:
                        dve.wait_ge(*after("split", name, j - 2))
                    for q in range(2):
                        k, vec = (j, q) if nt == 4 else (2 * j + q, 0)
                        factor = A[:, k:k + 1] if A is not None else modA[:, l, which, vec, k:k + 1]
                        shift = B[:, k:k + 1] if B is not None else modB[:, l, which, vec, k:k + 1]
                        ins = v.tensor_scalar(ftmp(l, which, j)[:, q * S:(q + 1) * S], src(name, j)[:, q * S:(q + 1) * S],
                                              factor, shift, ALU.mult, ALU.add)
                    ins.then_inc(*did("vector", ("modulated", name, j), ("read", name, j)))

            def rsqrt(out_, in_, n, e):
                w = out_.shape[-1]
                x, t = newton[:, 0, 0:w], newton[:, 1, 0:w]
                link(v.tensor_scalar(x, in_, 1.0 / n, e, ALU.mult, ALU.add))
                link(v.tensor_scalar(out_.bitcast(I32), x.bitcast(I32), -0.5, RSQRT_START, ALU.mult, ALU.add))
                for _ in range(NEWTON_STEPS):
                    link(v.tensor_tensor(t, out_, out_, ALU.mult))
                    link(v.scalar_tensor_tensor(out=t, in0=t, scalar=-0.5, in1=x, op0=ALU.mult, op1=ALU.mult))
                    link(v.scalar_tensor_tensor(out=out_, in0=t, scalar=1.5, in1=out_, op0=ALU.add, op1=ALU.mult))

            def deviation(col, in_, n, e):
                link(v.tensor_scalar(dev[:, col:col + in_.shape[-1]], in_, 1.0 / n, e, ALU.mult, ALU.add))

            def refined(col, w=1):
                y, x, t = rstd[:, col:col + w], dev[:, col:col + w], newton[:, 0, 0:w]
                link(v.reciprocal(y, y))
                link(v.tensor_tensor(t, y, y, ALU.mult))
                link(v.scalar_tensor_tensor(out=t, in0=t, scalar=-0.5, in1=x, op0=ALU.mult, op1=ALU.mult))
                link(v.scalar_tensor_tensor(out=y, in0=t, scalar=1.5, in1=y, op0=ALU.add, op1=ALU.mult))

            v.memset(eps[:, 0:1], EPS).then_inc(*did("vector"))
            v.memset(eps[:, 1:2], LN_EPS).then_inc(*did("vector"))

            dve.wait_ge(*after("cond high"))
            v.tensor_tensor(condp[:, :, 2:4], cond[:, :, :], condp[:, :, 0:2].bitcast(F32), ALU.subtract).then_inc(
                *did("vector", ("cond",)))
            low_features("fx", 2)
            split_lo(dve, v, 3, st, False)
            for g in range(4):
                split_to(("gate", g))

            def pooled_lo(g):
                for c in range(0, 4, 2):
                    dve.wait_ge(*after("phi", g, c))
                    v.tensor_tensor(plo[:, c:c + 2, :], src("pooled", g, c).rearrange("p (a b) -> p a b", a=2),
                                    phi[:, c:c + 2, :].bitcast(F32), ALU.subtract).then_inc(
                        *did("vector", ("pooled split", g, c), ("read", "pooled", g, c)))

            def gate_mixed(g):
                for e in range(4):
                    i = g * 4 + e
                    dve.wait_ge(*after("mixed", g, e))
                    dve.wait_ge(*after("sgate", i))
                    v.scalar_tensor_tensor(out=sgate[:, i, :], in0=src("mixed", g, e)[:, 0:S], scalar=scol[:, i:i + 1],
                                           in1=sgate[:, i, :], op0=ALU.mult, op1=ALU.mult).then_inc(
                        *did("vector", ("ymul", i), ("read", "mixed", g, e)))
                for e in range(4):
                    i = g * 4 + e
                    dve.wait_ge(*after("yhi", i))
                    v.tensor_tensor(ylo[:, i, :], sgate[:, i, :], yhi[:, i, :].bitcast(F32), ALU.subtract).then_inc(
                        *did("vector", ("y", i)))

            dve.wait_ge(loads["scol"], 16)
            for g in range(4):
                split_to(("u", g))
                if g == 1:
                    pooled_lo(0)
                if g:
                    split_to(("grp", g - 1))
                    gate_mixed(g - 1)
                    pooled_lo(g)
            split_to(("grp", 3))
            gate_mixed(3)

            def add_residual(name, n, t):
                dve.wait_ge(*after(name, n, t))
                hh = hx[:, t, n * NW:(n + 1) * NW]
                v.scalar_tensor_tensor(out=hh, in0=hh, scalar=ALPHA, in1=src(name, n, t), op0=ALU.mult, op1=ALU.add).then_inc(
                    *did("vector", ("read", name, n, t)))

            def layer_norm(i, name):
                for t in range(XT):
                    for n in range(2):
                        dve.wait_ge(*after("read", name, n, t))
                        link(v.bn_stats(stats[:, t, n, :], hx[:, t, n * NW:(n + 1) * NW]))
                    link(v.bn_aggr(mv[:, t, :], stats[:, t, :, :].rearrange("p a b -> p (a b)")), ("var", i, t))
                    deviation(t, mv[:, t, 1:2], 1, LN_EPS)
                before = ("q2", 0, 0) if i else ("k", 0, 0)
                split_mods(before, 0)
                for t in range(XT):
                    if i == 0:
                        split_mods(before, t + 1)
                    dve.wait_ge(*after("root", "ln", i, t))
                    refined(t)
                    h = hx[:, t, :]
                    labels = [("ln", i, t)] if i == 0 else [("centred", t)]
                    link(v.tensor_scalar(h, h, mv[:, t, 0:1], rstd[:, t:t + 1], ALU.subtract, ALU.mult), *labels)

            def mod_row(l, j):
                dve.wait_ge(*after("mod", l, j))
                if l or j > 3:
                    dve.wait_ge(loads[f"modsave{j % 4}"], 16 * (3 * l + j // 4))
                q = j % 4 * 32
                v.tensor_copy(modrow[q:q + 4, :], src("mod", l, j)[0:4, :]).then_inc(*did("vector", ("read", "mod", l, j)))

            for n in range(2):
                for kh in range(2):
                    split_to(("outa", n, kh))
                for t in range(XT):
                    add_residual("outa", n, t)
            layer_norm(0, "outa")
            split_mods(("k", 0, 0), 1)
            for m in MODS[("k", 0, 0)]:
                mod_row(*m)
            dve.wait_ge(loads["lncol"], 16)
            modulate("f1", 2, -1, 0, lncol[:, 0, :], lncol[:, 1, :])

            def maxima(i, it):
                kind, l, h, t = it
                parts, kt, _ = item_info(it)
                dve.wait_ge(*after("s", it))
                if kind in "AB":
                    for j, n in parts:
                        ins = v.reduce_max(nmax[:, i % ITEMS_KEPT, j:j + 1], src("s", it, j)[:, 0:n], AX_X, negate=True)
                    ins.then_inc(*did("vector", ("max", it)))
                    return
                if i >= 3:
                    _, kb, _ = item_info(items[i - 3])
                    dve.wait_ge(*after("t", items[i - 3], (kb - 1) // 4 * 4))
                e = (e1 if kind == "first" else EE[l])[:, i % 3, :]
                if kind == "first":
                    n = parts[0][1]
                    for g in range(NG):
                        bank = 0 if not t or g < 2 else 1
                        a = src("s", it, bank)[:, (0 if bank else g * n):(0 if bank else g * n) + n]
                        labels = []
                        if (t and g >= 1) or g == 2:
                            labels.append(("read", "s", it, bank))
                        ins = v.scalar_tensor_tensor(out=e[:, g * n:(g + 1) * n], in0=dist[:, g, 256 - n:256],
                                                     scalar=-SLOPES[g][l * 4 + h], in1=a, op0=ALU.mult, op1=ALU.add)
                        if labels and g < 2:
                            ins.then_inc(*did("vector", *labels))
                    link(ins, *labels)
                else:
                    if it == ("D", 1, 0, 0):
                        dve.wait_ge(*after("bias"))
                    a = src("s", it, 0)
                    v.tensor_tensor(e[:, 0:S], a[:, 0:S], band[:, t, :] if kind == "C" else bias_d(h, t), ALU.add).then_inc(
                        *did("vector", ("biased", it)))
                    link(v.tensor_copy(e[:, S:2 * S], a[:, S:2 * S]), ("read", "s", it, 0))
                ins = v.reduce_max(nmax[:, i % ITEMS_KEPT, 0:1], e[:, 0:kt * P], AX_X, negate=True)
                if kind == "C":
                    link(ins)
                    ins = v.tensor_tensor(nmax[:, i % ITEMS_KEPT, 0:1], nmax[:, i % ITEMS_KEPT, 0:1], nsink[:, h:h + 1], ALU.min)
                ins.then_inc(*did("vector", ("max", it)))

            def combine(i, it):
                _, kt, _ = item_info(it)
                n = kt * P
                e = EE[0][:, i % 3, :]
                inv, total = rinv[:, i % ITEMS_KEPT, :], rsum[:, i % ITEMS_KEPT, :]
                dve.wait_ge(*after("exp", it))
                link(v.reciprocal(inv, total))
                link(v.scalar_tensor_tensor(out=inv[:, 1:2], in0=inv[:, 1:2], scalar=lam[:, 3:4], in1=total[:, 0:1],
                                            op0=ALU.mult, op1=ALU.mult))
                v.scalar_tensor_tensor(out=e[:, 0:n], in0=e[:, 512:512 + n], scalar=inv[:, 1:2], in1=e[:, 0:n],
                                       op0=ALU.mult, op1=ALU.add).then_inc(*did("vector", ("probs", it)))

            def outputs(i, it):
                kind, l, h, t = it
                dve.wait_ge(*after("o", it))
                if kind != "B":
                    dve.wait_ge(*after("exp", it))
                    if kind == "C":
                        link(v.tensor_tensor(rsum[:, i % ITEMS_KEPT, 0:1], rsum[:, i % ITEMS_KEPT, 0:1], esink[:, i % ITEMS_KEPT:i % ITEMS_KEPT + 1], ALU.add))
                    link(v.reciprocal(rinv[:, i % ITEMS_KEPT, 0:1], rsum[:, i % ITEMS_KEPT, 0:1]))
                if kind == "first":
                    g = gb[:, t, (l * 4 + h) * DH:(l * 4 + h + 1) * DH]
                    dve.wait_ge(*after("gbs", l // 2, t))
                    v.scalar_tensor_tensor(out=g, in0=src("o", it)[:, 0:DH], scalar=rinv[:, i % ITEMS_KEPT, 0:1], in1=g,
                                           op0=ALU.mult, op1=ALU.mult).then_inc(*did("vector", ("gated", it), ("read", "o", it)))
                elif kind == "B":
                    v.tensor_scalar(mix[:, t, NW + h * P:NW + (h + 1) * P], src("o", it)[:, 0:P],
                                    rinv[:, i % ITEMS_KEPT, 0:1], None, ALU.mult).then_inc(
                        *did("vector", ("read", "o", it), *([("pairs", t)] if h == 3 else [])))
                else:
                    at = (NW if kind == "D" else 0) + h * DH
                    v.tensor_scalar(mix[:, t, at:at + DH], src("o", it)[:, 0:DH], rinv[:, i % ITEMS_KEPT, 0:1], None, ALU.mult).then_inc(
                        *did("vector", ("read", "o", it), *([("mixed out", 1, t)] if kind == "D" and h == 7 else [])))

            def pair_norm(t):
                m = mix[:, t, NW:2 * NW].rearrange("p (h d) -> p h d", d=P)
                dve.wait_ge(*after("pair squares", t))
                rsqrt(hrs[:, 0, 0:4], hss[:, 0, 0:4], P, EPS)
                link(v.tensor_tensor(m, m, heads_view(hrs[:, 0, 0:4], (1, 4), (0, P)), ALU.mult))
                link(v.tensor_tensor(m, m, heads_view(sublng[:, :], (0, 4), (1, P)), ALU.mult), ("mixed out", 0, t))

            def attend(items, mods, steps=()):
                for i in range(len(items) + 5):
                    if i < len(items):
                        maxima(i, items[i])
                    for at, step in steps:
                        if at == i and first_of_unit(step):
                            split_to(first_of_unit(step))
                        if at == i and step[0] == "mod":
                            mod_row(*step[1:])
                    for m in mods_at(i - 1, items, mods):
                        split_to(("mod",) + m)
                        mod_row(*m)
                    if items[0][0] == "B" and 0 <= i - 1 < len(items):
                        combine(i - 1, items[i - 1])
                    if 0 <= i - 4 < len(items):
                        outputs(i - 4, items[i - 4])
                    if 0 <= i - 5 < len(items) and items[i - 5][0] == "B" and items[i - 5][2] == 3:
                        pair_norm(items[i - 5][3])

            def mod_columns(l, r):
                n = 16 * (r + 1)
                dve.wait_ge(*after("modT", l, r))
                dve.wait_ge(loads["modb"], 16)
                dve.wait_ge(loads["normc"], 16)
                parts = src("modT", l, r)[:, 0:4 * n].rearrange("p (x a b) -> p x a b", x=2, a=2)
                link(v.tensor_tensor(modT[:, :, 0:n], parts[:, 0], heads_view(modb[:, l, 16 * r:], (0, 2), (1, n)), ALU.add))
                link(v.tensor_tensor(modT[:, :, 0:n], parts[:, 1], modT[:, :, 0:n], ALU.add), ("read", "modT", l, r))
                at = 8 * r
                gain = heads_view(normc[:, l, 2 * r, :], (0, 2), (1, KD))
                v.tensor_copy(modB[:, l, r, :, :], modT[:, :, at:at + KD]).then_inc(*did("vector"))
                link(v.scalar_tensor_tensor(out=modA[:, l, r, :, :], in0=modT[:, :, at + KD:at + 2 * KD], scalar=1.0,
                                            in1=gain, op0=ALU.add, op1=ALU.mult))
                if r:
                    for which in range(2):
                        gain = heads_view(normc[:, l, 2 * which + 1, :], (0, 2), (1, KD))
                        ins = v.tensor_tensor(gcol[:, which, :, :], modT[:, :, 24 * which:24 * which + KD], gain, ALU.mult)
                        ins.then_inc(*did("vector", *([("gcol", l)] if which else [])))

            def gate_rows(l):
                dve.wait_ge(*after("grow", l))
                if l:
                    dve.wait_ge(loads["gsave"], 16 * l)
                v.tensor_copy(grow[:, :], src("grow", l)[0:32, 0:P]).then_inc(*did("vector", ("growc", l), ("read", "grow", l)))

            dve.wait_ge(loads["dist"], 16)
            for what in "kqv":
                for g in range(NG):
                    split_to((what, 0, g))
            for n in range(2):
                split_to(("gb", n))
            items = items_first()
            attend(items, [], side_steps())
            low_features("fo1", 2)
            for n in range(2):
                split_to(("outb", n))
                for t in range(XT):
                    if n == 0:
                        dve.wait_ge(*after("h1", t))
                    add_residual("outb", n, t)
            layer_norm(1, "outb")
            dve.wait_ge(loads["lnb"], 32)
            link(v.tensor_tensor(hx[:, 0, :], hx[:, 0, :], lnrow[:, 0, :], ALU.mult))
            link(v.tensor_tensor(hx[:, 0, :], hx[:, 0, :], lnrow[:, 1, :], ALU.add), ("ln", 1, 0))

            def normed(l, which, group):
                t, n = group[0], len(group)
                dve.wait_ge(*after("sq", l, which, group[-1]))
                deviation(t, sumsq[:, t:t + n], D, EPS)
                dve.wait_ge(*after("stream root", l, which, group))
                refined(t, n)
                for t in group:
                    v.tensor_scalar(mix[:, t, :], H(t), rstd[:, t:t + 1], None, ALU.mult).then_inc(
                        *did("vector", ("xn", l, which, t)))

            def gated_half(l, which, t, n):
                vec = 0 if t < XT else 1
                if (t, n) == (0, 0):
                    dve.wait_ge(loads[f"g{l}{which}"], 16 * (2 - l))
                dve.wait_ge(*after("sqh", l, which, t, n))
                key = ("out2", l, n, t) if which == 0 else ("acc", t, n)
                v.tensor_tensor(mix[:, t, n * NW:(n + 1) * NW], src(*key), gates[:, vec, n * NW:(n + 1) * NW], ALU.mult).then_inc(
                    *did("vector", ("read",) + key, ("gated half", l, which, t, n)))

            def sum_halves(l, which, group):
                t, n = group[0], len(group)
                dve.wait_ge(*after("sqh", l, which, group[-1], 1))
                link(v.tensor_tensor(sumh[:, t:t + n, 0], sumh[:, t:t + n, 0], sumh[:, t:t + n, 1], ALU.add),
                     ("sumh", l, which, group))
                deviation(4 + t, sumh[:, t:t + n, 0], D, EPS)

            def residual(l, which, group):
                dve.wait_ge(*after("mixer root", l, which, group))
                refined(4 + group[0], len(group))
                for t in group:
                    for n in range(2):
                        dve.wait_ge(*after("gated half", l, which, t, n))
                    labels = [("resid", l, which, group)] if t == group[-1] else []
                    if l and which:
                        labels.append(("final", t))
                    v.scalar_tensor_tensor(out=H(t), in0=mix[:, t, :], scalar=rstd[:, 4 + t:5 + t], in1=H(t),
                                           op0=ALU.mult, op1=ALU.add).then_inc(*did("vector", *labels))
                dve.wait_ge(counts.sems["vector"], counts.now["vector"])

            def stage(what, l, part, t):
                key = (what, l, part, t)
                small = what == "k" and part == 0
                norm = l == 0 and part == 0
                if t >= XT and not norm and not small:
                    return
                w = P if small else NW
                nh = w // DH
                r = STAGE[key]
                a = src(what + "2", l, part, t)
                e = EE[l][:, r, :]
                i = 0 if what == "q" else 1
                dve.wait_ge(*after(what + "2", l, part, t))
                if STAGE_BEFORE[key]:
                    dve.wait_ge(*after(*STAGE_BEFORE[key]))
                if norm:
                    dve.wait_ge(*after("squared", *key))
                    link(v.reduce_sum(hss[:, r, 0:nh], e[:, 512:512 + w].rearrange("p (h d) -> p h d", d=DH), AX_X))
                    rsqrt(hrs[:, r, 0:nh], hss[:, r, 0:nh], DH, EPS)
                elif small:
                    dve.wait_ge(*after("vv", l, part, t))
                read = ("read", what + "2", l, part, t)
                heads = lambda ap: ap.rearrange("p (h d) -> p h d", d=DH)
                if t < XT:
                    cos = ropeg[:, i, 0, t, :] if norm else RO[l][:, 0, t, :]
                    sin = ropeg[:, i, 1, t, :] if norm else RO[l][:, 1, t, :]
                    v.tensor_tensor(heads(e[:, 512:512 + w]), heads(a[:, 0:w]), heads_view(cos, (0, nh), (1, DH)), ALU.mult).then_inc(
                        *did("vector"))
                    for half in range(2):
                        out_ = e[:, 0:w].rearrange("p (h x f d) -> p h x f d", x=2, f=2, d=16)[:, :, :, half, :]
                        in_ = a[:, 0:w].rearrange("p (h x f d) -> p h x f d", x=2, f=2, d=16)[:, :, :, 1 - half, :]
                        ins = v.tensor_tensor(out_, in_, heads_view(sin[:, half * 16:], (0, nh), (32, 2), (1, 16)), ALU.mult)
                        if half == 0:
                            ins.then_inc(*did("vector"))
                    link(ins, read)
                    if norm:
                        link(v.tensor_tensor(e[:, 0:w], e[:, 0:w], e[:, 512:512 + w], ALU.add))
                elif norm:
                    link(v.tensor_tensor(heads(e[:, 0:w]), heads(a[:, 0:w]), heads_view(qkg[:, i, :], (0, nh), (1, DH)), ALU.mult), read)
                if small:
                    dup = lambda ap: heads_view(ap, (DH, 2), (0, 2), (1, DH))
                    dst = e[:, 256:512].rearrange("p (h c d) -> p h c d", h=2, c=2)
                    if norm:
                        ins = v.tensor_tensor(dst, dup(e[:, 0:w]), heads_view(hrs[:, r, 0:2], (1, 2), (0, 2), (0, DH)), ALU.mult)
                    elif t < XT:
                        ins = v.tensor_tensor(dst, dup(e[:, 0:w]), dup(e[:, 512:512 + w]), ALU.add)
                    else:
                        v.tensor_copy(dst, dup(a[:, 0:w])).then_inc(*did("vector", ("staged",) + key, read))
                        return
                elif norm:
                    ins = v.tensor_tensor(heads(e[:, 0:w]), heads(e[:, 0:w]), heads_view(hrs[:, r, 0:nh], (1, nh), (0, DH)), ALU.mult)
                else:
                    ins = v.tensor_tensor(e[:, 0:w], e[:, 0:w], e[:, 512:512 + w], ALU.add)
                ins.then_inc(*did("vector", ("staged",) + key))

            for l in range(2):
                nt = 4 if l == 0 else 2
                groups = GROUPS[l]
                if l == 0:
                    for group in STREAM_GROUPS:
                        normed(0, 0, group)
                    split_mods(("q2", 0, 0), 1)
                mod_columns(l, 0)
                for m in MODS[("q2", l, 0)]:
                    mod_row(*m)
                if l == 0:
                    dve.wait_ge(loads["ropes"], 64)
                    for i in range(2):
                        v.tensor_tensor_reduce(lamrow[:, 2 * i, :], lamrow[:, 2 * i, :], lamrow[:, 2 * i + 1, :], 1.0, 0.0,
                                               ALU.mult, ALU.add, lam[:, i:i + 1]).then_inc(
                            *did("vector", *([("lam sums",)] if i else [])))
                modulate(("n1", l), 4, l, 0)
                if l == 0:
                    dve.wait_ge(*after("lam exp"))
                    link(v.tensor_tensor(lam[:, 2:3], lam[:, 1:2], lam[:, 0:1], ALU.subtract))
                    link(v.tensor_scalar(lam[:, 3:4], lam[:, 2:3], -LAM0, None, ALU.add))
                    link(v.tensor_scalar(sublng[:, :], sublng[:, :], 1.0 - LAM0, None, ALU.mult))
                    for i in range(2):
                        v.tensor_tensor(ropeg[:, i, 0, :, :], rope[:, 0, :, :], heads_view(qkg[:, i, :], (0, 2), (1, DH)),
                                        ALU.mult).then_inc(*did("vector"))
                        for half in range(2):
                            halves = lambda ap: ap.rearrange("p t (x f d) -> p t x f d", x=2, f=2)[:, :, :, half, :]
                            link(v.tensor_tensor(halves(ropeg[:, i, 1, :, :]), halves(rope[:, 1, :, :]),
                                                 heads_view(qkg[:, i, 16 * (1 - half):], (0, 2), (32, 2), (1, 16)), ALU.mult))
                else:
                    dve.wait_ge(loads["odd"], 48)
                    link(v.tensor_scalar(nsink[:, :], sinkr[:, :], -1.0, None, ALU.mult))
                for part in range(2 - l):
                    for what, tiles in (("q", range(nt)), ("k", range(4))):
                        split_to((what + "2", l, part))
                        for t in tiles:
                            stage(what, l, part, t)
                    for m in MODS.get(("turn", l, part), []):
                        split_to(("mod",) + m)
                        mod_row(*m)
                    if l == 0 and part == 0:
                        mod_columns(0, 1)
                        gate_rows(0)
                    if part == 1 and l == 0:
                        split_to(("v2", l, 1))
                    if l == 1:
                        mod_columns(1, 1)
                        gate_rows(1)
                    items = items_second(l, part)
                    attend(items, mods_second(l, part), side_steps_last() if l else ())
                for m in MODS.get(("fo", l), []):
                    split_to(("mod",) + m)
                    mod_row(*m)
                low_features(("fo", l), nt)
                for n in range(2):
                    split_to(("out2", l, n))
                    if n == 0:
                        for t in range(nt):
                            gated_half(l, 0, t, 0)
                for i in range(4):
                    if i < 2:
                        sum_halves(l, 0, groups[i])
                        for t in groups[i]:
                            gated_half(l, 0, t, 1)
                    if 0 <= i - 1 < 2:
                        residual(l, 0, groups[i - 1])
                    if 0 <= i - 2 < 2:
                        normed(l, 1, groups[i - 2])
                    if i == 3 and l == 0:
                        split_to(("mod",) + MODS["in", 0, 0][-1])
                for m in MODS.get(("in", l, 0), []):
                    mod_row(*m)
                modulate(("n2", l), nt, l, 1)
                for j in range(9):
                    if j < 8:
                        split_to(("in", l, j))
                        for e in range(4):
                            h = htmp[:, e % 2, 0:nt * P]
                            dve.wait_ge(*after("relu", l, j, e))
                            v.tensor_tensor(h, h, h, ALU.mult).then_inc(*did("vector", ("squared", l, j, e)))
                    if j:
                        split_to(("out", l, j - 1))
                        if l == 0:
                            for n in range(2):
                                for t in range(nt):
                                    m = mix[:, t, n * NW:(n + 1) * NW]
                                    key = ("acc", j - 1, t, n)
                                    dve.wait_ge(*after(*key))
                                    if j > 1:
                                        dve.wait_ge(*after("read", "acc", j - 2, t, n))
                                        ins = v.tensor_tensor(m, src(*key), m, ALU.add)
                                    else:
                                        ins = v.tensor_copy(m, src(*key))
                                    ins.then_inc(*did("vector", ("read",) + key, *([("summed", t, n)] if j == 8 else [])))
                if l == 1:
                    for t in range(nt):
                        gated_half(l, 1, t, 0)
                for i in range(4):
                    if i < 2:
                        sum_halves(l, 1, groups[i])
                        if l == 1:
                            for t in groups[i]:
                                gated_half(l, 1, t, 1)
                    if 0 <= i - 1 < 2:
                        residual(l, 1, groups[i - 1])
                    if l == 0 and 0 <= i - 2 < 2:
                        normed(1, 0, groups[i - 2])
                    if l == 0 and i >= 2:
                        split_mods(("q2", 1, 0), i - 2)

        @block.gpsimd
        def _(pool):
            p = nc.gpsimd
            st = [0]

            def split_to(name, ahead=1):
                split_lo(pool, p, last_split(name, ahead), st, True)

            def low_modulated(name, nt, l, which):
                per = 4 // nt
                for j in range(KD // per):
                    pool.wait_ge(*after("fhi", name, j))
                    dst = flo[:, j * per:(j + 1) * per, 0:nt * P]
                    hi = fhi[:, j * per:(j + 1) * per, 0:nt * P].bitcast(F32)
                    p.tensor_tensor(dst, ftmp(l, which, j).rearrange("p (a b) -> p a b", a=per), hi, ALU.subtract).then_inc(
                        *did("pool", ("split", name, j)))

            def gain_shift(t, *label):
                h = hx[:, t, :]
                p.tensor_tensor(h, h, lnrow[:, 0, :], ALU.mult).then_inc(*did("pool"))
                pool.wait_ge(counts.sems["pool"], counts.now["pool"])
                p.tensor_tensor(h, h, lnrow[:, 1, :], ALU.add).then_inc(*did("pool", label))

            split_to(("k", 0, 0), 0)
            low_modulated("f1", 2, -1, 0)
            split_to(("k", 0, 0))
            pool.wait_ge(*after("f1", 3))
            pool.wait_ge(loads["lna"], 32)
            for t in range(XT):
                gain_shift(t, "h1", t)
                split_to(("k", 0, 2))
            split_to(("outb", 1))
            pool.wait_ge(loads["lnb"], 32)
            pool.wait_ge(*after("centred", 1))
            gain_shift(1, "ln", 1, 1)

            for l in range(2):
                nt = 4 if l == 0 else 2
                split_to(("q2", l, 0), 0)
                low_modulated(("n1", l), 4, l, 0)
                if l == 1:
                    split_to(("v2", 1, 1), 0)
                    pool.wait_ge(loads["bias"], 16 * BIAS_LOADS)
                    for n, b in enumerate((mix[:, XT:2 * XT, :], hc[:, :, :])):
                        rows = b.rearrange("p t (h c) -> p (t h) c", c=S)
                        p.tensor_tensor(rows, rows, heads_view(colmask, (0, 8), (1, S)), ALU.add).then_inc(
                            *did("pool", *([("bias",)] if n else [])))
                split_to(("in", l, 0), 0)
                low_modulated(("n2", l), nt, l, 1)
                for j in range(9):
                    if j < 8:
                        split_to(("in", l, j))
                        for e in range(4):
                            pool.wait_ge(*after("hhi", l, j, e))
                            p.tensor_tensor(hlo[:, j % 2, e, 0:nt * P], htmp[:, e % 2, 0:nt * P],
                                            hhi[:, j % 2, e, 0:nt * P].bitcast(F32), ALU.subtract).then_inc(
                                *did("pool", ("hidden", l, j, e)))
                    if j:
                        split_to(("out", l, j - 1))
                if l == 0:
                    pool.wait_ge(loads["g01"], 32)
                    for t, n in [(t, 0) for t in range(4)] + [(t, 1) for t in range(4)]:
                        pool.wait_ge(*after("sqh", 0, 1, t, n))
                        m = mix[:, t, n * NW:(n + 1) * NW]
                        p.tensor_tensor(m, m, gates[:, 0 if t < XT else 1, n * NW:(n + 1) * NW], ALU.mult).then_inc(
                            *did("pool", ("gated half", 0, 1, t, n)))


def kernel(**inputs):
    import numpy as _np
    import concourse.bacc as _bacc
    from concourse import mybir as _mybir
    from concourse.bass_utils import run_bass_kernel_spmd as _run

    a = {k: _np.asarray(x) for k, x in inputs.items()}
    f32 = _np.float32
    stream = _np.empty((CHUNKS, P, CHUNK), f32)
    n = 0
    for u in UNITS:
        for name, idx, row, col in u.pieces:
            block = a[name][idx][row:row + u.nk * P, col:col + u.width]
            stream[n] = block.reshape(u.nk, P, u.width).transpose(1, 0, 2).reshape(P, CHUNK)
            n += 1

    def cols(x):
        y = x.reshape(x.shape[:-1] + (x.shape[-1] // P, P))
        return _np.ascontiguousarray(_np.moveaxis(y, -1, 0))

    rows = _np.zeros((4, 8, 4, P), f32)
    for r in range(4):
        rows[r, :, :, GRID - 16:GRID + 15] = a["rpb_d_2"][0, :, 7 - r:11 - r, :]
    arrays = {
        "wstream": stream,
        "x": a["x"], "ctx_2": a["ctx_2"],
        "cond": _np.ascontiguousarray(_np.moveaxis(cols(_np.stack([a["c_2"][0], a["c_ctx_2"]])), 1, 2)),
        "scale_cols": cols(a["scale_a"][0]),
        "b_mod_cols": cols(a["b_mod_2"]), "norm_cols": cols(a["norm_g_2"]),
        "ln_g": a["ln_g"], "ln_b": a["ln_b"],
        "ln_cols": cols(_np.stack([a["ln_g"][0], a["ln_b"][0]])),
        "qk_norm_a_2": a["qk_norm_a_2"], "diff_lambda_2": a["diff_lambda_2"],
        "diff_subln_2": a["diff_subln_2"], "sink_c_2": a["sink_c_2"],
        "rpb_rows": _np.ascontiguousarray(_np.broadcast_to(rows[:, :, :, None, :], (4, 8, 4, GRID, P))),
        **constants(),
    }
    arrays = {k: _np.ascontiguousarray(x) for k, x in arrays.items()}

    counts = None
    for _ in range(2):
        nc = _bacc.Bacc("TRN2", target_bir_lowering=False, num_devices=1)
        T = {k: nc.dram_tensor("in_" + k, x.shape, _mybir.dt.float32, kind="ExternalInput").ap() for k, x in arrays.items()}
        out = nc.dram_tensor("out", (1, S, D), _mybir.dt.float32, kind="ExternalOutput").ap()
        counts = Counts(counts)
        build(nc, T, out, counts)
    r = _run(nc, [{"in_" + k: x for k, x in arrays.items()}], core_ids=[0])
    return r.results[0]["out"]
```
